# Optimizing a Trainium2 kernel written in Bass

```python
import functools
import jax, jax.numpy as jnp
from jax import lax
import numpy as np

D_MODEL = 1024
BATCH = 1
SEQ = 256
DEPTH = 2
DEC_BATCH = 8
DEC_SEQ = 4
PAST_LEN = 2048
PAGE_SIZE = 128

HEAD_DIM = 64
A_HEADS = 8
A_DIM = A_HEADS * HEAD_DIM
LORA_W = 64
LORA_A = 64
LORA_G = 128
B_DIM = 512
CONV_W = 3
C_HEADS = 8
C_KV_HEADS = 4
C_DIM = C_HEADS * HEAD_DIM
C_KV_DIM = C_KV_HEADS * HEAD_DIM
IDX_HEADS = 8
IDX_DIM = 64
TOPK_MAX = 256
ROT_DIM = HEAD_DIM // 4
ROPE_THETA = 500000.0
D_FF = 2816
PLE_DIM = 256
N_BRANCH = 3
RMS_EPS = 1e-6
GN_EPS = 64e-5
Q_BLOCK = 128

RWKV_COLS = 3 * A_DIM + LORA_W + LORA_A + LORA_G
CONV_COLS = 3 * B_DIM
ATTN_COLS = C_DIM + 2 * C_KV_DIM + IDX_HEADS * IDX_DIM + IDX_DIM + IDX_HEADS
GATE_COLS = N_BRANCH * D_MODEL
IN_COLS = RWKV_COLS + CONV_COLS + ATTN_COLS + GATE_COLS

kernel_name = 'hybrid_rwkv7_shortconv_dsa_decoder_step'

def rmsnorm(x, g):
    xf = x.astype(jnp.float32)
    y = xf * lax.rsqrt(jnp.mean(xf * xf, axis=-1, keepdims=True) + RMS_EPS)
    return (y * g.astype(jnp.float32)).astype(x.dtype)

def swiglu(h, wg, wu, wd):
    return (jax.nn.silu(h @ wg) * (h @ wu)) @ wd

def rope_partial(x, pos):
    half = ROT_DIM // 2
    inv = ROPE_THETA ** (-jnp.arange(half, dtype=jnp.float32) / half)
    ang = pos.astype(jnp.float32)[:, None] * inv[None, :]
    cos = jnp.cos(ang)[:, None, :]
    sin = jnp.sin(ang)[:, None, :]
    xr = x[..., :ROT_DIM].astype(jnp.float32)
    x1, x2 = xr[..., :half], xr[..., half:]
    rot = jnp.concatenate([x1 * cos - x2 * sin, x2 * cos + x1 * sin], axis=-1)
    return jnp.concatenate([rot.astype(x.dtype), x[..., ROT_DIM:]], axis=-1)

def rwkv7_mixer(u, shift0, wkv0, lp):
    B, T, _ = u.shape
    u_prev = jnp.concatenate([shift0[:, None, :].astype(u.dtype), u[:, :-1]], axis=1)
    us = u + (u_prev - u) * lp['rwkv_mu']
    o1 = A_DIM; o2 = 2 * A_DIM; o3 = 3 * A_DIM
    r, k, v, xw, xa, xg = jnp.split(us, [o1, o2, o3, o3 + LORA_W, o3 + LORA_W + LORA_A], axis=-1)
    w_log = -jax.nn.softplus(-(lp['rwkv_w0'] + jnp.tanh(xw) @ lp['rwkv_w2'])) - 0.5
    decay = jnp.exp(-jnp.exp(w_log.astype(jnp.float32)))
    a = jax.nn.sigmoid(lp['rwkv_a0'] + xa @ lp['rwkv_a2'])
    g = jax.nn.sigmoid(xg) @ lp['rwkv_g2']
    heads = lambda t: t.reshape(B, T, A_HEADS, HEAD_DIM).astype(jnp.float32)
    kk = heads(k * lp['rwkv_kk'])
    kk = kk / jnp.maximum(jnp.sqrt(jnp.sum(kk * kk, axis=-1, keepdims=True)), 1e-12)
    k = k * (1.0 + (a - 1.0) * lp['rwkv_ka'])
    rh, kh, vh, ah, wh = heads(r), heads(k), heads(v), heads(a), heads(decay)
    a_vec = -kk
    b_vec = kk * ah

    def step(S, inp):
        r_t, w_t, k_t, v_t, a_t, b_t = inp
        sa = jnp.einsum('bhij,bhj->bhi', S, a_t)
        S = S * w_t[:, :, None, :] + sa[..., :, None] * b_t[..., None, :] + v_t[..., :, None] * k_t[..., None, :]
        return S, jnp.einsum('bhij,bhj->bhi', S, r_t)

    tm = lambda t: jnp.moveaxis(t, 1, 0)
    S_fin, o = lax.scan(step, wkv0.astype(jnp.float32), (tm(rh), tm(wh), tm(kh), tm(vh), tm(a_vec), tm(b_vec)))
    o = jnp.moveaxis(o, 0, 1)
    mean = jnp.mean(o, axis=-1, keepdims=True)
    var = jnp.mean(jnp.square(o - mean), axis=-1, keepdims=True)
    on = ((o - mean) * lax.rsqrt(var + GN_EPS)).reshape(B, T, A_DIM) * lp['rwkv_lnx_w'] + lp['rwkv_lnx_b']
    bonus = jnp.sum(rh * kh * lp['rwkv_rk'].astype(jnp.float32), axis=-1, keepdims=True) * vh
    out = (on + bonus.reshape(B, T, A_DIM)) * g
    return out.astype(u.dtype), u[:, -1], S_fin.astype(wkv0.dtype)

def shortconv_mixer(u, conv0, w_conv):
    T = u.shape[1]
    bg, cg, xin = jnp.split(u, [B_DIM, 2 * B_DIM], axis=-1)
    z = cg * xin
    zp = jnp.concatenate([conv0.astype(z.dtype), z], axis=1)
    y = zp[:, 0:T] * w_conv[0]
    for j in range(1, CONV_W):
        y = y + zp[:, j:j + T] * w_conv[j]
    return bg * y, zp[:, -(CONV_W - 1):]

def attn_project(u, pos, lp):
    B, T, _ = u.shape
    offs = np.cumsum([C_DIM, C_KV_DIM, C_KV_DIM, IDX_HEADS * IDX_DIM, IDX_DIM]).tolist()
    q, k, v, qi, ki, wi = jnp.split(u, offs, axis=-1)
    q = rope_partial(rmsnorm(q.reshape(B, T, C_HEADS, HEAD_DIM), lp['q_norm']), pos)
    k = rope_partial(rmsnorm(k.reshape(B, T, C_KV_HEADS, HEAD_DIM), lp['k_norm']), pos)
    v = v.reshape(B, T, C_KV_HEADS, HEAD_DIM)
    qi = rope_partial(qi.reshape(B, T, IDX_HEADS, IDX_DIM), pos)
    ki = rope_partial(rmsnorm(ki, lp['idx_k_norm'])[:, :, None, :], pos)[:, :, 0, :]
    return q, k, v, qi, ki, wi

def index_scores(qi, wi, ki):
    s = jnp.einsum('bthd,bsd->bths', qi, ki).astype(jnp.float32) * (IDX_DIM ** -0.5)
    return jnp.einsum('bths,bth->bts', jax.nn.relu(s), wi.astype(jnp.float32) * (IDX_HEADS ** -0.5))

def sparse_attend(q, k_sel, v_sel, valid):
    B, Tq = q.shape[:2]
    qg = q.reshape(B, Tq, C_KV_HEADS, C_HEADS // C_KV_HEADS, HEAD_DIM)
    s = jnp.einsum('bqgrd,bqkgd->bqgrk', qg, k_sel).astype(jnp.float32) * (HEAD_DIM ** -0.5)
    s = jnp.where(valid[:, :, None, None, :], s, -jnp.inf)
    p = jax.nn.softmax(s, axis=-1).astype(v_sel.dtype)
    o = jnp.einsum('bqgrk,bqkgd->bqgrd', p, v_sel)
    return o.reshape(B, Tq, C_DIM)

def prompt_sparse_attention(q, k, v, qi, ki, wi):
    B, S = q.shape[:2]
    topk = min(TOPK_MAX, S // 4)
    key_pos = jnp.arange(S)
    gather = jax.vmap(lambda kb, ib: kb[ib])

    def block(bi):
        start = bi * Q_BLOCK
        qb = lax.dynamic_slice_in_dim(q, start, Q_BLOCK, axis=1)
        qib = lax.dynamic_slice_in_dim(qi, start, Q_BLOCK, axis=1)
        wib = lax.dynamic_slice_in_dim(wi, start, Q_BLOCK, axis=1)
        qpos = start + jnp.arange(Q_BLOCK)
        sc = index_scores(qib, wib, ki)
        sc = jnp.where((key_pos[None, :] <= qpos[:, None])[None], sc, -jnp.inf)
        _, idx = lax.top_k(sc, topk)
        valid = idx <= qpos[None, :, None]
        return sparse_attend(qb, gather(k, idx), gather(v, idx), valid)

    out = lax.map(block, jnp.arange(S // Q_BLOCK))
    return jnp.moveaxis(out, 0, 1).reshape(B, S, C_DIM)

def sample_sparse_attention(q, k, v, qi, ki, wi, *, cache_k, cache_v, cache_kidx, page_table, layer):
    DB, T = q.shape[:2]
    n_pages = page_table.shape[1]
    page = cache_k.shape[2]
    past = n_pages * page
    L = past + T
    topk = min(TOPK_MAX, L // 4)
    ki_past = cache_kidx[layer, page_table].reshape(DB, past, IDX_DIM)
    ki_all = jnp.concatenate([ki_past.astype(ki.dtype), ki], axis=1)
    sc = index_scores(qi, wi, ki_all)
    qpos = past + jnp.arange(T)
    kpos = jnp.arange(L)
    sc = jnp.where((kpos[None, :] <= qpos[:, None])[None], sc, -jnp.inf)
    _, idx = lax.top_k(sc, topk)
    valid = idx <= qpos[None, :, None]
    in_past = idx < past
    pidx = jnp.minimum(idx, past - 1)
    phys_page = jnp.take_along_axis(page_table, (pidx // page).reshape(DB, -1), axis=1).reshape(DB, T, topk)
    phys = phys_page * page + pidx % page
    depth = cache_k.shape[0]
    ck = cache_k.reshape(depth, -1, C_KV_HEADS, HEAD_DIM)
    cv = cache_v.reshape(depth, -1, C_KV_HEADS, HEAD_DIM)
    nidx = jnp.clip(idx - past, 0, T - 1)
    gather = jax.vmap(lambda kb, ib: kb[ib])
    sel = in_past[..., None, None]
    k_sel = jnp.where(sel, ck[layer, phys].astype(k.dtype), gather(k, nidx))
    v_sel = jnp.where(sel, cv[layer, phys].astype(v.dtype), gather(v, nidx))
    return sparse_attend(q, k_sel, v_sel, valid)

def trunk_layer(x, p, pos, lp, shift0, conv0, wkv0, attn_fn):
    B, T, _ = x.shape
    h = rmsnorm(x, lp['ffn1_norm'])
    x = x + 0.5 * swiglu(h, lp['ffn1_wg'], lp['ffn1_wu'], lp['ffn1_wd'])
    h = rmsnorm(x, lp['mix_norm'])
    u = h @ lp['w_in']
    u_a, u_b, u_c, u_g = jnp.split(u, [RWKV_COLS, RWKV_COLS + CONV_COLS, RWKV_COLS + CONV_COLS + ATTN_COLS], axis=-1)
    o_a, shift1, wkv1 = rwkv7_mixer(u_a, shift0, wkv0, lp)
    o_b, conv1 = shortconv_mixer(u_b, conv0, lp['conv_w'])
    q, k, v, qi, ki, wi = attn_project(u_c, pos, lp)
    o_c = attn_fn(q, k, v, qi, ki, wi)
    gates = jax.nn.sigmoid(u_g).reshape(B, T, N_BRANCH, D_MODEL)
    merged = (gates[:, :, 0] * (o_a @ lp['w_pa']) + gates[:, :, 1] * (o_b @ lp['w_pb'])
              + gates[:, :, 2] * (o_c @ lp['w_pc']))
    x = x + merged @ lp['w_out']
    h = rmsnorm(x, lp['ffn2_norm'])
    x = x + 0.5 * swiglu(h, lp['ffn2_wg'], lp['ffn2_wu'], lp['ffn2_wd'])
    gate = jax.nn.sigmoid(rmsnorm(x, lp['ple_norm']) @ lp['ple_gate'])
    x = x + gate * (p.astype(x.dtype) @ lp['ple_proj'])
    return x, (k, v, ki, wkv1, shift1, conv1)

def setup_inputs(seed: int = 0) -> dict:
    key = jax.random.key(seed)
    keys = jax.random.split(key, 64)
    ctr = [0]

    def nxt():
        ctr[0] += 1
        return keys[ctr[0] - 1]

    def nrm(shape, scale=1.0):
        return jax.random.normal(nxt(), shape, jnp.float32) * scale

    def gain(shape):
        return 1.0 + 0.05 * nrm(shape)

    n_pages = PAST_LEN // PAGE_SIZE
    n_used = DEC_BATCH * n_pages
    n_phys = n_used + n_used // 4
    perm = jax.random.permutation(nxt(), n_phys)
    page_table = perm[:n_used].reshape(DEC_BATCH, n_pages).astype(jnp.int32)
    Ly = DEPTH
    return {
        'x_prompt': nrm((BATCH, SEQ, D_MODEL)),
        'x_sample': nrm((DEC_BATCH, DEC_SEQ, D_MODEL)),
        'cache_k': nrm((Ly, n_phys, PAGE_SIZE, C_KV_HEADS, HEAD_DIM)),
        'cache_v': nrm((Ly, n_phys, PAGE_SIZE, C_KV_HEADS, HEAD_DIM)),
        'cache_kidx': nrm((Ly, n_phys, PAGE_SIZE, IDX_DIM)),
        'state_wkv': nrm((Ly, DEC_BATCH, A_HEADS, HEAD_DIM, HEAD_DIM), 0.5),
        'state_shift': nrm((Ly, DEC_BATCH, RWKV_COLS)),
        'state_conv': nrm((Ly, DEC_BATCH, CONV_W - 1, B_DIM)),
        'page_table': page_table,
        'p_prompt': nrm((Ly, BATCH, SEQ, PLE_DIM)),
        'p_sample': nrm((Ly, DEC_BATCH, DEC_SEQ, PLE_DIM)),
        'ffn1_norm': gain((Ly, D_MODEL)),
        'ffn1_wg': nrm((Ly, D_MODEL, D_FF), D_MODEL ** -0.5),
        'ffn1_wu': nrm((Ly, D_MODEL, D_FF), D_MODEL ** -0.5),
        'ffn1_wd': nrm((Ly, D_FF, D_MODEL), D_FF ** -0.5),
        'mix_norm': gain((Ly, D_MODEL)),
        'w_in': nrm((Ly, D_MODEL, IN_COLS), D_MODEL ** -0.5),
        'rwkv_mu': jax.random.uniform(nxt(), (Ly, RWKV_COLS), jnp.float32),
        'rwkv_w0': nrm((Ly, A_DIM), 0.5),
        'rwkv_w2': nrm((Ly, LORA_W, A_DIM), 0.5 * LORA_W ** -0.5),
        'rwkv_a0': nrm((Ly, A_DIM), 0.1),
        'rwkv_a2': nrm((Ly, LORA_A, A_DIM), 0.5 * LORA_A ** -0.5),
        'rwkv_g2': nrm((Ly, LORA_G, A_DIM), LORA_G ** -0.5),
        'rwkv_kk': 0.85 + 0.05 * nrm((Ly, A_DIM)),
        'rwkv_ka': gain((Ly, A_DIM)),
        'rwkv_rk': nrm((Ly, A_HEADS, HEAD_DIM), 0.1),
        'rwkv_lnx_w': gain((Ly, A_DIM)),
        'rwkv_lnx_b': nrm((Ly, A_DIM), 0.01),
        'conv_w': nrm((Ly, CONV_W, B_DIM), CONV_W ** -0.5),
        'q_norm': gain((Ly, HEAD_DIM)),
        'k_norm': gain((Ly, HEAD_DIM)),
        'idx_k_norm': gain((Ly, IDX_DIM)),
        'w_pa': nrm((Ly, A_DIM, D_MODEL), A_DIM ** -0.5),
        'w_pb': nrm((Ly, B_DIM, D_MODEL), B_DIM ** -0.5),
        'w_pc': nrm((Ly, C_DIM, D_MODEL), C_DIM ** -0.5),
        'w_out': nrm((Ly, D_MODEL, D_MODEL), D_MODEL ** -0.5),
        'ffn2_norm': gain((Ly, D_MODEL)),
        'ffn2_wg': nrm((Ly, D_MODEL, D_FF), D_MODEL ** -0.5),
        'ffn2_wu': nrm((Ly, D_MODEL, D_FF), D_MODEL ** -0.5),
        'ffn2_wd': nrm((Ly, D_FF, D_MODEL), D_FF ** -0.5),
        'ple_norm': gain((Ly, D_MODEL)),
        'ple_gate': nrm((Ly, D_MODEL, D_MODEL), D_MODEL ** -0.5),
        'ple_proj': nrm((Ly, PLE_DIM, D_MODEL), PLE_DIM ** -0.5),
    }

def reference(x_prompt, x_sample, cache_k, cache_v, cache_kidx, state_wkv, state_shift, state_conv,
              page_table, p_prompt, p_sample,
              ffn1_norm, ffn1_wg, ffn1_wu, ffn1_wd, mix_norm, w_in,
              rwkv_mu, rwkv_w0, rwkv_w2, rwkv_a0, rwkv_a2, rwkv_g2, rwkv_kk, rwkv_ka, rwkv_rk,
              rwkv_lnx_w, rwkv_lnx_b, conv_w, q_norm, k_norm, idx_k_norm,
              w_pa, w_pb, w_pc, w_out, ffn2_norm, ffn2_wg, ffn2_wu, ffn2_wd,
              ple_norm, ple_gate, ple_proj):
    B, S, _ = x_prompt.shape
    DB, T, _ = x_sample.shape
    past = page_table.shape[1] * cache_k.shape[2]
    pos_p = jnp.arange(S, dtype=jnp.int32)
    pos_s = past + jnp.arange(T, dtype=jnp.int32)
    shift_zero = jnp.zeros((B, RWKV_COLS), x_prompt.dtype)
    conv_zero = jnp.zeros((B, CONV_W - 1, B_DIM), x_prompt.dtype)
    wkv_zero = jnp.zeros((B, A_HEADS, HEAD_DIM, HEAD_DIM), jnp.float32)
    xp, xs = x_prompt, x_sample
    outs_p, outs_s = [], []
    for i in range(DEPTH):
        lp = dict(ffn1_norm=ffn1_norm[i], ffn1_wg=ffn1_wg[i], ffn1_wu=ffn1_wu[i], ffn1_wd=ffn1_wd[i],
                  mix_norm=mix_norm[i], w_in=w_in[i], rwkv_mu=rwkv_mu[i], rwkv_w0=rwkv_w0[i],
                  rwkv_w2=rwkv_w2[i], rwkv_a0=rwkv_a0[i], rwkv_a2=rwkv_a2[i], rwkv_g2=rwkv_g2[i],
                  rwkv_kk=rwkv_kk[i], rwkv_ka=rwkv_ka[i], rwkv_rk=rwkv_rk[i], rwkv_lnx_w=rwkv_lnx_w[i],
                  rwkv_lnx_b=rwkv_lnx_b[i], conv_w=conv_w[i], q_norm=q_norm[i], k_norm=k_norm[i],
                  idx_k_norm=idx_k_norm[i], w_pa=w_pa[i], w_pb=w_pb[i], w_pc=w_pc[i], w_out=w_out[i],
                  ffn2_norm=ffn2_norm[i], ffn2_wg=ffn2_wg[i], ffn2_wu=ffn2_wu[i], ffn2_wd=ffn2_wd[i],
                  ple_norm=ple_norm[i], ple_gate=ple_gate[i], ple_proj=ple_proj[i])
        xp, st_p = trunk_layer(xp, p_prompt[i], pos_p, lp, shift_zero, conv_zero, wkv_zero,
                               prompt_sparse_attention)
        attn_s = functools.partial(sample_sparse_attention, cache_k=cache_k, cache_v=cache_v,
                                   cache_kidx=cache_kidx, page_table=page_table, layer=i)
        xs, st_s = trunk_layer(xs, p_sample[i], pos_s, lp, state_shift[i], state_conv[i], state_wkv[i], attn_s)
        outs_p.append(st_p)
        outs_s.append(st_s)
    k_p, v_p, kidx_p, wkv_p, shift_p, conv_p = [jnp.stack(z) for z in zip(*outs_p)]
    k_s, v_s, kidx_s, wkv_s, shift_s, conv_s = [jnp.stack(z) for z in zip(*outs_s)]
    return (xp, xs, k_p, v_p, kidx_p, wkv_p, shift_p, conv_p, k_s, v_s, kidx_s, wkv_s, shift_s, conv_s)


_drawn_inputs = setup_inputs


def setup_inputs(seed=0):
    import zlib

    import numpy as np

    out = dict(_drawn_inputs(seed))
    spreads = {}
    factors = {'rwkv_kk': 4.999,
     'rwkv_lnx_w': 3.162,
     'rwkv_lnx_b': 8.0,
     'q_norm': 7.47,
     'ple_norm': 4.368}
    for name, (base, spread) in spreads.items():
        noise = np.random.default_rng([zlib.crc32(name.encode()), seed]).standard_normal(out[name].shape)
        drawn = base * np.exp(spread * noise) if base else spread * noise
        out[name] = __import__('jax').numpy.asarray(drawn.astype(out[name].dtype))
    for name, factor in factors.items():
        out[name] = (out[name] * factor).astype(out[name].dtype)
    return out
```

```python
from contextlib import ExitStack

import numpy as np
import concourse.bass as bass
from concourse import mybir

F32 = mybir.dt.float32
I32 = mybir.dt.int32
ALU = mybir.AluOpType
ACT = mybir.ActivationFunctionType
AX = mybir.AxisListType

P = 128
D = 1024
DC = D // P
NPR = 256
NB, NS = 8, 4
NSM = NB * NS
T = NPR + NSM
DEPTH = 2
FC = 2816 // P
HD = 64
NH = 8
NPAGE = 16
PAGE = 128
NPHYS = 160
PAST = NPAGE * PAGE
KEYS = PAST + NSM
TOPK_P, TOPK_S = 64, 256
CH = 32
SLOTS, SLAB = 5, 2048
UC = 14
UX = 1 + NPR + NB * (NS + 1)
ZX = 2 + NPR + NB * (NS + 2)
NEG, TAKEN = -1e30, -3e38
EPS, GN_EPS = 1e-6, 64e-5

PCOL = {}
_n = 0
for _name, _w in (("ffn1", 8), ("mix", 8), ("ffn2", 8), ("ple", 8), ("mu", UC), ("w0", 4), ("a0", 4), ("kk", 4),
                  ("ka", 4), ("rk", 4), ("lnw", 4), ("lnb", 4), ("cw", 12), ("qn", 1), ("kn", 1), ("in", 1)):
    PCOL[_name] = _n
    _n += _w
NPARAM = _n


def constants():
    s, t = np.arange(P)[:, None], np.arange(P)[None, :]
    same = lambda n: s // n == t // n
    cols = {"ident": s == t, "ones": np.ones((P, P)), "blk": same(HD)}
    rot = np.zeros((P, P))
    for base in (0, HD):
        for i in range(8):
            rot[base + i + 8, base + i] = -1.0
            rot[base + i, base + i + 8] = 1.0
    cols["rot"] = rot
    pos = np.concatenate([np.arange(NPR), np.tile(PAST + np.arange(NS), NB)]).astype(np.float32)
    inv = np.float32(500000.0) ** (-np.arange(8, dtype=np.float32) / np.float32(8))
    ang = (pos[:, None] * inv[None, :].astype(np.float32)).astype(np.float32)
    cos, sin = np.ones((P, T)), np.zeros((P, T))
    for base in (0, HD):
        for i in range(16):
            cos[base + i] = np.cos(ang[:, i % 8])
            sin[base + i] = np.sin(ang[:, i % 8])
    cols["cos"], cols["sin"] = cos, sin
    up, low = s < t, s > t
    cols["gm"] = np.concatenate([up & same(8), (s <= t) & same(CH), up & same(CH), (s <= t) & same(CH)], 1)
    cols["y8"] = low & same(8)
    cols["y16"] = low & same(16) & ~same(8)
    cols["y32"] = low & same(32) & ~same(16)
    s4, t4 = np.arange(P)[:, None], np.arange(NSM)[None, :]
    b4 = s4 // 4 == t4 // 4
    cols["gs"] = np.concatenate([(s4 < t4) & b4, (s4 <= t4) & b4, (s4 < t4) & b4, (s4 <= t4) & b4], 1)
    cols["ys"] = (s4 > t4) & b4
    q, k = np.arange(P)[:, None], np.arange(NPR)[None, :]
    cols["causal"] = np.concatenate([np.where(k <= q + P * i, 0.0, NEG) for i in range(2)], 1)
    start = np.ones((P, T))
    start[:, 0:NPR:CH] = 0
    start[:, NPR::NS] = 0
    cols["keep"], cols["begin"] = start, 1 - start
    row = np.arange(P)[:, None]
    tok = np.arange(NSM)[None, :]
    for g in range(2):
        b, tt = 4 * g + row // 32, row % 4
        cols[f"wsel{g}"] = ((tok // 4 == b) & (tok % 4 == tt)) * np.float32(NH ** -0.5)
    col = np.arange(P)[None, :]
    cols["e8"] = (row == (col // 4) % 8) & (row < 8)
    for g in range(2):
        cols[f"exp{g}"] = (row < 32) & (row // 4 == 4 * g + col // 32) & (row % 4 == col % 4)
    cols["cs"] = np.where((row // 4 == tok // 4) & (tok % 4 <= row % 4), 0.0, NEG)
    cols["bsel"] = row // 4 == np.arange(NB)[None, :]
    where, parts, n = {}, [], 0
    for name, a in cols.items():
        where[name] = (n, n + a.shape[1])
        n += a.shape[1]
        parts.append(np.asarray(a, np.float32))
    return where, np.ascontiguousarray(np.concatenate(parts, 1))


CW, CONST = constants()
NCONST = CONST.shape[1]


class Lane:

    def __init__(self, eng, sems, marks, found):
        self.eng, self.sems, self.marks, self.found = eng, sems, marks, found
        self.sent, self.met, self.last, self.passed = {}, {}, None, {}

    def up(self, name, by=1):
        self.sent[name] = self.sent.get(name, 0) + by
        if by == 1:
            self.last = (name, self.sent[name])
        return self.sems(name), by

    def next(self, name, n=1):
        self.met[name] = self.met.get(name, 0) + n
        return self.sems(name), self.met[name]

    def own(self):
        name, n = self.last
        return self.sems(name), n

    def mark(self, name):
        self.found.setdefault(name, []).append(self.last)

    def after(self, name, n=1):
        at = self.passed[name] = self.passed.get(name, 0) + n
        sem, value = self.marks[name][at - 1] if self.marks else ("plan", 1)
        return self.sems(sem), value


def build(nc, io, marks, found):
    ctx = ExitStack()
    with ctx:
        named = {}

        def sems(name):
            if name not in named:
                named[name] = ctx.enter_context(nc.semaphore(name))
            return named[name]

        def sb(name, *shape, dt=F32):
            return ctx.enter_context(nc.sbuf_tensor(name, list(shape), dt))

        bank = [ctx.enter_context(nc.psum_tensor(f"bank{i}", [P, 512], F32))[:, :] for i in range(8)]
        ringA, ringV = bank[0:4], bank[4:8]

        cst = sb("cst", P, NCONST)
        C = lambda name: cst[:, CW[name][0]:CW[name][1]]
        ring = sb("ring", P, SLOTS, SLAB)
        x = sb("x", P, DC, T)
        h = sb("h", P, DC, T)
        tmp = sb("tmp", P, 2304)
        sq = tmp[:, :].rearrange("p (c t) -> p c t", t=T)
        gate = sb("gate", P, 2, T)
        oa, ob, oc = sb("oa", P, 4, T), sb("ob", P, 4, T), sb("oc", P, 4, T)
        prm = sb("prm", P, NPARAM)
        rstd = sb("rstd", P, T)
        ptk = sb("ptk", P, 2, T)
        pages = sb("pages", 1, NB * NPAGE, dt=I32)
        lora = sb("lora", P, 2, 512)
        sft = sb("sft", P, UC, NB)
        scv = sb("scv", P, 4, NB, 2)
        sho = sb("sho", P, UC, NB + 1)
        cvo = sb("cvo", P, 4, NB + 1, 2)
        m8 = sb("m8", P, 8)
        stat = sb("stat", P, 64)
        witok = sb("witok", P, 2, NH)
        wi = sb("wi", NH, T)
        pend = sb("pend", P, 4, 16)
        LEFT = (nc.sbuf_bytes_remaining - 64) // 4
        arena = sb("arena", P, LEFT)

        class Carve:

            def __init__(self, at=0):
                self.at = at

            def __call__(self, *shape):
                n = int(np.prod(shape))
                ap = arena[:, self.at:self.at + n]
                self.at += n
                assert self.at <= LEFT, (self.at, LEFT)
                if len(shape) == 2:
                    ap = ap.rearrange("p (a b) -> p a b", b=shape[1])
                elif len(shape) == 3:
                    ap = ap.rearrange("p (a b c) -> p a b c", b=shape[1], c=shape[2])
                return ap

        hid = Carve()(FC, T)
        c = Carve()
        uext = c(UC, UX)
        bgate, cgate, zx = c(4, T), c(4, T), c(4, ZX)
        q, k, v, qi = c(4, T), c(2, T), c(2, T), c(4, T)
        kid, kd, vtok = c(T), c(4, T), c(3, 256)
        qi0, qz, wsel = c(NB, 32), c(2, NB, 32), c(2, NSM)
        seenP = c(2, NPR)
        sidx = c(KEYS)
        sc, pt = c(KEYS), c(17, P)
        pr = sc[:, 0:2048].rearrange("p (a b) -> p a b", b=NPR)
        prT = pt[:, 0:16, :]
        ov = kd[:, :, :].rearrange("p a t -> p (a t)")[:, 0:512].rearrange("p (g b r) -> p g b r", g=2, b=NB)
        kv_at = c.at
        kvring = c(4, 1024)
        kiring = arena[:, kv_at:kv_at + 2048].rearrange("p (a b) -> p a b", b=512)
        rl = arena[:, kv_at + 2048:kv_at + 3072].rearrange("p (a b) -> p a b", b=512)
        r = Carve(UC * UX)
        gT, bon = r(4, T), r(4, T)
        AR, Bt, Kt = r(4, 2, T), r(4, T), r(4, T)
        keep_at = r.at
        us = r(UC, T)
        kk, aa, dec, pinv, pcum = r(4, T), r(4, T), r(4, T), r(4, T), r(4, T)
        lt = dec[:, 0:1, :]
        g = Carve(0)
        G = g(NH, 512)
        w = Carve(keep_at)
        tok = w(3, 3, 512)
        Ti = w(NH, P)
        MV = gate[:, :, :].rearrange("p a t -> p (a t)")[:, 0:512]
        S0 = w(4, NB, HD)
        work_at = w.at
        nm = {n: w(4, P) for n in ("y8", "yo16", "yo32", "iy8", "x2", "y2", "iy2", "h4", "fh", "dd", "dt", "qq")}
        t16 = nm["x2"]
        blk = Carve(work_at)
        ublk, vblk = blk(NB, P), blk(NB, P)
        zT, xs2, hs, us_s, s_sum = blk(4, NSM), blk(256), blk(256), blk(512), blk(512)
        R1 = tmp[:, 0:512]
        U = tmp[:, 512:1024]
        S = [tmp[:, 1024 + 512 * i:1536 + 512 * i].rearrange("p (c i) -> p c i", i=P) for i in range(2)]
        Ssum = tmp[:, 2048:2304].rearrange("p (c i) -> p c i", i=HD)
        rot_t = tmp[:, 0:T]
        chunk4 = lambda ap, n=4: ap.rearrange("p (a b) -> p a b", a=n)

        def bc(ap, n):
            return ap.rearrange("p (a m) -> p a m", a=1).to_broadcast([ap.shape[0], n, ap.shape[1]])

        half = lambda hd: slice(HD * (hd % 2), HD * (hd % 2) + HD)
        PAIRS = ((0, 2), (1, 3), (4, 6), (5, 7))
        BY_HALF = (0, 2, 4, 6, 1, 3, 5, 7)

        block = ctx.enter_context(nc.Block())

        def layers(eng, lane, body):
            for layer in range(DEPTH):
                body(layer)

        BAR = ("act", "dve", "pool")

        def barrier(lane, me):
            lane.eng.wait_ge(*lane.own())
            lane.eng.nop().then_inc(*lane.up(f"{me}_step"))
            lane.mark(f"phase_{me}")
            for other in BAR:
                if other != me:
                    lane.eng.wait_ge(*lane.after(f"phase_{other}"))

        @block.sync
        def _(eng):
            sp = Lane(eng, sems, marks, found)
            for dst, src in ((cst[:, :], io["const"]), (x[:, :, :], io["x"])):
                eng.dma_start(dst, src).then_inc(*sp.up("inputs_in", 16))

            def body(L):
                for n in range(NSLAB):
                    if L or n >= SLOTS:
                        eng.wait_ge(*sp.after("slab_used"))
                    eng.dma_start(ring[:, n % SLOTS, :], io["w"][bass.ds(L, 1), n, :, :].rearrange(
                        "a p n -> (a p) n")).then_inc(*sp.up(f"slab_in{n % SLOTS}", 16))
            layers(eng, sp, body)

        @block.gpsimd
        def _(eng):
            po = Lane(eng, sems, marks, found)
            eng.dma_start(pages[:, :], io["pages"]).then_inc(*po.up("pages_in", 16))
            eng.wait_ge(*po.next("pages_in", 16))
            eng.nop().then_inc(*po.up("pool_step"))

            def body(L):
                one = lambda ap: ap.rearrange("a p n -> (a p) n")
                eng.wait_ge(*po.own())
                eng.wait_ge(*po.after("layer_ready"))
                for dst, src, n in ((prm[:, :], io["prm"], 0), (ptk[:, :, :].rearrange("p a t -> p (a t)"), io["p"], 0),
                                    (lora[:, :, :].rearrange("p a t -> p (a t)"), io["lora"], 0),
                                    (sft[:, :, :].rearrange("p a t -> p (a t)"), io["sft"], 0),
                                    (scv[:, :, :, :].rearrange("p a b t -> p (a b t)"), io["scv"], 0)):
                    eng.dma_start(dst, one(src[bass.ds(L, 1)])).then_inc(*po.up("params_in", 16))
                eng.wait_ge(*po.after("ffn1_done"))
                n = 0

                def page(b, p):
                    return eng.value_load(pages[0:1, b * NPAGE + p:b * NPAGE + p + 1], min_val=0, max_val=NPHYS - 1)

                for kb in range(4):
                    for b in range(NB):
                        if n >= 4:
                            eng.wait_ge(*po.after("kiblock_free"))
                        for p in range(4):
                            at = page(b, 4 * kb + p) + L * NPHYS
                            eng.dma_start(kiring[0:HD, n % 4, PAGE * p:PAGE * (p + 1)],
                                                 one(io["ki"][bass.ds(at, 1)])).then_inc(*po.up(f"kiblock_in{n % 4}", 16))
                        n += 1
                eng.wait_ge(*po.after("kiblock_free", 4))
                eng.wait_ge(*po.after("rl_done"))
                n = 0
                for grp in range(2):
                    for name in ("k", "v"):
                        for i in range(16):
                            kb, b4 = (i // 4, i % 4) if name == "k" else (i % 4, i // 4)
                            if n >= 4:
                                eng.wait_ge(*po.after("kvblock_free"))
                            for p in range(4):
                                at = page(4 * grp + b4, 4 * kb + p) + L * NPHYS
                                if name == "k":
                                    dst = kvring[:, n % 4, :].rearrange("p (g k) -> p g k", g=2)[
                                        :, :, PAGE * p:PAGE * (p + 1)]
                                    src = io["k"][bass.ds(at, 1)].rearrange("a p (g k) -> (a p) g k", g=2)
                                else:
                                    dst, src = kvring[:, n % 4, 256 * p:256 * (p + 1)], one(io["v"][bass.ds(at, 1)])
                                eng.dma_start(dst, src).then_inc(*po.up(f"kvblock_in{n % 4}", 16))
                            n += 1
                eng.wait_ge(*po.after("kvblock_free", 4))
                barrier(po, "pool")
                barrier(po, "pool")
                eng.dma_start(S0[:, :, :, :].rearrange("p a b t -> p (a b t)"), one(io["s0"][bass.ds(L, 1)])).then_inc(*po.up("state_in", 16))
                for c4 in range(4):
                    for src, dst, ready in ((us_s, ublk, "u_sample"), (tok[:, 0, 2, :], vblk, None)):
                        if ready and c4 == 0:
                            eng.wait_ge(*po.after("u_sample"))
                        if c4 and dst is ublk:
                            eng.wait_ge(*po.after("blk_free"))
                        eng.tensor_tensor(
                            dst[0:NSM, :, :], bc(src[0:NSM, P * c4:P * (c4 + 1)], NB),
                            C("bsel")[0:NSM, :].rearrange("p (b m) -> p b m", m=1).to_broadcast([NSM, NB, P]),
                            ALU.mult).then_inc(*po.up("pool_step"))
                        po.mark("blk_ready")
                eng.wait_ge(*po.after("blk_free"))
                barrier(po, "pool")
            layers(eng, po, body)

        @block.tensor
        def _(eng):
            pe = Lane(eng, sems, marks, found)
            state = {"slab": 0, "A": 0, "V": 0, "last": None}
            eng.wait_ge(*pe.next("inputs_in", 32))

            def use(kind):
                eng.wait_ge(*pe.next("bankA_free" if kind == "A" else "bankV_free"))
                b = (ringA if kind == "A" else ringV)[state[kind] % 4]
                state[kind] += 1
                return b

            def mm(out, lhsT, rhs, start=True, stop=True):
                state["last"] = nc.tensor.matmul(out, lhsT, rhs, start=start, stop=stop, skip_group_check=True)

            def tr(out, in_):
                state["last"] = nc.tensor.transpose(out, in_, C("ident")[0:in_.shape[0], 0:in_.shape[0]])

            def last():
                ins, state["last"] = state["last"], None
                return ins

            def mark(name):
                if state["last"] is not None:
                    state["last"].then_inc(*pe.up("pe_step"))
                    state["last"] = None
                pe.mark(name)

            def slab():
                s = state["slab"] % SLOTS
                state["slab"] += 1
                eng.wait_ge(*pe.next(f"slab_in{s}", 16))
                return ring[:, s, :]

            def dense(s, nk, cols, j, src, kind, k0=0, start=True, stop=True, out=None):
                ps = use(kind) if out is None else out
                sv = s[:, 0:nk * cols].rearrange("p (k n) -> p k n", n=cols)
                for kk_ in range(nk):
                    mm(ps[:, 0:T], sv[:, kk_, P * j:P * (j + 1)], src[:, k0 + kk_, :],
                       start=start and kk_ == 0, stop=stop and kk_ == nk - 1)
                return ps

            def norm():
                eng.wait_ge(*pe.after("squares"))
                ps = use("V")
                for i in range(DC):
                    mm(ps[:, 0:T], C("ones"), sq[:, i, :], start=i == 0, stop=i == DC - 1)
                last().then_inc(*pe.up("bankV_full"))
                eng.wait_ge(*pe.after("h_ready"))

            def ffn():
                norm()
                for j in range(FC // 2):
                    for kind in "AV":
                        s = slab()
                        for i in range(2):
                            dense(s, DC, 256, i, h, kind)
                            last().then_inc(*pe.up(f"bank{kind}_full"))
                        mark_free(1)
                eng.wait_ge(*pe.after("hidden", FC))
                for j in range(4):
                    o = [use("V"), use("V")]
                    for part, (k0, nk) in enumerate(((0, 8), (8, 8), (16, 6))):
                        s = slab()
                        for i in range(2):
                            dense(s, nk, 256, i, hid, "V", k0, part == 0, part == 2, out=o[i])
                            if part == 2:
                                last().then_inc(*pe.up("bankV_full"))
                        mark_free(1)

            def mark_free(n):
                for _ in range(n):
                    mark("slab_used")

            def body(L):
                state.update(slab=0)
                ffn()
                norm()

                def project(n):
                    for _ in range(n):
                        s = slab()
                        for i in range(2):
                            dense(s, DC, 256, i, h, "A")
                            last().then_inc(*pe.up("bankA_full"))
                        mark_free(1)

                project(6)
                s = slab()
                sv = s.rearrange("p (k n) -> p k n", n=256)
                for lo, hi in ((0, HD), (HD, HD + NH)):
                    ps = use("A")
                    for i in range(DC):
                        mm(ps[0:hi - lo, 0:T], sv[:, i, lo:hi], h[:, i, :], i == 0, i == DC - 1)
                    last().then_inc(*pe.up("bankA_full"))
                mark_free(1)
                for name, src, n, m in (("q", q, 4, P), ("k", k, 2, P), ("ki", None, 1, HD)):
                    for i in range(n):
                        if i == 0:
                            eng.wait_ge(*pe.after("head_squares"))
                        ps = use("V")
                        mm(ps[0:m, 0:T], C("blk")[0:m, 0:m], sq[0:m, i, :])
                        last().then_inc(*pe.up("bankV_full"))
                for name, src, n, m in (("q", q, 4, P), ("k", k, 2, P), ("ki", kid, 1, HD), ("qi", qi, 4, P)):
                    eng.wait_ge(*pe.after("to_rotate"))
                    for i in range(n):
                        ps = use("V")
                        mm(ps[0:m, 0:T], C("rot")[0:m, 0:m], src[0:m, :] if src is kid else src[:, i, :])
                        last().then_inc(*pe.up("bankV_full"))
                for i in range(2):
                    ps = use("V")
                    tr(ps[:, 0:NH], wi[:, P * i:P * (i + 1)])
                    last().then_inc(*pe.up("bankV_full"))
                for i in range(3):
                    n = P if i < 2 else NSM
                    ps = use("A")
                    for j in range(2):
                        tr(ps[0:n, P * j:P * (j + 1)], v[:, j, P * i:P * i + n])
                    last().then_inc(*pe.up("bankA_full"))
                ps = use("V")
                mm(ps[:, 0:NSM], C("e8")[0:NH, :], wi[:, NPR:T])
                last().then_inc(*pe.up("bankV_full"))
                eng.wait_ge(*pe.after("rotated"))
                for i in range(2):
                    for pair in PAIRS:
                        ps = use("A")
                        for j, hd in enumerate(pair):
                            rows = half(hd)
                            mm(ps[:, NPR * j:NPR * (j + 1)], qi[rows, hd // 2, P * i:P * (i + 1)], kid[rows, 0:NPR])
                        last().then_inc(*pe.up("bankA_full"))
                eng.wait_ge(*pe.after("sample_queries"))

                def scores(i):
                    kb, grp = i // 2, i % 2
                    ps = use("A")
                    n = 512 if kb < 4 else NSM
                    for b4 in range(4):
                        b = 4 * grp + b4
                        if kb < 4:
                            slot = (NB * kb + b) % 4
                            eng.wait_ge(*pe.next(f"kiblock_in{slot}", 64))
                            rhs = kiring[0:HD, slot, :]
                        else:
                            rhs = kid[0:HD, NPR:T]
                        mm(ps[32 * b4:32 * b4 + 32, 0:n], qi0[0:HD, b, :], rhs)
                        if kb < 4 and b4 < 3:
                            mark("kiblock_free")
                    last().then_inc(*pe.up("bankA_full"))
                    if kb < 4:
                        mark("kiblock_free")

                out = None
                for i in range(11):
                    if i < 10:
                        scores(i)
                    if i >= 1:
                        kb, grp = (i - 1) // 2, (i - 1) % 2
                        n = 512 if kb < 4 else NSM
                        eng.wait_ge(*pe.after("rl_ready"))
                        if grp == 0:
                            out = use("V")
                        mm(out[0:NSM, 0:n], wsel[:, grp, :], rl[:, (i - 1) % 2, 0:n], grp == 0, grp == 1)
                        if grp == 0:
                            mark("rl_read")
                        else:
                            last().then_inc(*pe.up("bankV_full"))
                            mark("rl_read")
                mark("rl_done")
                project(6)
                project(7)
                for i in range(2):
                    eng.wait_ge(*pe.after("prompt_mask"))
                    for pair in PAIRS:
                        ps = use("V")
                        for j, hd in enumerate(pair):
                            rows = half(hd)
                            mm(ps[:, NPR * j:NPR * (j + 1)], q[rows, hd // 2, P * i:P * (i + 1)],
                               kd[rows, hd // 2, 0:NPR])
                        last().then_inc(*pe.up("bankV_full"))
                    for c4 in range(4):
                        eng.wait_ge(*pe.after("prompt_probs"))
                        ps = use("A")
                        for hh in range(2):
                            for kt in range(2):
                                j = 2 * hh + kt
                                tr(ps[:, P * j:P * (j + 1)], pr[:, 2 * c4 + hh, P * kt:P * (kt + 1)])
                        last().then_inc(*pe.up("bankA_full"))
                    for c4 in range(4):
                        eng.wait_ge(*pe.after("prompt_probsT"))
                        ps = use("V")
                        for hh in range(2):
                            for kt in range(2):
                                mm(ps[HD * hh:HD * hh + HD, 0:P], vtok[:, kt, HD * c4:HD * c4 + HD],
                                   prT[:, 4 * c4 + 2 * hh + kt, :], kt == 0, kt == 1)
                        last().then_inc(*pe.up("bankV_full"))
                eng.wait_ge(*pe.after("sample_mask"))
                nblk = 0
                for grp in range(2):
                    for kb in range(5):
                        ps = use("A")
                        n = 512 if kb < 4 else NSM
                        mm(ps[:, 0:n], C(f"exp{grp}")[0:NSM, :], sidx[0:NSM, 512 * kb:512 * kb + n], True, False)
                        for b4 in range(4):
                            if kb < 4:
                                eng.wait_ge(*pe.next(f"kvblock_in{nblk % 4}", 64))
                                kblk = kvring[:, nblk % 4, :].rearrange("p (g k) -> p g k", g=2)
                            for gp in range(2):
                                mm(ps[32 * b4:32 * b4 + 32, 0:n], qz[:, gp, 4 * grp + b4, :],
                                   kblk[:, gp, :] if kb < 4 else k[:, gp, NPR:T], False, b4 == 3 and gp == 1)
                            if kb < 4:
                                nblk += 1
                                if b4 < 3:
                                    mark("kvblock_free")
                        last().then_inc(*pe.up("bankA_full"))
                        if kb < 4:
                            mark("kvblock_free")
                    eng.wait_ge(*pe.after("sample_probs"))
                    for j in range(0, 17, 4):
                        ps = use("A")
                        for i in range(j, min(j + 4, 17)):
                            n = P if i < 16 else NSM
                            tr(ps[0:n, P * (i - j):P * (i - j + 1)], sc[:, P * i:P * i + n])
                        last().then_inc(*pe.up("bankA_full"))
                    eng.wait_ge(*pe.after("sample_probsT"))
                    for b4 in range(4):
                        ps = use("V")
                        for kb in range(4):
                            eng.wait_ge(*pe.next(f"kvblock_in{nblk % 4}", 64))
                            for p in range(4):
                                for gp in range(2):
                                    mm(ps[:, 32 * gp:32 * gp + 32],
                                       kvring[:, nblk % 4, 256 * p + P * gp:256 * p + P * gp + P],
                                       pt[:, 4 * kb + p, 32 * b4:32 * b4 + 32],
                                       kb == 0 and p == 0 and gp == 0, False)
                            nblk += 1
                            mark("kvblock_free")
                        for gp in range(2):
                            mm(ps[:, 32 * gp:32 * gp + 32], vtok[0:NSM, 2, P * gp:P * gp + P],
                               pt[0:NSM, 16, 32 * b4:32 * b4 + 32], False, gp == 1)
                        last().then_inc(*pe.up("bankV_full"))

                eng.wait_ge(*pe.after("lora_in"))
                for c4 in range(4):
                    cols = slice(P * c4, P * (c4 + 1))
                    ps = use("A")
                    mm(ps[:, 0:T], lora[0:HD, 0, cols], lt[0:HD, 0, :])
                    last().then_inc(*pe.up("bankA_full"))
                for c4 in range(4):
                    cols = slice(P * c4, P * (c4 + 1))
                    ps = use("A")
                    mm(ps[:, 0:T], lora[HD:P, 0, cols], us[HD:P, 12, :])
                    last().then_inc(*pe.up("bankA_full"))
                    ps = use("V")
                    mm(ps[:, 0:T], lora[:, 1, cols], us[:, 13, :])
                    last().then_inc(*pe.up("bankV_full"))
                eng.wait_ge(*pe.after("kk_squares"))
                for c4 in range(4):
                    ps = use("A")
                    mm(ps[:, 0:T], C("blk"), sq[:, c4, :])
                    last().then_inc(*pe.up("bankA_full"))
                eng.wait_ge(*pe.after("bonus_in"))
                for c4 in range(4):
                    ps = use("V")
                    mm(ps[:, 0:T], C("blk"), bon[:, c4, :])
                    last().then_inc(*pe.up("bankV_full"))
                eng.wait_ge(*pe.after("tilde_ready"))
                for j, src in enumerate((us[:, 8:12, :], Bt, Kt)):
                    for i in range(3):
                        n = P if i < 2 else NSM
                        ps = use("A")
                        for c4 in range(4):
                            tr(ps[0:n, P * c4:P * (c4 + 1)], src[:, c4, P * i:P * i + n])
                        last().then_inc(*pe.up("bankA_full"))

                def within(i, n):
                    for e, hd in enumerate(range(NH) if n == P else BY_HALF):
                        rows, c4 = half(hd), hd // 2
                        if n == P or e % 4 == 0:
                            ps = use("V")
                        at = 0 if n == P else 4 * n * (e % 4)
                        for j, src in enumerate((Bt, Kt)):
                            mm(ps[0:n, at + 2 * n * j:at + 2 * n * (j + 1)].rearrange("p (a t) -> p a t", a=2),
                               src[rows, c4, P * i:P * i + n], AR[rows, c4, :, P * i:P * i + n])
                        if n == P or e % 4 == 3:
                            last().then_inc(*pe.up("bankV_full"))

                def lower(i, n, hh):
                    ps = use("V")
                    for j, hd in enumerate(range(hh, NH, 2)):
                        rows, c4 = half(hd), hd // 2
                        mm(ps[0:n, n * j:n * (j + 1)], AR[rows, c4, 0, P * i:P * i + n], Bt[rows, c4, P * i:P * i + n])
                    last().then_inc(*pe.up("bankV_full"))

                def four(kind, lhs, rhs, need=None, transpose=None):
                    if need:
                        eng.wait_ge(*pe.after(need))
                    ps = use(kind)
                    for j in range(4):
                        if transpose is not None:
                            tr(ps[:, P * j:P * (j + 1)], transpose[:, j, :])
                        else:
                            mm(ps[:, P * j:P * (j + 1)], lhs(j), rhs(j))
                    last().then_inc(*pe.up(f"bank{kind}_full"))

                at = lambda name: (lambda j: nm[name][:, j, :])

                def values_in(i, n):
                    ps = use("V")
                    for hd in range(NH):
                        lhs = G[0:n, hd, 2 * n:3 * n]
                        mm(ps[0:n, HD * hd:HD * hd + HD], lhs, tok[0:n, 0, i, HD * hd:HD * hd + HD])
                    last().then_inc(*pe.up("bankV_full"))

                s_now = 0
                for i in range(2):
                    eng.wait_ge(*pe.after("chunks_go"))
                    eng.wait_ge(*pe.after("tile_done" if i else "tok_ready"))
                    within(i, P)
                    eng.wait_ge(*pe.after("g_ready"))
                    values_in(i, P)
                    for hh in range(2):
                        lower(i, P, hh)
                        x8 = lambda j, hh=hh: G[:, 2 * j + hh, 0:P]
                        four("A", at("y8"), x8, "y_ready")
                        four("V", x8, at("y8"))
                        eng.wait_ge(*pe.after("x2_ready"))
                        four("V", at("y2"), at("x2"), "y2_ready")
                        four("A", at("iy2"), at("h4"), "h4_ready")
                        four("A", at("iy8"), at("fh"), "fh_ready")
                        four("A", None, None, "dd_ready", nm["dd"])
                        four("A", at("yo16"), at("dd"))
                        four("V", at("dt"), at("qq"), "dtqq_ready")
                        four("A", None, None, "t16_ready", t16)
                        four("A", at("yo32"), lambda j: t16[:, j, :])
                        four("V", at("dt"), at("qq"), "dtqq_ready")
                    eng.wait_ge(*pe.after("t_ready"))
                    for cc in range(4):
                        o, t0 = 32 * cc, P * i + 32 * cc
                        eng.wait_ge(*pe.after("s_ready"))
                        ps = use("V")
                        for c4 in range(4):
                            mm(ps[o:o + 32, P * c4:P * (c4 + 1)], AR[:, c4, 0, t0:t0 + 32], S[s_now][:, c4, :])
                        last().then_inc(*pe.up("bankV_full"))
                        eng.wait_ge(*pe.after("r1_ready"))
                        ps = use("A")
                        for hd in range(NH):
                            mm(ps[o:o + 32, HD * hd:HD * hd + HD], Ti[o:o + 32, hd, o:o + 32],
                               R1[o:o + 32, HD * hd:HD * hd + HD])
                        last().then_inc(*pe.up("bankA_full"))
                        eng.wait_ge(*pe.after("u_ready"))
                        ps = use("V")
                        for c4 in range(4):
                            pc_ = slice(P * c4, P * (c4 + 1))
                            mm(ps[:, pc_], tok[o:o + 32, 1, i, pc_], U[o:o + 32, pc_], True, False)
                            mm(ps[:, pc_], tok[o:o + 32, 2, i, pc_], tok[o:o + 32, 0, i, pc_], False, True)
                        last().then_inc(*pe.up("bankV_full"))
                        ps = use("A")
                        for c4 in range(4):
                            mm(ps[:, 32 * c4:32 * c4 + 32], S[s_now][:, c4, :], AR[:, c4, 1, t0:t0 + 32], c4 == 0, False)
                        for hd in range(NH):
                            c4, hc = hd // 2, slice(HD * hd, HD * hd + HD)
                            to = ps[half(hd), 32 * c4:32 * c4 + 32]
                            mm(to, U[o:o + 32, hc], G[o:o + 32, hd, P + o:P + o + 32], False, False)
                            mm(to, tok[o:o + 32, 0, i, hc], G[o:o + 32, hd, 3 * P + o:3 * P + o + 32], False, True)
                        last().then_inc(*pe.up("bankA_full"))
                        s_now = 1 - s_now
                n, i = NSM, 2
                eng.wait_ge(*pe.after("chunks_go"))
                eng.wait_ge(*pe.after("tile_done"))
                eng.wait_ge(*pe.next("state_in", 16))
                within(i, n)
                lower(i, n, 0)
                lower(i, n, 1)
                eng.wait_ge(*pe.after("g_ready"))
                values_in(i, n)
                ps = use("A")
                for hd in range(NH):
                    mm(ps[0:n, n * hd:n * (hd + 1)], nm["y8"][0:n, :, :].rearrange("p a b -> p (a b)")[:, n * hd:n * (hd + 1)],
                       G[0:n, hd, 0:n])
                last().then_inc(*pe.up("bankA_full"))
                for hh in range(2):
                    ps = use("A")
                    rows = half(hh)
                    for c4 in range(4):
                        for b in range(NB):
                            mm(ps[rows, n * c4 + NS * b:n * c4 + NS * b + NS], S0[rows, c4, b, :],
                               AR[rows, c4, 0, NPR + NS * b:NPR + NS * b + NS])
                    last().then_inc(*pe.up("bankA_full"))
                eng.wait_ge(*pe.after("hs_ready"))
                ps = use("A")
                for hd in range(NH):
                    mm(ps[0:n, n * hd:n * (hd + 1)], nm["iy8"][0:n, :, :].rearrange("p a b -> p (a b)")[:, n * hd:n * (hd + 1)],
                       hs[0:n, n * hd:n * (hd + 1)])
                last().then_inc(*pe.up("bankA_full"))
                eng.wait_ge(*pe.after("zt_ready"))
                ps = use("V")
                for c4 in range(4):
                    mm(ps[0:n, P * c4:P * (c4 + 1)], zT[:, c4, :], C("ident"))
                last().then_inc(*pe.up("bankV_full"))
                eng.wait_ge(*pe.after("r1_ready"))
                eng.wait_ge(*pe.after("inverse_ready"))
                ps = use("A")
                for hd in range(NH):
                    hc = slice(HD * hd, HD * hd + HD)
                    mm(ps[0:n, hc], xs2[0:n, n * hd:n * (hd + 1)], R1[0:n, hc])
                last().then_inc(*pe.up("bankA_full"))
                eng.wait_ge(*pe.after("u_ready"))
                for hh in range(2):
                    ps = use("A")
                    rows = half(hh)
                    for c4 in range(4):
                        hd, hc = 2 * c4 + hh, slice(HD * (2 * c4 + hh), HD * (2 * c4 + hh) + HD)
                        to = ps[rows, n * c4:n * (c4 + 1)]
                        mm(to, us_s[0:n, hc], G[0:n, hd, n:2 * n], True, False)
                        mm(to, tok[0:n, 0, 2, hc], G[0:n, hd, 3 * n:4 * n], False, False)
                        for b in range(NB):
                            mm(ps[rows, n * c4 + NS * b:n * c4 + NS * b + NS], S0[rows, c4, b, :],
                               AR[rows, c4, 1, NPR + NS * b:NPR + NS * b + NS], False, b == NB - 1)
                    last().then_inc(*pe.up("bankA_full"))
                for c4 in range(4):
                    eng.wait_ge(*pe.after("blk_ready", 2))
                    ps = use("V")
                    for hh in range(2):
                        hc = slice(P * c4 + HD * hh, P * c4 + HD * hh + HD)
                        to = ps[HD * hh:HD * hh + HD, :].rearrange("p (b i) -> p b i", b=NB)
                        mm(to, tok[0:n, 1, 2, hc], ublk[0:n, :, HD * hh:HD * hh + HD], True, False)
                        mm(to, tok[0:n, 2, 2, hc], vblk[0:n, :, HD * hh:HD * hh + HD], False, True)
                    last().then_inc(*pe.up("bankV_full"))
                    mark("blk_free")
                for name in ("o_ready", "o_squares"):
                    eng.wait_ge(*pe.after(name))
                    for c4 in range(4):
                        ps = use("V")
                        mm(ps[:, 0:T], C("blk"), oa[:, c4, :] if name == "o_ready" else sq[:, c4, :])
                        last().then_inc(*pe.up("bankV_full"))
                eng.wait_ge(*pe.after("branches_ready"))
                for cp in range(4):
                    pab = pc = None
                    for br in range(3):
                        gs = slab()
                        for j in range(2):
                            dense(gs, DC, 256, j, h, "A")
                            last().then_inc(*pe.up("bankA_full"))
                        if br == 0:
                            pab = slab()
                        if br == 2:
                            pass
                        wslab = pab if br < 2 else pc
                        if br == 2:
                            wslab = pc = slab()
                        off = 1024 if br == 1 else 0
                        for j in range(2):
                            dense(wslab[:, off:off + 1024], 4, 256, j, (oa, ob, oc)[br], "V")
                            last().then_inc(*pe.up("bankV_full"))
                        mark_free(1 if br == 0 else 2)
                eng.wait_ge(*pe.after("merged"))
                for _ in range(4):
                    s = slab()
                    for j in range(2):
                        dense(s, DC, 256, j, sq, "V")
                        last().then_inc(*pe.up("bankV_full"))
                    mark_free(1)
                ffn()
                norm()
                for cp in range(4):
                    for kind, src, nk in (("A", h, DC), ("V", ptk, 2)):
                        s = slab()
                        for j in range(2):
                            dense(s, nk, 256, j, src, kind)
                            last().then_inc(*pe.up(f"bank{kind}_full"))
                        mark_free(1)
                assert state["slab"] == NSLAB, state
            layers(eng, pe, body)

        @block.scalar
        def _(eng):
            ac = Lane(eng, sems, marks, found)
            state = {"A": 0}
            a = nc.scalar.activation
            for _ in range(4):
                eng.nop().then_inc(*ac.up("bankA_free"))
            eng.wait_ge(*ac.next("inputs_in", 32))

            def take():
                eng.wait_ge(*ac.next("bankA_full"))
                b = ringA[state["A"] % 4]
                state["A"] += 1
                return b

            def norm():
                eng.wait_ge(*ac.after("x_ready"))
                a(sq[:, :, :], x[:, :, :], ACT.Square).then_inc(*ac.up("act_step"))
                ac.mark("squares")
                eng.wait_ge(*ac.after("mean_square"))
                a(rstd[:, :], rstd[:, :], ACT.Sqrt).then_inc(*ac.up("act_step"))
                ac.mark("root")

            def ffn():
                norm()
                for j in range(FC):
                    ps = take()
                    a(hid[:, j, :], ps[:, 0:T], ACT.Silu).then_inc(*ac.up("bankA_free"))
                    ac.mark("silu")

            def rows2(ap, b, n):
                return ap.rearrange("p (b s) -> p b s", b=b)[:, :, 0:n]

            def body(L):
                one = lambda ap: ap[bass.ds(L, 1)].rearrange("a p n -> (a p) n")
                ffn()
                norm()
                for dst, n in ((q, 4), (k, 2), (v, 2), (qi, 4)):
                    for i in range(n):
                        a(dst[:, i, :], take()[:, 0:T], ACT.Copy).then_inc(*ac.up("bankA_free"))
                a(kid[0:HD, :], take()[0:HD, 0:T], ACT.Copy).then_inc(*ac.up("bankA_free"))
                a(wi[:, :], take()[0:NH, 0:T], ACT.Copy).then_inc(*ac.up("bankA_free"))
                eng.wait_ge(*ac.own())
                for src, n, m in ((q, 4, P), (k, 2, P), (kid, 1, HD)):
                    if src is not q:
                        eng.wait_ge(*ac.after("sums_taken"))
                    if src is kid:
                        a(sq[0:m, 0, :], kid[0:m, :], ACT.Square).then_inc(*ac.up("act_step"))
                        ac.mark("head_squares")
                    else:
                        a(sq[:, 0:n, :], src[:, :, :], ACT.Square).then_inc(*ac.up("act_step"))
                        ac.mark("head_squares")
                    eng.wait_ge(*ac.after("head_means"))
                    a(sq[0:m, 4:4 + n, :], sq[0:m, 4:4 + n, :], ACT.Sqrt).then_inc(*ac.up("act_step"))
                    ac.mark("head_roots")
                for i in range(3):
                    n = P if i < 2 else NSM
                    a(vtok[0:n, i, :], take()[0:n, 0:256], ACT.Copy).then_inc(*ac.up("bankA_free"))
                eng.wait_ge(*ac.after("rope_done"))
                for dst in range(2):
                    to = slice(HD * dst, HD * dst + HD)
                    for gh in range(2):
                        a(kd[to, gh:4:2, :], k[HD * gh:HD * gh + HD, :, :], ACT.Copy).then_inc(*ac.up("act_step"))
                a(kid[HD:P, :], kid[0:HD, :], ACT.Copy).then_inc(*ac.up("act_step"))
                ac.mark("rotated")
                for b in range(NB):
                    tk = slice(NPR + NS * b, NPR + NS * b + NS)
                    for hh in range(2):
                        src = slice(HD * hh, HD * hh + HD)
                        a(qi0[0:HD, b, :].rearrange("p (h t) -> p h t", t=NS)[:, hh::2, :], qi[src, :, tk], ACT.Copy).then_inc(*ac.up("act_step"))
                eng.wait_ge(*ac.after("qz_clear"))
                for c4 in range(4):
                    to = slice(HD * (c4 % 2), HD * (c4 % 2) + HD)
                    for hh in range(2):
                        hd = 2 * c4 + hh
                        a(qz[to, c4 // 2, :, NS * hd:NS * hd + NS],
                               q[HD * hh:HD * hh + HD, c4, NPR:T].rearrange("p (b t) -> p b t", t=NS), ACT.Copy).then_inc(*ac.up("act_step"))
                ac.mark("sample_queries")
                for dst, src in (("k_out", k), ("v_out", v)):
                    eng.dma_start(one(io[dst]), src[:, :, :].rearrange("p a t -> p (a t)")).then_inc(*ac.up("kv_out", 16))
                eng.dma_start(one(io["ki_out"]), kid[0:HD, :]).then_inc(*ac.up("kv_out", 16))
                for i in range(8):
                    if i >= 2:
                        eng.wait_ge(*ac.after("rl_read_v"))
                    a(rl[:, i % 2, :], take(), ACT.Relu, scale=0.125).then_inc(*ac.up("bankA_free"))
                    ac.mark("rl_prompt")
                eng.wait_ge(*ac.after("rl_read_v", 2))
                for i in range(10):
                    if i >= 2:
                        eng.wait_ge(*ac.after("rl_read"))
                    n = 512 if i < 8 else NSM
                    a(rl[:, i % 2, 0:n], take()[:, 0:n], ACT.Relu, scale=0.125).then_inc(*ac.up("bankA_free"))
                    ac.mark("rl_ready")
                eng.wait_ge(*ac.after("rl_read", 2))
                for dst in (bgate, cgate):
                    for i in range(4):
                        a(dst[:, i, :], take()[:, 0:T], ACT.Copy).then_inc(*ac.up("bankA_free"))
                for i in range(4):
                    ps = take()
                    a(zx[:, i, 2:2 + NPR], ps[:, 0:NPR], ACT.Copy).then_inc(*ac.up("act_step"))
                    a(zx[:, i, 2 + NPR:ZX].rearrange("p (b s) -> p b s", b=NB)[:, :, 2:2 + NS],
                           ps[:, NPR:T].rearrange("p (b t) -> p b t", t=NS), ACT.Copy).then_inc(*ac.up("bankA_free"))
                ac.mark("conv_in")
                for i in range(UC):
                    ps = take()
                    a(uext[:, i, 1:1 + NPR], ps[:, 0:NPR], ACT.Copy).then_inc(*ac.up("act_step"))
                    a(uext[:, i, 1 + NPR:UX].rearrange("p (b s) -> p b s", b=NB)[:, :, 1:1 + NS],
                           ps[:, NPR:T].rearrange("p (b t) -> p b t", t=NS), ACT.Copy).then_inc(*ac.up("bankA_free"))
                ac.mark("u_in")
                for i in range(2):
                    for pos, hd in enumerate(sum(PAIRS, ())):
                        if pos % 2 == 0:
                            eng.wait_ge(*ac.after("prompt_max"))
                        a(pr[:, hd, :], pr[:, hd, :], ACT.Exp, bias=stat[:, 8 + hd:9 + hd], scale=0.125,
                               accum_out=stat[:, 16 + hd:17 + hd]).then_inc(*ac.up("act_step"))
                        ac.mark("prompt_exp")
                    for c4 in range(4):
                        a(prT[:, 4 * c4:4 * c4 + 4, :].rearrange("p a b -> p (a b)"), take(), ACT.Copy).then_inc(*ac.up("bankA_free"))
                        ac.mark("prompt_probsT")
                for grp in range(2):
                    if grp == 0:
                        eng.wait_ge(*ac.after("prompt_out"))
                    for kb in range(5):
                        n = 512 if kb < 4 else NSM
                        a(sc[:, 512 * kb:512 * kb + n], take()[:, 0:n], ACT.Copy).then_inc(*ac.up("bankA_free"))
                    ac.mark("sample_scores")
                    eng.wait_ge(*ac.after("sample_max"))
                    a(sc[:, :], sc[:, :], ACT.Exp, bias=stat[:, 25:26], scale=0.125, accum_out=stat[:, 26:27]).then_inc(*ac.up("act_step"))
                    ac.mark("sample_exp")
                    for j in range(0, 17, 4):
                        n, m = (P, 512) if j < 16 else (NSM, P)
                        a(pt[0:n, j:j + m // P, :].rearrange("p a b -> p (a b)"), take()[0:n, 0:m], ACT.Copy).then_inc(*ac.up("bankA_free"))
                    ac.mark("sample_probsT")
                eng.wait_ge(*ac.next("kv_out", 48))
                barrier(ac, "act")
                eng.wait_ge(*ac.after("us_ready"))
                a(lt[0:HD, 0, :], us[0:HD, 12, :], ACT.Tanh).then_inc(*ac.up("act_step"))
                a(us[:, 13, :], us[:, 13, :], ACT.Sigmoid).then_inc(*ac.up("act_step"))
                ac.mark("lora_in")
                for i in range(4):
                    ps = take()
                    a(pcum[:, i, :], ps[:, 0:T], ACT.Sigmoid, bias=prm[:, PCOL["w0"] + i:PCOL["w0"] + i + 1]).then_inc(*ac.up("bankA_free"))
                for i in range(4):
                    ps = take()
                    a(aa[:, i, :], ps[:, 0:T], ACT.Sigmoid, bias=prm[:, PCOL["a0"] + i:PCOL["a0"] + i + 1]).then_inc(*ac.up("bankA_free"))
                eng.wait_ge(*ac.own())
                a(dec[:, :, :], pcum[:, :, :], ACT.Exp, scale=-float(np.exp(-0.5))).then_inc(*ac.up("act_step"))
                eng.wait_ge(*ac.after("kk_raw"))
                a(sq[:, 0:4, :], kk[:, :, :], ACT.Square).then_inc(*ac.up("act_step"))
                ac.mark("kk_squares")
                eng.wait_ge(*ac.after("sho_ready"))
                eng.dma_start(one(io["shift_out"]), sho[:, :, :].rearrange("p a t -> p (a t)")).then_inc(*ac.up("small_out", 16))
                eng.dma_start(one(io["conv_out"]), cvo[:, :, :, :].rearrange("p a b t -> p (a b t)")).then_inc(*ac.up("small_out", 16))
                for i in range(4):
                    ps = take()
                    a(sq[:, 4 + i, :], ps[:, 0:T], ACT.Sqrt).then_inc(*ac.up("bankA_free"))
                ac.mark("kk_norm")
                barrier(ac, "act")
                for j in range(3):
                    for i in range(3):
                        n = P if i < 2 else NSM
                        a(tok[0:n, j, i, :], take()[0:n, :], ACT.Copy).then_inc(*ac.up("bankA_free"))
                ac.mark("tok_ready")
                for i in range(2):
                    for hb in (0, 4):
                        for names, ready in ((("x2",), "x2_ready"), (("fh",), "fh_ready"), (("dd",), "dd_ready"),
                                             (("dt", "qq"), "dtqq_ready"), (("dt", "qq"), "dtqq_ready")):
                            for name in names:
                                a(nm[name][:, :, :].rearrange("p a b -> p (a b)"), take(), ACT.Copy).then_inc(*ac.up("bankA_free"))
                            eng.wait_ge(*ac.own())
                            ac.mark(ready)
                    for cc in range(4):
                        o, t0 = 32 * cc, P * i + 32 * cc
                        a(U[o:o + 32, :], take()[o:o + 32, :], ACT.Copy).then_inc(*ac.up("bankA_free"))
                        ac.mark("u_ready")
                        a(oa[:, :, t0:t0 + 32], chunk4(take()[:, 0:P]), ACT.Copy).then_inc(*ac.up("bankA_free"))
                        ac.mark("o_read")
                    ac.mark("tile_done")
                a(xs2[0:NSM, :], take()[0:NSM, 0:256], ACT.Copy).then_inc(*ac.up("bankA_free"))
                for hh in range(2):
                    a(zT[half(hh), :, :].rearrange("p a b -> p (a b)"), take()[half(hh), 0:P], ACT.Copy).then_inc(*ac.up("bankA_free"))
                ac.mark("xs2_ready")
                ac.mark("zt_ready")
                eng.wait_ge(*ac.after("hs_made"))
                a(xs2[0:NSM, :], take()[0:NSM, 0:256], ACT.Copy).then_inc(*ac.up("bankA_free"))
                ac.mark("inverse_ready")
                a(us_s[0:NSM, :], take()[0:NSM, :], ACT.Copy).then_inc(*ac.up("bankA_free"))
                ac.mark("u_ready")
                ac.mark("u_sample")
                for hh in range(2):
                    a(oa[half(hh), :, NPR:T], chunk4(take()[half(hh), 0:P]), ACT.Copy).then_inc(*ac.up("bankA_free"))
                ac.mark("o_ready")
                eng.wait_ge(*ac.after("prompt_state"))
                for hh in range(2):
                    eng.dma_start(
                        one(io["s_out"]).rearrange("p (c b i) -> p c b i", c=4, b=NB + 1)[half(hh), :, NB, :],
                        S[0][half(hh), :, half(hh)]).then_inc(*ac.up("small_out", 16))
                eng.wait_ge(*ac.next("small_out", 64))
                eng.wait_ge(*ac.after("o_centred"))
                a(sq[:, 0:4, :], oa[:, :, :], ACT.Square).then_inc(*ac.up("act_step"))
                ac.mark("o_squares")
                eng.wait_ge(*ac.after("o_var"))
                a(sq[:, 4:8, :], sq[:, 4:8, :], ACT.Sqrt).then_inc(*ac.up("act_step"))
                ac.mark("o_root")
                eng.wait_ge(*ac.after("state_ready"))
                eng.dma_start(one(io["s_out"]).rearrange("p (c b i) -> p c b i", c=4, b=NB + 1)[:, :, 0:NB, :],
                                     S0[:, :, :, :]).then_inc(*ac.up("small_out", 16))
                eng.wait_ge(*ac.next("small_out", 16))
                barrier(ac, "act")
                for cp in range(4):
                    for br in range(3):
                        for j in range(2):
                            if cp or br:
                                eng.wait_ge(*ac.after("gate_free"))
                            a(gate[:, j, :], take()[:, 0:T], ACT.Sigmoid).then_inc(*ac.up("bankA_free"))
                            ac.mark("gate_ready")
                eng.wait_ge(*ac.after("gate_free", 2))
                ffn()
                norm()
                for cp in range(4):
                    for j in range(2):
                        if cp:
                            eng.wait_ge(*ac.after("gate_free"))
                        a(gate[:, j, :], take()[:, 0:T], ACT.Sigmoid).then_inc(*ac.up("bankA_free"))
                        ac.mark("gate_ready")
                eng.wait_ge(*ac.after("gate_free", 2))
            layers(eng, ac, body)
            eng.wait_ge(*ac.after("x_final", DEPTH))
            eng.dma_start(io["y_out"], x[:, :, :]).then_inc(sems("y_out"), 16)
            eng.wait_ge(sems("y_out"), 16)

        @block.vector
        def _(eng):
            ve = Lane(eng, sems, marks, found)
            state = {"V": 0}
            tt, ts, stt = nc.vector.tensor_tensor, nc.vector.tensor_scalar, nc.vector.scalar_tensor_tensor
            cp = nc.vector.tensor_copy
            for _ in range(4):
                eng.nop().then_inc(*ve.up("bankV_free"))
            eng.wait_ge(*ve.next("inputs_in", 32))
            eng.nop().then_inc(*ve.up("dve_step"))
            ve.mark("x_ready")

            def take():
                eng.wait_ge(*ve.next("bankV_full"))
                b = ringV[state["V"] % 4]
                state["V"] += 1
                return b

            pc = lambda name, i=0: prm[:, PCOL[name] + i:PCOL[name] + i + 1]

            def norm(gain):
                ts(rstd[:, :], take()[:, 0:T], 1.0 / D, EPS, ALU.mult, ALU.add).then_inc(*ve.up("bankV_free"))
                eng.wait_ge(*ve.own())
                ve.mark("mean_square")
                eng.wait_ge(*ve.after("root"))
                nc.vector.reciprocal(rstd[:, :], rstd[:, :]).then_inc(*ve.up("dve_step"))
                eng.wait_ge(*ve.own())
                for i in range(DC):
                    stt(h[:, i, :], x[:, i, :], pc(gain, i), rstd[:, :], ALU.mult, ALU.mult).then_inc(*ve.up("dve_step"))
                ve.mark("h_ready")

            def ffn(gain):
                norm(gain)
                for j in range(FC):
                    eng.wait_ge(*ve.after("silu"))
                    tt(hid[:, j, :], take()[:, 0:T], hid[:, j, :], ALU.mult).then_inc(*ve.up("bankV_free"))
                    eng.wait_ge(*ve.own())
                    ve.mark("hidden")
                for j in range(DC):
                    stt(x[:, j, :], take()[:, 0:T], 0.5, x[:, j, :], ALU.mult, ALU.add).then_inc(*ve.up("bankV_free"))
                ve.mark("x_ready")

            def body(L):
                ve.mark("layer_ready")
                eng.wait_ge(*ve.next("params_in", 80))
                ffn("ffn1")
                ve.mark("ffn1_done")
                norm("mix")
                nc.vector.memset(qz[:, :, :, :], 0.0).then_inc(*ve.up("dve_step"))
                eng.wait_ge(*ve.own())
                ve.mark("qz_clear")
                for src, n, m, gain in ((q, 4, P, "qn"), (k, 2, P, "kn"), (kid, 1, HD, "in")):
                    for i in range(n):
                        ts(sq[0:m, 4 + i, :], take()[0:m, 0:T], 1.0 / HD, EPS, ALU.mult, ALU.add).then_inc(*ve.up("bankV_free"))
                    ve.mark("head_means")
                    eng.wait_ge(*ve.after("head_roots"))
                    nc.vector.reciprocal(sq[0:m, 4:4 + n, :], sq[0:m, 4:4 + n, :]).then_inc(*ve.up("dve_step"))
                    eng.wait_ge(*ve.own())
                    for i in range(n):
                        ap = kid[0:m, :] if src is kid else src[:, i, :]
                        stt(ap, ap, prm[0:m, PCOL[gain]:PCOL[gain] + 1], sq[0:m, 4 + i, :], ALU.mult, ALU.mult).then_inc(*ve.up("dve_step"))
                    eng.wait_ge(*ve.own())
                    if src is not kid:
                        ve.mark("sums_taken")
                    ve.mark("to_rotate")
                ve.mark("to_rotate")
                for src, n, m in ((q, 4, P), (k, 2, P), (kid, 1, HD), (qi, 4, P)):
                    for i in range(n):
                        ap = kid[0:m, :] if src is kid else src[:, i, :]
                        tt(rot_t[0:m, :], take()[0:m, 0:T], C("sin")[0:m, :], ALU.mult).then_inc(*ve.up("bankV_free"))
                        tt(ap, ap, C("cos")[0:m, :], ALU.mult).then_inc(*ve.up("dve_step"))
                        eng.wait_ge(*ve.own())
                        tt(ap, ap, rot_t[0:m, :], ALU.add).then_inc(*ve.up("dve_step"))
                        eng.wait_ge(*ve.own())
                ve.mark("rope_done")
                for i in range(2):
                    ts(witok[:, i, :], take()[:, 0:NH], float(np.float32(NH ** -0.5)), None, ALU.mult).then_inc(*ve.up("bankV_free"))
                    if i == 1:
                        eng.wait_ge(*ve.own())
                ps = take()
                tt(wsel[:, 0, :], ps[:, 0:NSM], C("wsel0"), ALU.mult).then_inc(*ve.up("dve_step"))
                tt(wsel[:, 1, :], ps[:, 0:NSM], C("wsel1"), ALU.mult).then_inc(*ve.up("bankV_free"))
                ve.mark("wsel_ready")
                for i in range(2):
                    for n, pair in enumerate(PAIRS):
                        eng.wait_ge(*ve.after("rl_prompt"))
                        for j, hd in enumerate(pair):
                            before = C("causal")[:, NPR * i:NPR * (i + 1)] if n + j == 0 else seenP[:, i, :]
                            stt(seenP[:, i, :], rl[:, (4 * i + n) % 2, NPR * j:NPR * (j + 1)], witok[:, i, hd:hd + 1],
                                   before, ALU.mult, ALU.add).then_inc(*ve.up("dve_step"))
                            eng.wait_ge(*ve.own())
                        ve.mark("rl_read_v")
                for kb in range(5):
                    n = 512 if kb < 4 else NSM
                    ps = take()
                    if kb < 4:
                        cp(sidx[0:NSM, 512 * kb:512 * kb + n], ps[0:NSM, 0:n]).then_inc(*ve.up("bankV_free"))
                    else:
                        tt(sidx[0:NSM, PAST:KEYS], ps[0:NSM, 0:n], C("cs")[0:NSM, :], ALU.add).then_inc(*ve.up("bankV_free"))
                        eng.wait_ge(*ve.own())

                def choose(ap, k_, m):
                    for _ in range(k_ // 8):
                        nc.vector.max(out=m8[0:m, :], in_=ap).then_inc(*ve.up("dve_step"))
                        eng.wait_ge(*ve.own())
                        nc.vector.match_replace(out=ap, in_to_replace=m8[0:m, :], in_values=ap, imm_value=TAKEN).then_inc(*ve.up("dve_step"))
                        eng.wait_ge(*ve.own())

                for i in range(2):
                    choose(seenP[:, i, :], TOPK_P, P)
                    ts(seenP[:, i, :], seenP[:, i, :], TAKEN / 2, NEG, ALU.is_gt, ALU.mult).then_inc(*ve.up("dve_step"))
                    eng.wait_ge(*ve.own())
                    tt(seenP[:, i, :], seenP[:, i, :], C("causal")[:, NPR * i:NPR * (i + 1)], ALU.add).then_inc(*ve.up("dve_step"))
                    eng.wait_ge(*ve.own())
                    ve.mark("prompt_mask")
                choose(sidx[0:NSM, :], TOPK_S, NSM)
                ts(sidx[0:NSM, :], sidx[0:NSM, :], TAKEN / 2, NEG, ALU.is_gt, ALU.mult).then_inc(*ve.up("dve_step"))
                eng.wait_ge(*ve.own())
                ve.mark("sample_mask")
                nc.vector.memset(zx[:, :, 0:2], 0.0).then_inc(*ve.up("dve_step"))
                eng.wait_ge(*ve.own())
                for i in range(4):
                    cp(zx[:, i, 2 + NPR:ZX].rearrange("p (b s) -> p b s", b=NB)[:, :, 0:2], scv[:, i, :, :]).then_inc(*ve.up("dve_step"))
                    eng.wait_ge(*ve.own())
                eng.wait_ge(*ve.after("conv_in"))
                for i in range(4):
                    zp = zx[:, i, 0:2 + NPR]
                    zs = zx[:, i, 2 + NPR:ZX].rearrange("p (b s) -> p b s", b=NB)
                    c_s = cgate[:, i, NPR:T].rearrange("p (b t) -> p b t", t=NS)
                    o_s = ob[:, i, NPR:T].rearrange("p (b t) -> p b t", t=NS)
                    tt(zp[:, 2:], zp[:, 2:], cgate[:, i, 0:NPR], ALU.mult).then_inc(*ve.up("dve_step"))
                    tt(zs[:, :, 2:], zs[:, :, 2:], c_s, ALU.mult).then_inc(*ve.up("dve_step"))
                    eng.wait_ge(*ve.own())
                    cp(cvo[:, i, NB, :], zp[:, NPR:NPR + 2]).then_inc(*ve.up("dve_step"))
                    cp(cvo[:, i, 0:NB, :], zs[:, :, NS:NS + 2]).then_inc(*ve.up("dve_step"))
                    for j in range(3):
                        wj = pc("cw", 4 * j + i)
                        if j == 0:
                            ts(ob[:, i, 0:NPR], zp[:, 0:NPR], wj, None, ALU.mult).then_inc(*ve.up("dve_step"))
                            ts(o_s, zs[:, :, 0:NS], wj, None, ALU.mult).then_inc(*ve.up("dve_step"))
                            eng.wait_ge(*ve.own())
                        else:
                            stt(ob[:, i, 0:NPR], zp[:, j:j + NPR], wj, ob[:, i, 0:NPR], ALU.mult, ALU.add).then_inc(*ve.up("dve_step"))
                            stt(o_s, zs[:, :, j:j + NS], wj, o_s, ALU.mult, ALU.add).then_inc(*ve.up("dve_step"))
                            eng.wait_ge(*ve.own())
                tt(ob[:, :, :], ob[:, :, :], bgate[:, :, :], ALU.mult).then_inc(*ve.up("dve_step"))
                eng.wait_ge(*ve.own())
                for i in range(2):
                    for pair in PAIRS:
                        two = pr[:, pair[0]:pair[1] + 1:2, :]
                        tt(two, take()[:, :].rearrange("p (a b) -> p a b", a=2), bc(seenP[:, i, :], 2), ALU.add).then_inc(*ve.up("bankV_free"))
                        eng.wait_ge(*ve.own())
                        nc.vector.tensor_reduce(stat[:, pair[0]:pair[1] + 1:2], two, AX.X, ALU.max).then_inc(*ve.up("dve_step"))
                        eng.wait_ge(*ve.own())
                        ts(stat[:, 8 + pair[0]:9 + pair[1]:2], stat[:, pair[0]:pair[1] + 1:2], -0.125, None, ALU.mult).then_inc(*ve.up("dve_step"))
                        eng.wait_ge(*ve.own())
                        ve.mark("prompt_max")
                    for c4 in range(4):
                        if c4 % 2 == 0:
                            eng.wait_ge(*ve.after("prompt_exp", 4))
                        nc.vector.reciprocal(stat[:, 32 + 2 * c4:34 + 2 * c4], stat[:, 16 + 2 * c4:18 + 2 * c4]).then_inc(*ve.up("dve_step"))
                        eng.wait_ge(*ve.own())
                        for hd in (2 * c4, 2 * c4 + 1):
                            ts(pr[:, hd, :], pr[:, hd, :], stat[:, 32 + hd:33 + hd], None, ALU.mult).then_inc(*ve.up("dve_step"))
                        ve.mark("prompt_probs")
                    for c4 in range(4):
                        cp(oc[:, c4, P * i:P * (i + 1)], take()[:, 0:P]).then_inc(*ve.up("bankV_free"))
                ve.mark("prompt_out")
                for grp in range(2):
                    eng.wait_ge(*ve.after("sample_scores"))
                    nc.vector.tensor_reduce(stat[:, 24:25], sc[:, :], AX.X, ALU.max).then_inc(*ve.up("dve_step"))
                    eng.wait_ge(*ve.own())
                    ts(stat[:, 25:26], stat[:, 24:25], -0.125, None, ALU.mult).then_inc(*ve.up("dve_step"))
                    eng.wait_ge(*ve.own())
                    ve.mark("sample_max")
                    eng.wait_ge(*ve.after("sample_exp"))
                    nc.vector.reciprocal(stat[:, 27:28], stat[:, 26:27]).then_inc(*ve.up("dve_step"))
                    eng.wait_ge(*ve.own())
                    ts(sc[:, :], sc[:, :], stat[:, 27:28], None, ALU.mult).then_inc(*ve.up("dve_step"))
                    eng.wait_ge(*ve.own())
                    ve.mark("sample_probs")
                    for b4 in range(4):
                        cp(ov[:, :, 4 * grp + b4, :], take()[:, 0:64].rearrange("p (g r) -> p g r", g=2)).then_inc(*ve.up("bankV_free"))
                eng.wait_ge(*ve.own())
                for c4 in range(4):
                    for hh in range(2):
                        hd = 2 * c4 + hh
                        cp(oc[HD * hh:HD * hh + HD, c4, NPR:T].rearrange("p (b t) -> p b t", t=NS),
                              ov[HD * (c4 % 2):HD * (c4 % 2) + HD, c4 // 2, :, NS * hd:NS * hd + NS]).then_inc(*ve.up("dve_step"))
                eng.wait_ge(*ve.after("u_in"))
                barrier(ve, "dve")
                nc.vector.memset(uext[:, :, 0:1], 0.0).then_inc(*ve.up("dve_step"))
                sv = uext[:, :, 1 + NPR:UX].rearrange("p a (b s) -> p a b s", b=NB)
                cp(sv[:, :, :, 0], sft[:, :, :]).then_inc(*ve.up("dve_step"))
                eng.wait_ge(*ve.own())
                cp(sho[:, :, NB], uext[:, :, NPR]).then_inc(*ve.up("dve_step"))
                cp(sho[:, :, 0:NB], sv[:, :, :, NS]).then_inc(*ve.up("dve_step"))
                ve.mark("sho_ready")
                for i in range(UC):
                    d = sq[:, (i % 2) * 2:(i % 2) * 2 + 2, :].rearrange("p a t -> p (a t)")[:, 0:UX - 1]
                    tt(d, uext[:, i, 0:UX - 1], uext[:, i, 1:UX], ALU.subtract).then_inc(*ve.up("dve_step"))
                    eng.wait_ge(*ve.own())
                    stt(us[:, i, 0:NPR], d[:, 0:NPR], pc("mu", i), uext[:, i, 1:1 + NPR], ALU.mult, ALU.add).then_inc(*ve.up("dve_step"))
                    ds_ = d[:, NPR:NPR + NB * (NS + 1)].rearrange("p (b s) -> p b s", b=NB)[:, :, 1:1 + NS]
                    stt(us[:, i, NPR:T].rearrange("p (b t) -> p b t", t=NS), ds_, pc("mu", i),
                           sv[:, i, :, 1:1 + NS], ALU.mult, ALU.add).then_inc(*ve.up("dve_step"))
                ve.mark("us_ready")
                rT, kT_, vT = us[:, 0:4, :], us[:, 4:8, :], us[:, 8:12, :]
                for i in range(4):
                    ts(kk[:, i, :], kT_[:, i, :], pc("kk", i), None, ALU.mult).then_inc(*ve.up("dve_step"))
                ve.mark("kk_raw")
                for i in range(4):
                    cp(gT[:, i, :], take()[:, 0:T]).then_inc(*ve.up("bankV_free"))
                eng.wait_ge(*ve.after("kk_norm"))
                ts(sq[:, 4:8, :], sq[:, 4:8, :], 1e-12, None, ALU.max).then_inc(*ve.up("dve_step"))
                eng.wait_ge(*ve.own())
                nc.vector.reciprocal(sq[:, 4:8, :], sq[:, 4:8, :]).then_inc(*ve.up("dve_step"))
                eng.wait_ge(*ve.own())
                tt(kk[:, :, :], kk[:, :, :], sq[:, 4:8, :], ALU.mult).then_inc(*ve.up("dve_step"))
                for i in range(4):
                    ts(sq[:, i, :], aa[:, i, :], 1.0, pc("ka", i), ALU.subtract, ALU.mult).then_inc(*ve.up("dve_step"))
                eng.wait_ge(*ve.own())
                stt(kT_, sq[:, 0:4, :], 1.0, kT_, ALU.add, ALU.mult).then_inc(*ve.up("dve_step"))
                eng.wait_ge(*ve.own())
                tt(bon[:, :, :], rT, kT_, ALU.mult).then_inc(*ve.up("dve_step"))
                eng.wait_ge(*ve.own())
                for i in range(4):
                    ts(bon[:, i, :], bon[:, i, :], pc("rk", i), None, ALU.mult).then_inc(*ve.up("dve_step"))
                ve.mark("bonus_in")
                flat = lambda ap: ap.rearrange("p a t -> p (a t)")
                tt(sq[:, 0:4, :], dec[:, :, :], bc(C("keep"), 4), ALU.mult).then_inc(*ve.up("dve_step"))
                tt(sq[:, 4:8, :], dec[:, :, :], bc(C("begin"), 4), ALU.mult).then_inc(*ve.up("dve_step"))
                eng.wait_ge(*ve.own())
                nc.vector.tensor_tensor_scan(flat(pcum[:, :, :]), flat(sq[:, 0:4, :]), flat(sq[:, 4:8, :]), 0.0,
                                                ALU.mult, ALU.add).then_inc(*ve.up("dve_step"))
                eng.wait_ge(*ve.own())
                nc.vector.reciprocal(pinv[:, :, :], pcum[:, :, :]).then_inc(*ve.up("dve_step"))
                cp(pend[:, :, 0:8], pcum[:, :, CH - 1:NPR:CH]).then_inc(*ve.up("dve_step"))
                cp(pend[:, :, 8:16], pcum[:, :, NPR + NS - 1:T:NS]).then_inc(*ve.up("dve_step"))
                tt(AR[:, :, 1, :], rT, pcum[:, :, :], ALU.mult).then_inc(*ve.up("dve_step"))
                stt(AR[:, :, 0, 1:T], kk[:, :, 1:T], -1.0, pcum[:, :, 0:T - 1], ALU.mult, ALU.mult).then_inc(*ve.up("dve_step"))
                eng.wait_ge(*ve.own())
                ts(AR[:, :, 0, 0:NPR:CH], kk[:, :, 0:NPR:CH], -1.0, None, ALU.mult).then_inc(*ve.up("dve_step"))
                ts(AR[:, :, 0, NPR:T:NS], kk[:, :, NPR:T:NS], -1.0, None, ALU.mult).then_inc(*ve.up("dve_step"))
                tt(Bt[:, :, :], kk[:, :, :], aa[:, :, :], ALU.mult).then_inc(*ve.up("dve_step"))
                eng.wait_ge(*ve.own())
                tt(Kt[:, :, :], kT_, pinv[:, :, :], ALU.mult).then_inc(*ve.up("dve_step"))
                tt(Bt[:, :, :], Bt[:, :, :], pinv[:, :, :], ALU.mult).then_inc(*ve.up("dve_step"))
                eng.wait_ge(*ve.own())
                for i in range(4):
                    tt(bon[:, i, :], take()[:, 0:T], vT[:, i, :], ALU.mult).then_inc(*ve.up("bankV_free"))
                eng.wait_ge(*ve.own())
                barrier(ve, "dve")
                ve.mark("tilde_ready")
                nc.vector.memset(S[0][:, :, :], 0.0).then_inc(*ve.up("dve_step"))
                nc.vector.memset(S[1][:, :, :], 0.0).then_inc(*ve.up("dve_step"))
                eng.wait_ge(*ve.own())
                ident4 = bc(C("ident"), 4)
                s_now = 0
                for i in range(2):
                    if i == 0:
                        eng.wait_ge(*ve.after("tok_ready"))
                    else:
                        eng.wait_ge(*ve.after("tile_done"))
                    ve.mark("chunks_go")
                    for hd in range(NH):
                        tt(G[:, hd, :], take(), C("gm"), ALU.mult).then_inc(*ve.up("bankV_free"))
                    ve.mark("g_ready")
                    cp(MV[:, :], take()).then_inc(*ve.up("bankV_free"))
                    eng.wait_ge(*ve.own())
                    for hh in range(2):
                        ps = chunk4(take()[:, :])
                        tt(nm["y8"][:, :, :], ps, bc(C("y8"), 4), ALU.mult).then_inc(*ve.up("dve_step"))
                        tt(nm["yo16"][:, :, :], ps, bc(C("y16"), 4), ALU.mult).then_inc(*ve.up("dve_step"))
                        tt(nm["yo32"][:, :, :], ps, bc(C("y32"), 4), ALU.mult).then_inc(*ve.up("bankV_free"))
                        eng.wait_ge(*ve.own())
                        tt(nm["iy8"][:, :, :], nm["y8"][:, :, :], ident4, ALU.add).then_inc(*ve.up("dve_step"))
                        eng.wait_ge(*ve.own())
                        ve.mark("y_ready")
                        ps = chunk4(take()[:, :])
                        cp(nm["y2"][:, :, :], ps).then_inc(*ve.up("dve_step"))
                        tt(nm["iy2"][:, :, :], ps, ident4, ALU.add).then_inc(*ve.up("bankV_free"))
                        ve.mark("y2_ready")
                        tt(nm["h4"][:, :, :], chunk4(take()[:, :]), ident4, ALU.add).then_inc(*ve.up("bankV_free"))
                        ve.mark("h4_ready")
                        tt(t16, chunk4(take()[:, :]), nm["dd"][:, :, :], ALU.add).then_inc(*ve.up("bankV_free"))
                        ve.mark("t16_ready")
                        tt(Ti[:, hh::2, :], chunk4(take()[:, :]), t16, ALU.add).then_inc(*ve.up("bankV_free"))
                        eng.wait_ge(*ve.own())
                    ve.mark("t_ready")
                    for cc in range(4):
                        o = 32 * cc
                        ve.mark("s_ready")
                        tt(R1[o:o + 32, :], take()[o:o + 32, :], MV[o:o + 32, :], ALU.add).then_inc(*ve.up("bankV_free"))
                        ve.mark("r1_ready")
                        s_new = 1 - s_now
                        ps = chunk4(take())
                        tt(Ssum[0:HD, :, :], ps[0:HD, :, 0:HD], S[s_now][0:HD, :, 0:HD], ALU.add).then_inc(*ve.up("dve_step"))
                        tt(Ssum[HD:P, :, :], ps[HD:P, :, HD:P], S[s_now][HD:P, :, HD:P], ALU.add).then_inc(*ve.up("bankV_free"))
                        eng.wait_ge(*ve.own())
                        if i or cc:
                            eng.wait_ge(*ve.after("o_read"))
                        for rows in (slice(0, HD), slice(HD, P)):
                            tt(S[s_new][rows, :, rows], Ssum[rows, :, :],
                                  pend[rows, :, 4 * i + cc:4 * i + cc + 1].to_broadcast([HD, 4, HD]), ALU.mult).then_inc(*ve.up("dve_step"))
                        eng.wait_ge(*ve.own())
                        s_now = s_new
                ve.mark("prompt_state")
                n = NSM
                eng.wait_ge(*ve.after("tile_done"))
                ve.mark("chunks_go")
                eng.wait_ge(*ve.after("o_read"))
                for hh in range(2):
                    tt(G[0:n, hh::2, 0:4 * n], chunk4(take()[0:n, :]), bc(C("gs")[0:n, :], 4), ALU.mult).then_inc(*ve.up("bankV_free"))
                flat_s = lambda ap: ap[0:n, :, :].rearrange("p a b -> p (a b)")[:, 0:NH * n].rearrange(
                    "p (a b) -> p a b", b=n)
                for hh in range(2):
                    tt(flat_s(nm["y8"])[:, hh::2, :], take()[0:n, 0:4 * n].rearrange("p (a b) -> p a b", b=n),
                            bc(C("ys")[0:n, :], 4), ALU.mult).then_inc(*ve.up("bankV_free"))
                    eng.wait_ge(*ve.own())
                idn = bc(C("ident")[0:n, 0:n], NH)
                tt(flat_s(nm["iy8"]), flat_s(nm["y8"]), idn, ALU.add).then_inc(*ve.up("dve_step"))
                eng.wait_ge(*ve.own())
                ve.mark("g_ready")
                cp(MV[0:n, :], take()[0:n, :]).then_inc(*ve.up("bankV_free"))
                eng.wait_ge(*ve.own())
                eng.wait_ge(*ve.after("xs2_ready"))
                v8 = lambda ap: ap[0:n, :].rearrange("p (a b) -> p a b", b=n)
                tt(v8(hs), v8(xs2), idn, ALU.add).then_inc(*ve.up("dve_step"))
                eng.wait_ge(*ve.own())
                ve.mark("hs_ready")
                ve.mark("hs_made")
                tt(R1[0:n, :], take()[0:n, :], MV[0:n, :], ALU.add).then_inc(*ve.up("bankV_free"))
                ve.mark("r1_ready")
                for c4 in range(4):
                    sm = s_sum.rearrange("p (b i) -> p b i", b=NB)
                    tt(sm, take()[:, :].rearrange("p (b i) -> p b i", b=NB), S0[:, c4, :, :], ALU.add).then_inc(*ve.up("bankV_free"))
                    eng.wait_ge(*ve.own())
                    tt(S0[:, c4, :, :], sm, pend[:, c4, 8:16].rearrange("p (b m) -> p b m", m=1).to_broadcast([P, NB, HD]),
                          ALU.mult).then_inc(*ve.up("dve_step"))
                    eng.wait_ge(*ve.own())
                ve.mark("state_ready")
                eng.wait_ge(*ve.after("o_ready"))
                for i in range(4):
                    stt(oa[:, i, :], take()[:, 0:T], -1.0 / HD, oa[:, i, :], ALU.mult, ALU.add).then_inc(*ve.up("bankV_free"))
                ve.mark("o_centred")
                for i in range(4):
                    ts(sq[:, 4 + i, :], take()[:, 0:T], 1.0 / HD, GN_EPS, ALU.mult, ALU.add).then_inc(*ve.up("bankV_free"))
                ve.mark("o_var")
                eng.wait_ge(*ve.after("o_root"))
                nc.vector.reciprocal(sq[:, 4:8, :], sq[:, 4:8, :]).then_inc(*ve.up("dve_step"))
                eng.wait_ge(*ve.own())
                tt(oa[:, :, :], oa[:, :, :], sq[:, 4:8, :], ALU.mult).then_inc(*ve.up("dve_step"))
                eng.wait_ge(*ve.own())
                for i in range(4):
                    ts(oa[:, i, :], oa[:, i, :], pc("lnw", i), pc("lnb", i), ALU.mult, ALU.add).then_inc(*ve.up("dve_step"))
                eng.wait_ge(*ve.own())
                tt(oa[:, :, :], oa[:, :, :], bon[:, :, :], ALU.add).then_inc(*ve.up("dve_step"))
                eng.wait_ge(*ve.own())
                tt(oa[:, :, :], oa[:, :, :], gT[:, :, :], ALU.mult).then_inc(*ve.up("dve_step"))
                eng.wait_ge(*ve.own())
                barrier(ve, "dve")
                ve.mark("branches_ready")
                for cp_ in range(4):
                    for br in range(3):
                        for j in range(2):
                            eng.wait_ge(*ve.after("gate_ready"))
                            ps = take()
                            to = sq[:, 2 * cp_ + j, :]
                            if br == 0:
                                tt(to, ps[:, 0:T], gate[:, j, :], ALU.mult).then_inc(*ve.up("bankV_free"))
                                eng.wait_ge(*ve.own())
                            else:
                                tt(gate[:, j, :], ps[:, 0:T], gate[:, j, :], ALU.mult).then_inc(*ve.up("bankV_free"))
                                eng.wait_ge(*ve.own())
                                tt(to, to, gate[:, j, :], ALU.add).then_inc(*ve.up("dve_step"))
                                eng.wait_ge(*ve.own())
                            ve.mark("gate_free")
                ve.mark("merged")
                for j in range(DC):
                    tt(x[:, j, :], take()[:, 0:T], x[:, j, :], ALU.add).then_inc(*ve.up("bankV_free"))
                ve.mark("x_ready")
                ffn("ffn2")
                norm("ple")
                for j in range(DC):
                    eng.wait_ge(*ve.after("gate_ready"))
                    tt(gate[:, j % 2, :], take()[:, 0:T], gate[:, j % 2, :], ALU.mult).then_inc(*ve.up("bankV_free"))
                    eng.wait_ge(*ve.own())
                    tt(x[:, j, :], x[:, j, :], gate[:, j % 2, :], ALU.add).then_inc(*ve.up("dve_step"))
                    eng.wait_ge(*ve.own())
                    ve.mark("gate_free")
                ve.mark("x_final")
                ve.mark("x_ready")
            layers(eng, ve, body)


NSLAB = 34 + 20 + 20 + 4 + 34 + 8


def pack(i):
    f = lambda a: np.asarray(a, np.float32) if np.asarray(a).dtype == np.float32 else np.asarray(a)
    i = {n: f(a) for n, a in i.items()}
    tokens = lambda a, b: np.concatenate([a.reshape(NPR, -1), b.reshape(NSM, -1)], 0)
    fm = lambda a: np.ascontiguousarray(a.T.reshape(-1, P, a.shape[0]).transpose(1, 0, 2))
    cols = lambda a: a.reshape(-1, P).T
    out = {"const": CONST, "x": fm(tokens(i["x_prompt"], i["x_sample"])),
           "pages": np.ascontiguousarray(i["page_table"].reshape(1, -1))}
    w = np.zeros((DEPTH, NSLAB, P, SLAB), np.float32)
    prm = np.zeros((DEPTH, P, NPARAM), np.float32)
    p = np.zeros((DEPTH, P, 2 * T), np.float32)
    lora = np.zeros((DEPTH, P, 2 * 512), np.float32)
    for L in range(DEPTH):
        n = 0

        def slab(*mats):
            nonlocal n
            at = 0
            for m in mats:
                k, c = m.shape
                m = m.reshape(k // P, P, c).transpose(1, 0, 2).reshape(P, -1)
                w[L, n, :, at:at + m.shape[1]] = m
                at += m.shape[1]
            n += 1

        def ffn(name):
            for j in range(FC // 2):
                slab(i[name + "_wg"][L][:, 256 * j:256 * (j + 1)])
                slab(i[name + "_wu"][L][:, 256 * j:256 * (j + 1)])
            for j in range(4):
                for k0, k1 in ((0, 8), (8, 16), (16, 22)):
                    slab(i[name + "_wd"][L][P * k0:P * k1, 256 * j:256 * (j + 1)])

        ffn("ffn1")
        win = i["w_in"][L]
        a0 = 1792 + 1536
        for j in range(6):
            slab(win[:, a0 + 256 * j:a0 + 256 * (j + 1)])
        kiwi = np.zeros((D, 256), np.float32)
        kiwi[:, 0:72] = win[:, a0 + 1536:a0 + 1608]
        slab(kiwi)
        for j in range(6):
            slab(win[:, 1792 + 256 * j:1792 + 256 * (j + 1)])
        for j in range(7):
            slab(win[:, 256 * j:256 * (j + 1)])
        g0 = a0 + 1608
        for j in range(4):
            cs = slice(256 * j, 256 * (j + 1))
            for br in range(3):
                slab(win[:, g0 + 1024 * br + 256 * j:g0 + 1024 * br + 256 * (j + 1)])
                if br == 0:
                    slab(i["w_pa"][L][:, cs], i["w_pb"][L][:, cs])
                if br == 2:
                    slab(i["w_pc"][L][:, cs])
        for j in range(4):
            slab(i["w_out"][L][:, 256 * j:256 * (j + 1)])
        ffn("ffn2")
        for j in range(4):
            slab(i["ple_gate"][L][:, 256 * j:256 * (j + 1)])
            slab(i["ple_proj"][L][:, 256 * j:256 * (j + 1)])
        assert n == NSLAB
        put = lambda name, a: prm[L].__setitem__((slice(None), slice(PCOL[name], PCOL[name] + a.shape[1])), a)
        for name, src in (("ffn1", "ffn1_norm"), ("mix", "mix_norm"), ("ffn2", "ffn2_norm"), ("ple", "ple_norm"),
                          ("mu", "rwkv_mu"), ("w0", "rwkv_w0"), ("a0", "rwkv_a0"), ("kk", "rwkv_kk"), ("ka", "rwkv_ka"),
                          ("rk", "rwkv_rk"), ("lnw", "rwkv_lnx_w"), ("lnb", "rwkv_lnx_b")):
            put(name, cols(i[src][L].reshape(-1)))
        put("cw", cols(i["conv_w"][L].reshape(-1)))
        for name, src in (("qn", "q_norm"), ("kn", "k_norm"), ("in", "idx_k_norm")):
            put(name, np.concatenate([i[src][L], i[src][L]])[:, None])
        p[L] = fm(tokens(i["p_prompt"][L], i["p_sample"][L])).reshape(P, -1)
        lora[L, 0:HD, 0:512] = i["rwkv_w2"][L]
        lora[L, HD:P, 0:512] = i["rwkv_a2"][L]
        lora[L, :, 512:] = i["rwkv_g2"][L]
    out.update(w=w, prm=prm, p=p, lora=lora)
    s = i["state_shift"].reshape(DEPTH, NB, UC, P).transpose(0, 3, 2, 1)
    out["sft"] = np.ascontiguousarray(s.reshape(DEPTH, P, -1))
    s = i["state_conv"].reshape(DEPTH, NB, 2, 4, P).transpose(0, 4, 3, 1, 2)
    out["scv"] = np.ascontiguousarray(s.reshape(DEPTH, P, -1))
    s = i["state_wkv"].reshape(DEPTH, NB, 4, 2, HD, HD).transpose(0, 3, 5, 2, 1, 4)
    out["s0"] = np.ascontiguousarray(s.reshape(DEPTH, P, -1))
    s = i["cache_k"].reshape(DEPTH * NPHYS, PAGE, 2, 2, HD).transpose(0, 3, 4, 2, 1)
    out["k"] = np.ascontiguousarray(s.reshape(DEPTH * NPHYS, P, 256))
    out["v"] = np.ascontiguousarray(i["cache_v"].reshape(DEPTH * NPHYS, PAGE, 256))
    out["ki"] = np.ascontiguousarray(i["cache_kidx"].reshape(DEPTH * NPHYS, PAGE, HD).transpose(0, 2, 1))
    return out


OUTS = {"y_out": (P, DC, T), "k_out": (DEPTH, P, 2 * T), "v_out": (DEPTH, P, 2 * T), "ki_out": (DEPTH, HD, T),
        "s_out": (DEPTH, P, 4 * (NB + 1) * HD), "shift_out": (DEPTH, P, UC * (NB + 1)),
        "conv_out": (DEPTH, P, 4 * (NB + 1) * 2)}


def unpack(r):
    tok = lambda a: a.transpose(2, 1, 0).reshape(a.shape[2], -1)
    y = tok(r["y_out"])
    kv = {}
    for name in ("k_out", "v_out"):
        a = np.stack([tok(r[name][L].reshape(P, 2, T)) for L in range(DEPTH)])
        kv[name] = (a[:, :NPR].reshape(DEPTH, 1, NPR, 4, HD), a[:, NPR:].reshape(DEPTH, NB, NS, 4, HD))
    ki = r["ki_out"].transpose(0, 2, 1)
    s = r["s_out"].reshape(DEPTH, 2, HD, 4, NB + 1, HD).transpose(0, 4, 3, 1, 5, 2).reshape(DEPTH, NB + 1, NH, HD, HD)
    sh = r["shift_out"].reshape(DEPTH, P, UC, NB + 1).transpose(0, 3, 2, 1).reshape(DEPTH, NB + 1, UC * P)
    cv = r["conv_out"].reshape(DEPTH, P, 4, NB + 1, 2).transpose(0, 3, 4, 2, 1).reshape(DEPTH, NB + 1, 2, 512)
    got = (y[:NPR].reshape(1, NPR, D), y[NPR:].reshape(NB, NS, D), kv["k_out"][0], kv["v_out"][0],
           ki[:, :NPR].reshape(DEPTH, 1, NPR, HD), s[:, NB:], sh[:, NB:], cv[:, NB:],
           kv["k_out"][1], kv["v_out"][1], ki[:, NPR:].reshape(DEPTH, NB, NS, HD), s[:, :NB], sh[:, :NB], cv[:, :NB])
    return tuple(np.ascontiguousarray(a) for a in got)


def program(make, arrays):
    marks = {}
    for _ in range(2):
        nc, found, io = make(), {}, {}
        for name, a in arrays.items():
            io[name] = nc.dram_tensor(f"in_{name}", a.shape, I32 if name == "pages" else F32, kind="ExternalInput").ap()
        for name, shape in OUTS.items():
            io[name] = nc.dram_tensor(f"{name}", shape, F32, kind="ExternalOutput").ap()
        build(nc, io, marks, found)
        marks = found
    return nc


def kernel(**inputs):
    import concourse.bacc as bacc
    from concourse.bass_utils import run_bass_kernel_spmd as run

    arrays = pack(inputs)
    nc = program(lambda: bacc.Bacc("TRN2", target_bir_lowering=False, num_devices=1), arrays)
    r = run(nc, [{f"in_{n}": a for n, a in arrays.items()}], core_ids=[0]).results[0]
    return unpack({n: r[n] for n in OUTS})
```

```python
from contextlib import ExitStack

import numpy as np
import concourse.bass as bass
from concourse import mybir

F32 = mybir.dt.float32
F32R = mybir.dt.float32r
I32 = mybir.dt.int32
ALU = mybir.AluOpType
ACT = mybir.ActivationFunctionType
AX = mybir.AxisListType

P = 128
D = 1024
DC = D // P
NPR = 256
NB, NS = 8, 4
NSM = NB * NS
T = NPR + NSM
DEPTH = 2
FC = 2816 // P
HD = 64
NH = 8
NPAGE = 16
PAGE = 128
NPHYS = 160
PAST = NPAGE * PAGE
KEYS = PAST + NSM
TOPK_P, TOPK_S = 64, 256
CH = 32
SLOTS, SLAB = 5, 2048
ROUNDED = 3
UC = 14
UX = 1 + NPR + NB * (NS + 1)
ZX = 2 + NPR + NB * (NS + 2)
NEG, TAKEN = -1e30, -3e38
EPS, GN_EPS = 1e-6, 64e-5

PCOL = {}
_n = 0
for _name, _w in (("ffn1", 8), ("mix", 8), ("ffn2", 8), ("ple", 8), ("mu", UC), ("w0", 4), ("a0", 4), ("kk", 4),
                  ("ka", 4), ("rk", 4), ("lnw", 4), ("lnb", 4), ("cw", 12), ("qn", 1), ("kn", 1), ("in", 1)):
    PCOL[_name] = _n
    _n += _w
NPARAM = _n


def constants():
    s, t = np.arange(P)[:, None], np.arange(P)[None, :]
    same = lambda n: s // n == t // n
    cols = {"ident": s == t, "ones": np.ones((P, P)), "blk": same(HD)}
    rot = np.zeros((P, P))
    for base in (0, HD):
        for i in range(8):
            rot[base + i + 8, base + i] = -1.0
            rot[base + i, base + i + 8] = 1.0
    cols["rot"] = rot
    pos = np.concatenate([np.arange(NPR), np.tile(PAST + np.arange(NS), NB)]).astype(np.float32)
    inv = np.float32(500000.0) ** (-np.arange(8, dtype=np.float32) / np.float32(8))
    ang = (pos[:, None] * inv[None, :].astype(np.float32)).astype(np.float32)
    cos, sin = np.ones((P, T)), np.zeros((P, T))
    for base in (0, HD):
        for i in range(16):
            cos[base + i] = np.cos(ang[:, i % 8])
            sin[base + i] = np.sin(ang[:, i % 8])
    cols["cos"], cols["sin"] = cos, sin
    up, low = s < t, s > t
    cols["gm"] = np.concatenate([up & same(8), (s <= t) & same(CH), up & same(CH), (s <= t) & same(CH)], 1)
    cols["y8"] = low & same(8)
    cols["y16"] = low & same(16) & ~same(8)
    cols["y32"] = low & same(32) & ~same(16)
    s4, t4 = np.arange(P)[:, None], np.arange(NSM)[None, :]
    b4 = s4 // 4 == t4 // 4
    cols["gs"] = np.concatenate([(s4 < t4) & b4, (s4 <= t4) & b4, (s4 < t4) & b4, (s4 <= t4) & b4], 1)
    cols["ys"] = (s4 > t4) & b4
    q, k = np.arange(P)[:, None], np.arange(NPR)[None, :]
    cols["causal"] = np.concatenate([np.where(k <= q + P * i, 0.0, NEG) for i in range(2)], 1)
    start = np.ones((P, T))
    start[:, 0:NPR:CH] = 0
    start[:, NPR::NS] = 0
    cols["keep"], cols["begin"] = start, 1 - start
    row = np.arange(P)[:, None]
    tok = np.arange(NSM)[None, :]
    for g in range(2):
        b, tt = 4 * g + row // 32, row % 4
        cols[f"wsel{g}"] = ((tok // 4 == b) & (tok % 4 == tt)) * np.float32(NH ** -0.5)
    col = np.arange(P)[None, :]
    cols["e8"] = (row == (col // 4) % 8) & (row < 8)
    for g in range(2):
        cols[f"exp{g}"] = (row < 32) & (row // 4 == 4 * g + col // 32) & (row % 4 == col % 4)
    cols["cs"] = np.where((row // 4 == tok // 4) & (tok % 4 <= row % 4), 0.0, NEG)
    cols["bsel"] = row // 4 == np.arange(NB)[None, :]
    where, parts, n = {}, [], 0
    for name, a in cols.items():
        where[name] = (n, n + a.shape[1])
        n += a.shape[1]
        parts.append(np.asarray(a, np.float32))
    return where, np.ascontiguousarray(np.concatenate(parts, 1))


CW, CONST = constants()
NCONST = CONST.shape[1]


class Lane:

    def __init__(self, eng, sems, marks, found):
        self.eng, self.sems, self.marks, self.found = eng, sems, marks, found
        self.sent, self.met, self.last, self.passed = {}, {}, None, {}

    def up(self, name, by=1):
        self.sent[name] = self.sent.get(name, 0) + by
        if by == 1:
            self.last = (name, self.sent[name])
        return self.sems(name), by

    def next(self, name, n=1):
        self.met[name] = self.met.get(name, 0) + n
        return self.sems(name), self.met[name]

    def own(self):
        name, n = self.last
        return self.sems(name), n

    def mark(self, name):
        self.found.setdefault(name, []).append(self.last)

    def after(self, name, n=1):
        at = self.passed[name] = self.passed.get(name, 0) + n
        sem, value = self.marks[name][at - 1] if self.marks else ("plan", 1)
        return self.sems(sem), value


def build(nc, io, marks, found):
    ctx = ExitStack()
    with ctx:
        named = {}

        def sems(name):
            if name not in named:
                named[name] = ctx.enter_context(nc.semaphore(name))
            return named[name]

        laid_out, float32_names = [], ExitStack()

        def sb(name, *shape, dt=F32):
            laid_out.append((name, shape, dt))
            return float32_names.enter_context(nc.sbuf_tensor(name, list(shape), dt))

        bank = [ctx.enter_context(nc.psum_tensor(f"bank{i}", [P, 512], F32))[:, :] for i in range(8)]
        ringA, ringV = bank[0:4], bank[4:8]

        cst = sb("cst", P, NCONST)
        C = lambda name: cst[:, CW[name][0]:CW[name][1]]
        ring = sb("ring", P, SLOTS, SLAB)
        x = sb("x", P, DC, T)
        h = sb("h", P, DC, T)
        tmp = sb("tmp", P, 2304)
        sq = tmp[:, :].rearrange("p (c t) -> p c t", t=T)
        gate = sb("gate", P, 2, T)
        oa, ob, oc = sb("oa", P, 4, T), sb("ob", P, 4, T), sb("oc", P, 4, T)
        prm = sb("prm", P, NPARAM)
        rstd = sb("rstd", P, T)
        ptk = sb("ptk", P, 2, T)
        pages = sb("pages", 1, NB * NPAGE, dt=I32)
        lora = sb("lora", P, 2, 512)
        sft = sb("sft", P, UC, NB)
        scv = sb("scv", P, 4, NB, 2)
        sho = sb("sho", P, UC, NB + 1)
        cvo = sb("cvo", P, 4, NB + 1, 2)
        m8 = sb("m8", P, 8)
        stat = sb("stat", P, 64)
        witok = sb("witok", P, 2, NH)
        wi = sb("wi", NH, T)
        pend = sb("pend", P, 4, 16)
        LEFT = (nc.sbuf_bytes_remaining - 64) // 4
        arena = sb("arena", P, LEFT)
        float32_names.close()
        rounded_name = {name: ctx.enter_context(nc.sbuf_tensor(name + "_r", list(shape), F32R if dt == F32 else dt))
                        for name, shape, dt in laid_out}

        def as_r(ap):
            return bass.AP(rounded_name[ap.tensor.name], ap.offset, ap.ap)


        class Carve:

            def __init__(self, at=0):
                self.at = at

            def __call__(self, *shape):
                n = int(np.prod(shape))
                ap = arena[:, self.at:self.at + n]
                self.at += n
                assert self.at <= LEFT, (self.at, LEFT)
                if len(shape) == 2:
                    ap = ap.rearrange("p (a b) -> p a b", b=shape[1])
                elif len(shape) == 3:
                    ap = ap.rearrange("p (a b c) -> p a b c", b=shape[1], c=shape[2])
                return ap

        d = Carve()
        hid, hid_r = d(FC, T), d(FC, T)
        h_r, slab_r = d(DC, T), d(ROUNDED, SLAB)
        m = Carve()
        oa_r, ob_r, oc_r, sq_r = m(4, T), m(4, T), m(4, T), m(DC, T)
        ptk_r = oa[:, 0:2, :]
        c = Carve()
        uext = c(UC, UX)
        bgate, cgate, zx = c(4, T), c(4, T), c(4, ZX)
        q, k, v, qi = c(4, T), c(2, T), c(2, T), c(4, T)
        kid, kd, vtok = c(T), c(4, T), c(3, 256)
        qi0, qz, wsel = c(NB, 32), c(2, NB, 32), c(2, NSM)
        seenP = c(2, NPR)
        sidx = c(KEYS)
        sc, pt = c(KEYS), c(17, P)
        scg = (sc, tmp[:, 0:KEYS])
        pt1_at = UC * UX + 2 * 4 * T + 4 * ZX + 4 * T + 2 * T + 2 * T + 4 * T + T + 4 * T + 3 * 256 + NB * 32 + 2 * NB * 32 + 2 * NSM
        ptg = (pt, arena[:, pt1_at:pt1_at + 17 * P].rearrange("p (a b) -> p a b", b=P))
        pr = sc[:, 0:2048].rearrange("p (a b) -> p a b", b=NPR)
        prT = pt[:, 0:16, :]
        ov = kd[:, :, :].rearrange("p a t -> p (a t)")[:, 0:512].rearrange("p (g b r) -> p g b r", g=2, b=NB)
        halves = oa[:, :, :].rearrange("p a t -> p (a t)")[:, 0:KEYS // 2]
        flags_at = UC * UX + 2 * 4 * T + 4 * ZX + 4 * T + 2 * T
        flags = arena[:, flags_at:flags_at + KEYS]
        best, best2 = seenP[:, 0, :], seenP[:, 1, :]
        falling_to_rising = lambda ap: bass.AP(ap.tensor, ap.offset + ap.shape[1] - 1, [ap.ap[0], [-1, ap.shape[1]]])
        orow = qi[:, :, :].rearrange("p a t -> p (a t)")[:, 0:512].rearrange("p (g c) -> p g c", g=2)
        kv_at = LEFT - 4096
        assert c.at <= kv_at and d.at <= kv_at
        kvring = Carve(kv_at)(4, 1024)
        kiring = arena[:, kv_at:kv_at + 2048].rearrange("p (a b) -> p a b", b=512)
        rl = arena[:, kv_at + 2048:kv_at + 3072].rearrange("p (a b) -> p a b", b=512)
        r = Carve(UC * UX)
        gT, bon = r(4, T), r(4, T)
        AR, Bt, Kt = r(4, 2, T), r(4, T), r(4, T)
        keep_at = r.at
        us = r(UC, T)
        kk, aa, dec, pinv, pcum = r(4, T), r(4, T), r(4, T), r(4, T), r(4, T)
        lt = dec[:, 0:1, :]
        g = Carve(0)
        G = g(NH, 512)
        w = Carve(keep_at)
        tok = w(3, 3, 512)
        Ti = w(NH, P)
        MV = gate[:, :, :].rearrange("p a t -> p (a t)")[:, 0:512]
        S0 = w(4, NB, HD)
        work_at = w.at
        nm = {n: w(4, P) for n in ("y8", "yo16", "yo32", "iy8", "x2", "y2", "iy2", "h4", "fh", "dd", "dt", "qq")}
        t16 = nm["x2"]
        blk = Carve(work_at)
        ublk, vblk = blk(NB, P), blk(NB, P)
        zT, xs2, hs, us_s, s_sum = blk(4, NSM), blk(256), blk(256), blk(512), blk(512)
        R1 = tmp[:, 0:512]
        U = tmp[:, 512:1024]
        S = [tmp[:, 1024 + 512 * i:1536 + 512 * i].rearrange("p (c i) -> p c i", i=P) for i in range(2)]
        Ssum = tmp[:, 2048:2304].rearrange("p (c i) -> p c i", i=HD)
        rot_t = tmp[:, 0:T]
        chunk4 = lambda ap, n=4: ap.rearrange("p (a b) -> p a b", a=n)

        def bc(ap, n):
            return ap.rearrange("p (a m) -> p a m", a=1).to_broadcast([ap.shape[0], n, ap.shape[1]])

        half = lambda hd: slice(HD * (hd % 2), HD * (hd % 2) + HD)
        PAIRS = ((0, 2), (1, 3), (4, 6), (5, 7))
        BY_HALF = (0, 2, 4, 6, 1, 3, 5, 7)

        block = ctx.enter_context(nc.Block())

        def layers(eng, lane, body):
            for layer in range(DEPTH):
                body(layer)

        BAR = ("act", "dve", "pool")

        def barrier(lane, me):
            lane.eng.wait_ge(*lane.own())
            lane.eng.nop().then_inc(*lane.up(f"{me}_step"))
            lane.mark(f"phase_{me}")
            for other in BAR:
                if other != me:
                    lane.eng.wait_ge(*lane.after(f"phase_{other}"))

        one = lambda ap: ap.rearrange("a p n -> (a p) n")

        def slab_in(g):
            return sems(f"slab_in{g % SLOTS}"), 16 * (g // SLOTS + 1)

        SPLIT = [NSLAB * L_ + n for L_ in range(DEPTH) for n in range(NSLAB) if n < 34 or n >= 54]

        LOADER = {"sp": mybir.EngineType.SP, "pool": mybir.EngineType.Pool}

        def page(who, b, p):
            return nc.values_load(pages[0:1, b * NPAGE + p:b * NPAGE + p + 1], [LOADER[who]], min_val=0, max_val=NPHYS - 1,
                                  skip_runtime_bounds_check_because="page ids index the pool of NPHYS pages")

        def index_blocks(eng, ln, who, mine, L, lo, hi):
            for n in range(lo, hi):
                if n >= 4:
                    eng.wait_ge(*ln.after("kiblock_free"))
                for p in mine:
                    at = page(who, n % NB, 4 * (n // NB) + p) + L * NPHYS
                    eng.dma_start(kiring[0:HD, n % 4, PAGE * p:PAGE * (p + 1)], one(io["ki"][bass.ds(at, 1)])).then_inc(*ln.up(f"{who}_kiblock_in{n % 4}", 16))

        def kv_blocks(eng, ln, who, mine, L, lo, hi):
            for n in range(lo, hi):
                name, grp, i = "kv"[n // 32], n // 16 % 2, n % 16
                kb, b4 = (i // 4, i % 4) if name == "k" else (i % 4, i // 4)
                if n >= 4:
                    eng.wait_ge(*ln.after("kvblock_free"))
                for p in mine:
                    at = page(who, 4 * grp + b4, 4 * kb + p) + L * NPHYS
                    if name == "k":
                        dst = kvring[:, n % 4, :].rearrange("p (g k) -> p g k", g=2)[:, :, PAGE * p:PAGE * (p + 1)]
                        src = io["k"][bass.ds(at, 1)].rearrange("a p (g k) -> (a p) g k", g=2)
                    else:
                        dst, src = kvring[:, n % 4, 256 * p:256 * (p + 1)], one(io["v"][bass.ds(at, 1)])
                    eng.dma_start(dst, src).then_inc(*ln.up(f"{who}_kvblock_in{n % 4}", 16))

        @block.sync
        def _(eng):
            sp = Lane(eng, sems, marks, found)
            for dst, src in ((x[:, :, :], io["x"]), (cst[:, 0:4 * P], io["const"][:, 0:4 * P])):
                eng.dma_start(dst, src).then_inc(*sp.up("inputs_in", 16))
            eng.dma_start(pages[:, :], io["pages"]).then_inc(*sp.up("pages_in", 16))

            def slabs(L, lo, hi):
                for n in range(lo, hi):
                    if L or n >= SLOTS:
                        eng.wait_ge(*sp.after("slab_used"))
                    eng.dma_start(ring[:, (NSLAB * L + n) % SLOTS, :], one(io["w"][bass.ds(L, 1), n])).then_inc(*sp.up(f"slab_in{(NSLAB * L + n) % SLOTS}", 16))

            def body(L):
                slabs(L, 0, 4)
                if L == 0:
                    eng.dma_start(cst[:, 4 * P:NCONST], io["const"][:, 4 * P:NCONST]).then_inc(*sp.up("tables_in", 16))
                slabs(L, 4, 10)
                if L == 0:
                    eng.wait_ge(*sp.next("pages_in", 16))
                eng.wait_ge(*sp.after("layer_ready"))
                index_blocks(eng, sp, "sp", (0, 1), L, 0, 4)
                slabs(L, 10, 51 + SLOTS)
                index_blocks(eng, sp, "sp", (0, 1), L, 4, 32)
                eng.wait_ge(*sp.after("rl_done"))
                kv_blocks(eng, sp, "sp", (0, 1), L, 0, 4)
                slabs(L, 51 + SLOTS, 54 + SLOTS)
                kv_blocks(eng, sp, "sp", (0, 1), L, 4, 64)
                slabs(L, 54 + SLOTS, NSLAB)
                eng.wait_ge(*sp.after("kiblock_free", 4))
                eng.wait_ge(*sp.after("kvblock_free", 4))
            layers(eng, sp, body)

        @block.gpsimd
        def _(eng):
            po = Lane(eng, sems, marks, found)
            eng.nop().then_inc(*po.up("pool_step"))
            eng.wait_ge(*po.next("pages_in", 16))

            def body(L):
                eng.wait_ge(*po.own())
                eng.wait_ge(*po.after("layer_ready"))
                for dst, src in ((prm[:, :], io["prm"]), (ptk[:, :, :].rearrange("p a t -> p (a t)"), io["p"]),
                                 (lora[:, :, :].rearrange("p a t -> p (a t)"), io["lora"]),
                                 (sft[:, :, :].rearrange("p a t -> p (a t)"), io["sft"]),
                                 (scv[:, :, :, :].rearrange("p a b t -> p (a b t)"), io["scv"])):
                    eng.dma_start(dst, one(src[bass.ds(L, 1)])).then_inc(*po.up("params_in", 16))
                index_blocks(eng, po, "pool", (2, 3), L, 0, 32)
                if L == 0:
                    eng.wait_ge(*po.next("tables_in", 16))
                eng.wait_ge(*po.after("kiblock_free", 4))
                eng.wait_ge(*po.after("rl_done"))
                kv_blocks(eng, po, "pool", (2, 3), L, 0, 64)
                eng.wait_ge(*po.after("kvblock_free", 4))
                barrier(po, "pool")
                barrier(po, "pool")
                eng.dma_start(S0[:, :, :, :].rearrange("p a b t -> p (a b t)"), one(io["s0"][bass.ds(L, 1)])).then_inc(*po.up("state_in", 16))
                for c4 in range(4):
                    for src, dst, ready in ((us_s, ublk, "u_sample"), (tok[:, 0, 2, :], vblk, None)):
                        if ready and c4 == 0:
                            eng.wait_ge(*po.after("u_sample"))
                        if c4 and dst is ublk:
                            eng.wait_ge(*po.after("blk_free"))
                        eng.tensor_tensor(
                            dst[0:NSM, :, :], bc(src[0:NSM, P * c4:P * (c4 + 1)], NB),
                            C("bsel")[0:NSM, :].rearrange("p (b m) -> p b m", m=1).to_broadcast([NSM, NB, P]),
                            ALU.mult).then_inc(*po.up("pool_step"))
                        po.mark("blk_ready")
                eng.wait_ge(*po.after("blk_free"))
                barrier(po, "pool")
            layers(eng, po, body)

        @block.tensor
        def _(eng):
            pe = Lane(eng, sems, marks, found)
            state = {"slab": 0, "split": 0, "A": 0, "V": 0, "last": None}
            eng.wait_ge(*pe.next("inputs_in", 32))

            def use(kind):
                eng.wait_ge(*pe.next("bankA_free" if kind == "A" else "bankV_free"))
                b = (ringA if kind == "A" else ringV)[state[kind] % 4]
                state[kind] += 1
                return b

            def mm(out, lhsT, rhs, start=True, stop=True):
                state["last"] = nc.tensor.matmul(out, lhsT, rhs, start=start, stop=stop, skip_group_check=True)

            def tr(out, in_):
                state["last"] = nc.tensor.transpose(out, in_, C("ident")[0:in_.shape[0], 0:in_.shape[0]])

            def last():
                ins, state["last"] = state["last"], None
                return ins

            def mark(name):
                if state["last"] is not None:
                    state["last"].then_inc(*pe.up("pe_step"))
                    state["last"] = None
                pe.mark(name)

            def slab():
                g = state["slab"]
                state["slab"] += 1
                eng.wait_ge(*slab_in(g))
                return ring[:, g % SLOTS, :]

            def slab3():
                g = state["slab"]
                state["slab"] += 1
                state["split"] += 1
                eng.wait_ge(*pe.after("slab_split"))
                return as_r(slab_r[:, (state["split"] - 1) % ROUNDED, :]), as_r(ring[:, g % SLOTS, :])

            def dense(s, nk, cols, j, src, kind):
                ps = use(kind)
                sv = s[:, 0:nk * cols].rearrange("p (k n) -> p k n", n=cols)
                for kk_ in range(nk):
                    mm(ps[:, 0:T], sv[:, kk_, P * j:P * (j + 1)], src[:, kk_, :], start=kk_ == 0, stop=kk_ == nk - 1)
                return ps

            def dense3(s, nk, cols, j, src, kind, k0=0, start=True, stop=True, out=None, at=0, ready=None):
                ps = use(kind) if out is None else out
                w_r, w_b = (p_[:, at:at + nk * cols].rearrange("p (k n) -> p k n", n=cols) for p_ in s)
                x_r, x_b = as_r(src[0][:, :, :]), as_r(src[1][:, :, :])
                for kk_ in range(nk):
                    if ready:
                        eng.wait_ge(*pe.after(ready))
                    c_ = slice(P * j, P * (j + 1))
                    mm(ps[:, 0:T], w_r[:, kk_, c_], x_r[:, k0 + kk_, :], start=start and kk_ == 0, stop=False)
                    mm(ps[:, 0:T], w_r[:, kk_, c_], x_b[:, k0 + kk_, :], start=False, stop=False)
                    mm(ps[:, 0:T], w_b[:, kk_, c_], x_r[:, k0 + kk_, :], start=False, stop=stop and kk_ == nk - 1)
                return ps

            def norm():
                ps = use("V")
                for i in range(DC):
                    eng.wait_ge(*pe.after("squares"))
                    mm(ps[:, 0:T], C("ones"), sq[:, i, :], start=i == 0, stop=i == DC - 1)
                last().then_inc(*pe.up("bankV_full"))

            def ffn():
                norm()
                for j in range(FC // 2):
                    for kind in "AV":
                        s = slab3()
                        for i in range(2):
                            dense3(s, DC, 256, i, (h_r, h), kind, ready="h_ready" if j == i == 0 and kind == "A" else None)
                            last().then_inc(*pe.up(f"bank{kind}_full"))
                        mark_free(1, True)
                for j in range(4):
                    o = [use("V"), use("V")]
                    for part, (k0, nk) in enumerate(((0, 8), (8, 8), (16, 6))):
                        s = slab3()
                        for i in range(2):
                            dense3(s, nk, 256, i, (hid_r, hid), "V", k0, part == 0, part == 2, out=o[i],
                                   ready="hidden" if j == i == 0 else None)
                            if part == 2:
                                last().then_inc(*pe.up("bankV_full"))
                        mark_free(1, True)

            def mark_free(n, split=False):
                for _ in range(n):
                    mark("slab_used")
                    if split:
                        mark("split_used")

            def body(L):
                ffn()
                norm()
                eng.wait_ge(*pe.after("h_whole"))
                if L == 0:
                    eng.wait_ge(*pe.next("tables_in", 16))

                def project(n):
                    for _ in range(n):
                        s = slab()
                        for i in range(2):
                            dense(s, DC, 256, i, h, "A")
                            last().then_inc(*pe.up("bankA_full"))
                        mark_free(1)

                project(6)
                s = slab()
                sv = s.rearrange("p (k n) -> p k n", n=256)
                for lo, hi in ((0, HD), (HD, HD + NH)):
                    ps = use("A")
                    for i in range(DC):
                        mm(ps[0:hi - lo, 0:T], sv[:, i, lo:hi], h[:, i, :], i == 0, i == DC - 1)
                    last().then_inc(*pe.up("bankA_full"))
                mark_free(1)
                for name, src, n, m in (("q", q, 4, P), ("k", k, 2, P), ("ki", None, 1, HD)):
                    project(2)
                    eng.wait_ge(*pe.after("head_squares"))
                    for i in range(n):
                        ps = use("V")
                        mm(ps[0:m, 0:T], C("blk")[0:m, 0:m], sq[0:m, i, :])
                        last().then_inc(*pe.up("bankV_full"))
                for name, src, n, m in (("q", q, 4, P), ("k", k, 2, P), ("ki", kid, 1, HD), ("qi", qi, 4, P)):
                    eng.wait_ge(*pe.after("to_rotate"))
                    for i in range(n):
                        ps = use("V")
                        mm(ps[0:m, 0:T], C("rot")[0:m, 0:m], src[0:m, :] if src is kid else src[:, i, :])
                        last().then_inc(*pe.up("bankV_full"))
                    project(1)
                for i in range(2):
                    ps = use("V")
                    tr(ps[:, 0:NH], wi[:, P * i:P * (i + 1)])
                    last().then_inc(*pe.up("bankV_full"))
                for i in range(3):
                    n = P if i < 2 else NSM
                    ps = use("A")
                    for j in range(2):
                        tr(ps[0:n, P * j:P * (j + 1)], v[:, j, P * i:P * i + n])
                    last().then_inc(*pe.up("bankA_full"))
                ps = use("V")
                mm(ps[:, 0:NSM], C("e8")[0:NH, :], wi[:, NPR:T])
                last().then_inc(*pe.up("bankV_full"))
                eng.wait_ge(*pe.after("rotated"))
                for i in range(2):
                    for pair in PAIRS:
                        ps = use("A")
                        for j, hd in enumerate(pair):
                            rows = half(hd)
                            mm(ps[:, NPR * j:NPR * (j + 1)], qi[rows, hd // 2, P * i:P * (i + 1)], kid[rows, 0:NPR])
                        last().then_inc(*pe.up("bankA_full"))
                eng.wait_ge(*pe.after("sample_queries"))

                def scores(i):
                    kb, grp = i // 2, i % 2
                    ps = use("A")
                    n = 512 if kb < 4 else NSM
                    for b4 in range(4):
                        b = 4 * grp + b4
                        if kb < 4:
                            slot = (NB * kb + b) % 4
                            eng.wait_ge(*pe.next(f"sp_kiblock_in{slot}", 32))
                            eng.wait_ge(*pe.next(f"pool_kiblock_in{slot}", 32))
                            rhs = kiring[0:HD, slot, :]
                        else:
                            rhs = kid[0:HD, NPR:T]
                        mm(ps[32 * b4:32 * b4 + 32, 0:n], qi0[0:HD, b, :], rhs)
                        if kb < 4 and b4 < 3:
                            mark("kiblock_free")
                    last().then_inc(*pe.up("bankA_full"))
                    if kb < 4:
                        mark("kiblock_free")

                out = None
                for i in range(11):
                    if i < 10:
                        scores(i)
                    if i >= 1:
                        kb, grp = (i - 1) // 2, (i - 1) % 2
                        n = 512 if kb < 4 else NSM
                        eng.wait_ge(*pe.after("rl_ready"))
                        if grp == 0:
                            out = use("V")
                        mm(out[0:NSM, 0:n], wsel[:, grp, :], rl[:, (i - 1) % 2, 0:n], grp == 0, grp == 1)
                        if grp == 0:
                            mark("rl_read")
                        else:
                            last().then_inc(*pe.up("bankV_full"))
                            mark("rl_read")
                mark("rl_done")
                project(2)
                for i in range(2):
                    eng.wait_ge(*pe.after("prompt_mask"))
                    for pair in PAIRS:
                        ps = use("V")
                        for j, hd in enumerate(pair):
                            rows = half(hd)
                            mm(ps[:, NPR * j:NPR * (j + 1)], q[rows, hd // 2, P * i:P * (i + 1)],
                               kd[rows, hd // 2, 0:NPR])
                        last().then_inc(*pe.up("bankV_full"))
                    for c4 in range(4):
                        eng.wait_ge(*pe.after("prompt_probs"))
                        ps = use("A")
                        for hh in range(2):
                            for kt in range(2):
                                j = 2 * hh + kt
                                tr(ps[:, P * j:P * (j + 1)], pr[:, 2 * c4 + hh, P * kt:P * (kt + 1)])
                        last().then_inc(*pe.up("bankA_full"))
                    for c4 in range(4):
                        eng.wait_ge(*pe.after("prompt_probsT"))
                        ps = use("V")
                        for hh in range(2):
                            for kt in range(2):
                                mm(ps[HD * hh:HD * hh + HD, 0:P], vtok[:, kt, HD * c4:HD * c4 + HD],
                                   prT[:, 4 * c4 + 2 * hh + kt, :], kt == 0, kt == 1)
                        last().then_inc(*pe.up("bankV_full"))
                project(1)
                nblk = 0

                def block_in():
                    slot = nblk % 4
                    eng.wait_ge(*pe.next(f"sp_kvblock_in{slot}", 32))
                    eng.wait_ge(*pe.next(f"pool_kvblock_in{slot}", 32))
                    return slot

                for grp in range(2):
                    for kb in range(5):
                        ps = use("A")
                        n = 512 if kb < 4 else NSM
                        for b4 in range(4):
                            if kb < 4:
                                kblk = kvring[:, block_in(), :].rearrange("p (g k) -> p g k", g=2)
                            for gp in range(2):
                                mm(ps[32 * b4:32 * b4 + 32, 0:n], qz[:, gp, 4 * grp + b4, :],
                                   kblk[:, gp, :] if kb < 4 else k[:, gp, NPR:T], gp == 0, gp == 1)
                            if kb < 4:
                                nblk += 1
                                if b4 < 3:
                                    mark("kvblock_free")
                        last().then_inc(*pe.up("bankA_full"))
                        if kb < 4:
                            mark("kvblock_free")
                eng.wait_ge(*pe.after("sample_mask"))
                for grp in range(2):
                    for kb in range(5):
                        ps = use("V")
                        n = 512 if kb < 4 else NSM
                        mm(ps[:, 0:n], C(f"exp{grp}")[0:NSM, :], sidx[0:NSM, 512 * kb:512 * kb + n])
                        last().then_inc(*pe.up("bankV_full"))
                mark("sidx_read")
                for grp in range(2):
                    eng.wait_ge(*pe.after("sample_exp"))
                    for j in range(0, 17, 4):
                        ps = use("A")
                        for i in range(j, min(j + 4, 17)):
                            n = P if i < 16 else NSM
                            tr(ps[0:n, P * (i - j):P * (i - j + 1)], scg[grp][:, P * i:P * i + n])
                        last().then_inc(*pe.up("bankA_full"))
                    eng.wait_ge(*pe.after("sample_probsT"))
                    ps = use("V")
                    for b4 in range(4):
                        rows, to = slice(32 * b4, 32 * b4 + 32), ps[32 * b4:32 * b4 + 32, 0:256]
                        for kb in range(4):
                            vblk_ = kvring[:, block_in(), :]
                            for p in range(4):
                                mm(to, ptg[grp][:, 4 * kb + p, rows], vblk_[:, 256 * p:256 * p + 256],
                                   kb == 0 and p == 0, False)
                            nblk += 1
                            mark("kvblock_free")
                        mm(to, ptg[grp][0:NSM, 16, rows], vtok[0:NSM, 2, :], False, True)
                    last().then_inc(*pe.up("bankV_full"))
                for grp in range(2):
                    eng.wait_ge(*pe.after("sample_rows"))
                    ps = use("V")
                    for gp in range(2):
                        tr(ps[:, P * gp:P * (gp + 1)], orow[:, grp, P * gp:P * (gp + 1)])
                    last().then_inc(*pe.up("bankV_full"))

                eng.wait_ge(*pe.after("lora_in"))
                for c4 in range(4):
                    cols = slice(P * c4, P * (c4 + 1))
                    ps = use("A")
                    mm(ps[:, 0:T], lora[0:HD, 0, cols], lt[0:HD, 0, :])
                    last().then_inc(*pe.up("bankA_full"))
                for c4 in range(4):
                    cols = slice(P * c4, P * (c4 + 1))
                    ps = use("A")
                    mm(ps[:, 0:T], lora[HD:P, 0, cols], us[HD:P, 12, :])
                    last().then_inc(*pe.up("bankA_full"))
                    ps = use("V")
                    mm(ps[:, 0:T], lora[:, 1, cols], us[:, 13, :])
                    last().then_inc(*pe.up("bankV_full"))
                eng.wait_ge(*pe.after("kk_squares"))
                for c4 in range(4):
                    ps = use("A")
                    mm(ps[:, 0:T], C("blk"), sq[:, c4, :])
                    last().then_inc(*pe.up("bankA_full"))
                eng.wait_ge(*pe.after("bonus_in"))
                for c4 in range(4):
                    ps = use("V")
                    mm(ps[:, 0:T], C("blk"), bon[:, c4, :])
                    last().then_inc(*pe.up("bankV_full"))
                eng.wait_ge(*pe.after("tilde_ready"))
                for j, src in enumerate((us[:, 8:12, :], Bt, Kt)):
                    for i in range(3):
                        n = P if i < 2 else NSM
                        ps = use("A")
                        for c4 in range(4):
                            tr(ps[0:n, P * c4:P * (c4 + 1)], src[:, c4, P * i:P * i + n])
                        last().then_inc(*pe.up("bankA_full"))

                def within(i, n):
                    for e, hd in enumerate(range(NH) if n == P else BY_HALF):
                        rows, c4 = half(hd), hd // 2
                        if n == P or e % 4 == 0:
                            ps = use("V")
                        at = 0 if n == P else 4 * n * (e % 4)
                        for j, src in enumerate((Bt, Kt)):
                            mm(ps[0:n, at + 2 * n * j:at + 2 * n * (j + 1)].rearrange("p (a t) -> p a t", a=2),
                               src[rows, c4, P * i:P * i + n], AR[rows, c4, :, P * i:P * i + n])
                        if n == P or e % 4 == 3:
                            last().then_inc(*pe.up("bankV_full"))

                def lower(i, n, hh):
                    ps = use("V")
                    for j, hd in enumerate(range(hh, NH, 2)):
                        rows, c4 = half(hd), hd // 2
                        mm(ps[0:n, n * j:n * (j + 1)], AR[rows, c4, 0, P * i:P * i + n], Bt[rows, c4, P * i:P * i + n])
                    last().then_inc(*pe.up("bankV_full"))

                def four(kind, lhs, rhs, need=None, transpose=None):
                    if need:
                        eng.wait_ge(*pe.after(need))
                    ps = use(kind)
                    for j in range(4):
                        if transpose is not None:
                            tr(ps[:, P * j:P * (j + 1)], transpose[:, j, :])
                        else:
                            mm(ps[:, P * j:P * (j + 1)], lhs(j), rhs(j))
                    last().then_inc(*pe.up(f"bank{kind}_full"))

                at = lambda name: (lambda j: nm[name][:, j, :])

                def values_in(i, n):
                    ps = use("V")
                    for hd in range(NH):
                        lhs = G[0:n, hd, 2 * n:3 * n]
                        mm(ps[0:n, HD * hd:HD * hd + HD], lhs, tok[0:n, 0, i, HD * hd:HD * hd + HD])
                    last().then_inc(*pe.up("bankV_full"))

                s_now = 0
                for i in range(2):
                    eng.wait_ge(*pe.after("chunks_go"))
                    eng.wait_ge(*pe.after("tile_done" if i else "tok_ready"))
                    within(i, P)
                    eng.wait_ge(*pe.after("g_ready"))
                    values_in(i, P)
                    for hh in range(2):
                        lower(i, P, hh)
                        x8 = lambda j, hh=hh: G[:, 2 * j + hh, 0:P]
                        four("A", at("y8"), x8, "y_ready")
                        four("V", x8, at("y8"))
                        eng.wait_ge(*pe.after("x2_ready"))
                        four("V", at("y2"), at("x2"), "y2_ready")
                        four("A", at("iy2"), at("h4"), "h4_ready")
                        four("A", at("iy8"), at("fh"), "fh_ready")
                        four("A", None, None, "dd_ready", nm["dd"])
                        four("A", at("yo16"), at("dd"))
                        four("V", at("dt"), at("qq"), "dtqq_ready")
                        four("A", None, None, "t16_ready", t16)
                        four("A", at("yo32"), lambda j: t16[:, j, :])
                        four("V", at("dt"), at("qq"), "dtqq_ready")
                    eng.wait_ge(*pe.after("t_ready"))
                    for cc in range(4):
                        o, t0 = 32 * cc, P * i + 32 * cc
                        eng.wait_ge(*pe.after("s_ready"))
                        ps = use("V")
                        for c4 in range(4):
                            mm(ps[o:o + 32, P * c4:P * (c4 + 1)], AR[:, c4, 0, t0:t0 + 32], S[s_now][:, c4, :])
                        last().then_inc(*pe.up("bankV_full"))
                        eng.wait_ge(*pe.after("r1_ready"))
                        ps = use("A")
                        for hd in range(NH):
                            mm(ps[o:o + 32, HD * hd:HD * hd + HD], Ti[o:o + 32, hd, o:o + 32],
                               R1[o:o + 32, HD * hd:HD * hd + HD])
                        last().then_inc(*pe.up("bankA_full"))
                        eng.wait_ge(*pe.after("u_ready"))
                        ps = use("V")
                        for c4 in range(4):
                            pc_ = slice(P * c4, P * (c4 + 1))
                            mm(ps[:, pc_], tok[o:o + 32, 1, i, pc_], U[o:o + 32, pc_], True, False)
                            mm(ps[:, pc_], tok[o:o + 32, 2, i, pc_], tok[o:o + 32, 0, i, pc_], False, True)
                        last().then_inc(*pe.up("bankV_full"))
                        ps = use("A")
                        for c4 in range(4):
                            mm(ps[:, 32 * c4:32 * c4 + 32], S[s_now][:, c4, :], AR[:, c4, 1, t0:t0 + 32], c4 == 0, False)
                        for hd in range(NH):
                            c4, hc = hd // 2, slice(HD * hd, HD * hd + HD)
                            to = ps[half(hd), 32 * c4:32 * c4 + 32]
                            mm(to, U[o:o + 32, hc], G[o:o + 32, hd, P + o:P + o + 32], False, False)
                            mm(to, tok[o:o + 32, 0, i, hc], G[o:o + 32, hd, 3 * P + o:3 * P + o + 32], False, True)
                        last().then_inc(*pe.up("bankA_full"))
                        s_now = 1 - s_now
                n, i = NSM, 2
                eng.wait_ge(*pe.after("chunks_go"))
                eng.wait_ge(*pe.after("tile_done"))
                eng.wait_ge(*pe.next("state_in", 16))
                within(i, n)
                lower(i, n, 0)
                lower(i, n, 1)
                eng.wait_ge(*pe.after("g_ready"))
                values_in(i, n)
                ps = use("A")
                for hd in range(NH):
                    mm(ps[0:n, n * hd:n * (hd + 1)], nm["y8"][0:n, :, :].rearrange("p a b -> p (a b)")[:, n * hd:n * (hd + 1)],
                       G[0:n, hd, 0:n])
                last().then_inc(*pe.up("bankA_full"))
                for hh in range(2):
                    ps = use("A")
                    rows = half(hh)
                    for c4 in range(4):
                        for b in range(NB):
                            mm(ps[rows, n * c4 + NS * b:n * c4 + NS * b + NS], S0[rows, c4, b, :],
                               AR[rows, c4, 0, NPR + NS * b:NPR + NS * b + NS])
                    last().then_inc(*pe.up("bankA_full"))
                eng.wait_ge(*pe.after("hs_ready"))
                ps = use("A")
                for hd in range(NH):
                    mm(ps[0:n, n * hd:n * (hd + 1)], nm["iy8"][0:n, :, :].rearrange("p a b -> p (a b)")[:, n * hd:n * (hd + 1)],
                       hs[0:n, n * hd:n * (hd + 1)])
                last().then_inc(*pe.up("bankA_full"))
                eng.wait_ge(*pe.after("zt_ready"))
                ps = use("V")
                for c4 in range(4):
                    mm(ps[0:n, P * c4:P * (c4 + 1)], zT[:, c4, :], C("ident"))
                last().then_inc(*pe.up("bankV_full"))
                eng.wait_ge(*pe.after("r1_ready"))
                eng.wait_ge(*pe.after("inverse_ready"))
                ps = use("A")
                for hd in range(NH):
                    hc = slice(HD * hd, HD * hd + HD)
                    mm(ps[0:n, hc], xs2[0:n, n * hd:n * (hd + 1)], R1[0:n, hc])
                last().then_inc(*pe.up("bankA_full"))
                eng.wait_ge(*pe.after("u_ready"))
                for hh in range(2):
                    ps = use("A")
                    rows = half(hh)
                    for c4 in range(4):
                        hd, hc = 2 * c4 + hh, slice(HD * (2 * c4 + hh), HD * (2 * c4 + hh) + HD)
                        to = ps[rows, n * c4:n * (c4 + 1)]
                        mm(to, us_s[0:n, hc], G[0:n, hd, n:2 * n], True, False)
                        mm(to, tok[0:n, 0, 2, hc], G[0:n, hd, 3 * n:4 * n], False, False)
                        for b in range(NB):
                            mm(ps[rows, n * c4 + NS * b:n * c4 + NS * b + NS], S0[rows, c4, b, :],
                               AR[rows, c4, 1, NPR + NS * b:NPR + NS * b + NS], False, b == NB - 1)
                    last().then_inc(*pe.up("bankA_full"))
                for c4 in range(4):
                    eng.wait_ge(*pe.after("blk_ready", 2))
                    ps = use("V")
                    for hh in range(2):
                        hc = slice(P * c4 + HD * hh, P * c4 + HD * hh + HD)
                        to = ps[HD * hh:HD * hh + HD, :].rearrange("p (b i) -> p b i", b=NB)
                        mm(to, tok[0:n, 1, 2, hc], ublk[0:n, :, HD * hh:HD * hh + HD], True, False)
                        mm(to, tok[0:n, 2, 2, hc], vblk[0:n, :, HD * hh:HD * hh + HD], False, True)
                    last().then_inc(*pe.up("bankV_full"))
                    mark("blk_free")
                for name in ("o_ready", "o_squares"):
                    eng.wait_ge(*pe.after(name))
                    for c4 in range(4):
                        ps = use("V")
                        mm(ps[:, 0:T], C("blk"), oa[:, c4, :] if name == "o_ready" else sq[:, c4, :])
                        last().then_inc(*pe.up("bankV_full"))
                eng.wait_ge(*pe.after("branches_ready"))
                for cp in range(4):
                    for br in range(3):
                        gs = slab3()
                        for j in range(2):
                            dense3(gs, DC, 256, j, (h_r, h), "A")
                            last().then_inc(*pe.up("bankA_full"))
                        if br != 1:
                            wslab = slab3()
                        for j in range(2):
                            dense3(wslab, 4, 256, j, ((oa_r, oa), (ob_r, ob), (oc_r, oc))[br], "V",
                                   at=1024 if br == 1 else 0)
                            last().then_inc(*pe.up("bankV_full"))
                        mark_free(1 if br == 0 else 2, True)
                eng.wait_ge(*pe.after("merged"))
                for _ in range(4):
                    s = slab3()
                    for j in range(2):
                        dense3(s, DC, 256, j, (sq_r, sq), "V")
                        last().then_inc(*pe.up("bankV_full"))
                    mark_free(1, True)
                ffn()
                norm()
                for cp in range(4):
                    for kind, src, nk in (("A", (h_r, h), DC), ("V", (ptk_r, ptk), 2)):
                        s = slab3()
                        for j in range(2):
                            dense3(s, nk, 256, j, src, kind, ready="h_ready" if cp == j == 0 and kind == "A" else None)
                            last().then_inc(*pe.up(f"bank{kind}_full"))
                        mark_free(1, True)
                assert state["slab"] == NSLAB * (L + 1), state
            layers(eng, pe, body)

        @block.scalar
        def _(eng):
            ac = Lane(eng, sems, marks, found)
            state = {"A": 0, "split": 0, "merging": True}
            a = nc.scalar.activation
            for _ in range(4):
                eng.nop().then_inc(*ac.up("bankA_free"))
            eng.wait_ge(*ac.next("inputs_in", 32))

            def take():
                eng.wait_ge(*ac.next("bankA_full"))
                b = ringA[state["A"] % 4]
                state["A"] += 1
                return b

            def split(n=1):
                for _ in range(n):
                    m_ = state["split"]
                    if m_ == len(SPLIT) or (SPLIT[m_] % NSLAB == 54 and not state["merging"]):
                        return
                    state["split"] += 1
                    if m_ >= ROUNDED:
                        eng.wait_ge(*ac.after("split_used"))
                    eng.wait_ge(*slab_in(SPLIT[m_]))
                    a(as_r(slab_r[:, m_ % ROUNDED, :]), ring[:, SPLIT[m_] % SLOTS, :], ACT.Copy).then_inc(*ac.up("act_step"))
                    ac.mark("slab_rounded")

            def norm(rounded=True):
                for i in range(DC):
                    eng.wait_ge(*ac.after("x_ready"))
                    a(sq[:, i, :], x[:, i, :], ACT.Square).then_inc(*ac.up("act_step"))
                    ac.mark("squares")
                eng.wait_ge(*ac.after("mean_square"))
                a(rstd[:, :], rstd[:, :], ACT.Sqrt).then_inc(*ac.up("act_step"))
                ac.mark("root")
                if rounded:
                    for i in range(DC):
                        eng.wait_ge(*ac.after("h_chunk"))
                        a(as_r(h_r[:, i, :]), h[:, i, :], ACT.Copy).then_inc(*ac.up("act_step"))
                        ac.mark("h_rounded")

            def ffn():
                norm()
                for j in range(FC):
                    ps = take()
                    a(hid[:, j, :], ps[:, 0:T], ACT.Silu).then_inc(*ac.up("bankA_free"))
                    ac.mark("silu")
                    if j % 2:
                        split(2)
                split(12)

            def rows2(ap, b, n):
                return ap.rearrange("p (b s) -> p b s", b=b)[:, :, 0:n]

            def body(L):
                one = lambda ap: ap[bass.ds(L, 1)].rearrange("a p n -> (a p) n")
                state["merging"] = False
                if L == 0:
                    split(ROUNDED)
                ffn()
                norm(False)
                for dst, n in ((q, 4), (k, 2), (v, 2), (qi, 4)):
                    for i in range(n):
                        a(dst[:, i, :], take()[:, 0:T], ACT.Copy).then_inc(*ac.up("bankA_free"))
                a(kid[0:HD, :], take()[0:HD, 0:T], ACT.Copy).then_inc(*ac.up("bankA_free"))
                a(wi[:, :], take()[0:NH, 0:T], ACT.Copy).then_inc(*ac.up("bankA_free"))
                eng.wait_ge(*ac.own())

                def conv_inputs(j):
                    for i in range(4):
                        if j < 2:
                            a((bgate, cgate)[j][:, i, :], take()[:, 0:T], ACT.Copy).then_inc(*ac.up("bankA_free"))
                        else:
                            ps = take()
                            a(zx[:, i, 2:2 + NPR], ps[:, 0:NPR], ACT.Copy).then_inc(*ac.up("act_step"))
                            a(zx[:, i, 2 + NPR:ZX].rearrange("p (b s) -> p b s", b=NB)[:, :, 2:2 + NS],
                                   ps[:, NPR:T].rearrange("p (b t) -> p b t", t=NS), ACT.Copy).then_inc(*ac.up("bankA_free"))

                def rwkv_inputs(lo, hi):
                    for i in range(lo, hi):
                        ps = take()
                        a(uext[:, i, 1:1 + NPR], ps[:, 0:NPR], ACT.Copy).then_inc(*ac.up("act_step"))
                        a(uext[:, i, 1 + NPR:UX].rearrange("p (b s) -> p b s", b=NB)[:, :, 1:1 + NS],
                               ps[:, NPR:T].rearrange("p (b t) -> p b t", t=NS), ACT.Copy).then_inc(*ac.up("bankA_free"))

                for j, (src, n, m) in enumerate(((q, 4, P), (k, 2, P), (kid, 1, HD))):
                    if src is not q:
                        eng.wait_ge(*ac.after("sums_taken"))
                    if src is kid:
                        a(sq[0:m, 0, :], kid[0:m, :], ACT.Square).then_inc(*ac.up("act_step"))
                        ac.mark("head_squares")
                    else:
                        a(sq[:, 0:n, :], src[:, :, :], ACT.Square).then_inc(*ac.up("act_step"))
                        ac.mark("head_squares")
                    conv_inputs(j)
                    eng.wait_ge(*ac.after("head_means"))
                    a(sq[0:m, 4:4 + n, :], sq[0:m, 4:4 + n, :], ACT.Sqrt).then_inc(*ac.up("act_step"))
                    ac.mark("head_roots")
                ac.mark("conv_in")
                rwkv_inputs(0, 8)
                for i in range(3):
                    n = P if i < 2 else NSM
                    a(vtok[0:n, i, :], take()[0:n, 0:256], ACT.Copy).then_inc(*ac.up("bankA_free"))
                eng.wait_ge(*ac.after("rope_done"))
                for dst in range(2):
                    to = slice(HD * dst, HD * dst + HD)
                    for gh in range(2):
                        a(kd[to, gh:4:2, :], k[HD * gh:HD * gh + HD, :, :], ACT.Copy).then_inc(*ac.up("act_step"))
                a(kid[HD:P, :], kid[0:HD, :], ACT.Copy).then_inc(*ac.up("act_step"))
                ac.mark("rotated")
                for b in range(NB):
                    tk = slice(NPR + NS * b, NPR + NS * b + NS)
                    for hh in range(2):
                        src = slice(HD * hh, HD * hh + HD)
                        a(qi0[0:HD, b, :].rearrange("p (h t) -> p h t", t=NS)[:, hh::2, :], qi[src, :, tk], ACT.Copy).then_inc(*ac.up("act_step"))
                eng.wait_ge(*ac.after("qz_clear"))
                for c4 in range(4):
                    to = slice(HD * (c4 % 2), HD * (c4 % 2) + HD)
                    for hh in range(2):
                        hd = 2 * c4 + hh
                        a(qz[to, c4 // 2, :, NS * hd:NS * hd + NS],
                               q[HD * hh:HD * hh + HD, c4, NPR:T].rearrange("p (b t) -> p b t", t=NS), ACT.Copy).then_inc(*ac.up("act_step"))
                ac.mark("sample_queries")
                for dst, src in (("k_out", k), ("v_out", v)):
                    eng.dma_start(one(io[dst]), src[:, :, :].rearrange("p a t -> p (a t)")).then_inc(*ac.up("kv_out", 16))
                eng.dma_start(one(io["ki_out"]), kid[0:HD, :]).then_inc(*ac.up("kv_out", 16))
                for i in range(8):
                    if i >= 2:
                        eng.wait_ge(*ac.after("rl_read_v"))
                    a(rl[:, i % 2, :], take(), ACT.Relu, scale=0.125).then_inc(*ac.up("bankA_free"))
                    ac.mark("rl_prompt")
                eng.wait_ge(*ac.after("rl_read_v", 2))
                for i in range(10):
                    if i >= 2:
                        eng.wait_ge(*ac.after("rl_read"))
                    n = 512 if i < 8 else NSM
                    a(rl[:, i % 2, 0:n], take()[:, 0:n], ACT.Relu, scale=0.125).then_inc(*ac.up("bankA_free"))
                    ac.mark("rl_ready")
                eng.wait_ge(*ac.after("rl_read", 2))
                rwkv_inputs(8, 12)
                for i in range(2):
                    for pos, hd in enumerate(sum(PAIRS, ())):
                        if pos % 2 == 0:
                            eng.wait_ge(*ac.after("prompt_max"))
                        a(pr[:, hd, :], pr[:, hd, :], ACT.Exp, bias=stat[:, 8 + hd:9 + hd], scale=0.125,
                               accum_out=stat[:, 16 + hd:17 + hd]).then_inc(*ac.up("act_step"))
                        ac.mark("prompt_exp")
                    for c4 in range(4):
                        a(prT[:, 4 * c4:4 * c4 + 4, :].rearrange("p a b -> p (a b)"), take(), ACT.Copy).then_inc(*ac.up("bankA_free"))
                        ac.mark("prompt_probsT")
                rwkv_inputs(12, UC)
                ac.mark("u_in")
                for grp in range(2):
                    if grp == 0:
                        eng.wait_ge(*ac.after("prompt_out"))
                    for kb in range(5):
                        n = 512 if kb < 4 else NSM
                        a(scg[grp][:, 512 * kb:512 * kb + n], take()[:, 0:n], ACT.Copy).then_inc(*ac.up("bankA_free"))
                    ac.mark("sample_scores")
                for grp in range(2):
                    eng.wait_ge(*ac.after("sample_max"))
                    a(scg[grp], scg[grp], ACT.Exp, bias=stat[:, 25 + 16 * grp:26 + 16 * grp], scale=0.125,
                           accum_out=stat[:, 26 + 16 * grp:27 + 16 * grp]).then_inc(*ac.up("act_step"))
                    ac.mark("sample_exp")
                for grp in range(2):
                    if grp:
                        eng.wait_ge(*ac.after("sidx_read"))
                    for j in range(0, 17, 4):
                        n, m = (P, 512) if j < 16 else (NSM, P)
                        a(ptg[grp][0:n, j:j + m // P, :].rearrange("p a b -> p (a b)"), take()[0:n, 0:m], ACT.Copy).then_inc(*ac.up("bankA_free"))
                    ac.mark("sample_probsT")
                eng.wait_ge(*ac.next("kv_out", 48))
                barrier(ac, "act")
                eng.wait_ge(*ac.after("us_ready"))
                a(lt[0:HD, 0, :], us[0:HD, 12, :], ACT.Tanh).then_inc(*ac.up("act_step"))
                a(us[:, 13, :], us[:, 13, :], ACT.Sigmoid).then_inc(*ac.up("act_step"))
                ac.mark("lora_in")
                for i in range(4):
                    ps = take()
                    a(pcum[:, i, :], ps[:, 0:T], ACT.Sigmoid, bias=prm[:, PCOL["w0"] + i:PCOL["w0"] + i + 1]).then_inc(*ac.up("bankA_free"))
                for i in range(4):
                    ps = take()
                    a(aa[:, i, :], ps[:, 0:T], ACT.Sigmoid, bias=prm[:, PCOL["a0"] + i:PCOL["a0"] + i + 1]).then_inc(*ac.up("bankA_free"))
                eng.wait_ge(*ac.own())
                a(dec[:, :, :], pcum[:, :, :], ACT.Exp, scale=-float(np.exp(-0.5))).then_inc(*ac.up("act_step"))
                eng.wait_ge(*ac.after("kk_raw"))
                a(sq[:, 0:4, :], kk[:, :, :], ACT.Square).then_inc(*ac.up("act_step"))
                ac.mark("kk_squares")
                eng.wait_ge(*ac.after("sho_ready"))
                eng.dma_start(one(io["shift_out"]), sho[:, :, :].rearrange("p a t -> p (a t)")).then_inc(*ac.up("small_out", 16))
                eng.dma_start(one(io["conv_out"]), cvo[:, :, :, :].rearrange("p a b t -> p (a b t)")).then_inc(*ac.up("small_out", 16))
                for i in range(4):
                    ps = take()
                    a(sq[:, 4 + i, :], ps[:, 0:T], ACT.Sqrt).then_inc(*ac.up("bankA_free"))
                ac.mark("kk_norm")
                barrier(ac, "act")
                for j in range(3):
                    for i in range(3):
                        n = P if i < 2 else NSM
                        a(tok[0:n, j, i, :], take()[0:n, :], ACT.Copy).then_inc(*ac.up("bankA_free"))
                ac.mark("tok_ready")
                for i in range(2):
                    for hb in (0, 4):
                        for names, ready in ((("x2",), "x2_ready"), (("fh",), "fh_ready"), (("dd",), "dd_ready"),
                                             (("dt", "qq"), "dtqq_ready"), (("dt", "qq"), "dtqq_ready")):
                            for name in names:
                                a(nm[name][:, :, :].rearrange("p a b -> p (a b)"), take(), ACT.Copy).then_inc(*ac.up("bankA_free"))
                            eng.wait_ge(*ac.own())
                            ac.mark(ready)
                    for cc in range(4):
                        o, t0 = 32 * cc, P * i + 32 * cc
                        a(U[o:o + 32, :], take()[o:o + 32, :], ACT.Copy).then_inc(*ac.up("bankA_free"))
                        ac.mark("u_ready")
                        a(oa[:, :, t0:t0 + 32], chunk4(take()[:, 0:P]), ACT.Copy).then_inc(*ac.up("bankA_free"))
                        ac.mark("o_read")
                    ac.mark("tile_done")
                a(xs2[0:NSM, :], take()[0:NSM, 0:256], ACT.Copy).then_inc(*ac.up("bankA_free"))
                for hh in range(2):
                    a(zT[half(hh), :, :].rearrange("p a b -> p (a b)"), take()[half(hh), 0:P], ACT.Copy).then_inc(*ac.up("bankA_free"))
                ac.mark("xs2_ready")
                ac.mark("zt_ready")
                eng.wait_ge(*ac.after("hs_made"))
                a(xs2[0:NSM, :], take()[0:NSM, 0:256], ACT.Copy).then_inc(*ac.up("bankA_free"))
                ac.mark("inverse_ready")
                a(us_s[0:NSM, :], take()[0:NSM, :], ACT.Copy).then_inc(*ac.up("bankA_free"))
                ac.mark("u_ready")
                ac.mark("u_sample")
                for hh in range(2):
                    a(oa[half(hh), :, NPR:T], chunk4(take()[half(hh), 0:P]), ACT.Copy).then_inc(*ac.up("bankA_free"))
                ac.mark("o_ready")
                eng.wait_ge(*ac.after("prompt_state"))
                for hh in range(2):
                    eng.dma_start(
                        one(io["s_out"]).rearrange("p (c b i) -> p c b i", c=4, b=NB + 1)[half(hh), :, NB, :],
                        S[0][half(hh), :, half(hh)]).then_inc(*ac.up("small_out", 16))
                eng.wait_ge(*ac.next("small_out", 64))
                eng.wait_ge(*ac.after("o_centred"))
                a(sq[:, 0:4, :], oa[:, :, :], ACT.Square).then_inc(*ac.up("act_step"))
                ac.mark("o_squares")
                eng.wait_ge(*ac.after("o_var"))
                a(sq[:, 4:8, :], sq[:, 4:8, :], ACT.Sqrt).then_inc(*ac.up("act_step"))
                ac.mark("o_root")
                eng.wait_ge(*ac.after("state_ready"))
                eng.dma_start(one(io["s_out"]).rearrange("p (c b i) -> p c b i", c=4, b=NB + 1)[:, :, 0:NB, :],
                                     S0[:, :, :, :]).then_inc(*ac.up("small_out", 16))
                eng.wait_ge(*ac.next("small_out", 16))
                barrier(ac, "act")
                for dst, src in ((h_r, h), (oa_r, oa), (ob_r, ob), (oc_r, oc)):
                    a(as_r(dst[:, :, :]), src[:, :, :], ACT.Copy).then_inc(*ac.up("act_step"))
                    ac.mark("branch_rounded")
                state["merging"] = True
                split(ROUNDED)
                for cp in range(4):
                    for br in range(3):
                        for j in range(2):
                            if cp or br:
                                eng.wait_ge(*ac.after("gate_free"))
                            a(gate[:, j, :], take()[:, 0:T], ACT.Sigmoid).then_inc(*ac.up("bankA_free"))
                            ac.mark("gate_ready")
                        split(1 if br == 0 else 2)
                eng.wait_ge(*ac.after("gate_free", 2))
                eng.wait_ge(*ac.after("merged_sum"))
                a(as_r(sq_r[:, :, :]), sq[:, :, :], ACT.Copy).then_inc(*ac.up("act_step"))
                ac.mark("merged_rounded")
                a(as_r(ptk_r), ptk[:, :, :], ACT.Copy).then_inc(*ac.up("act_step"))
                ac.mark("ptk_rounded")
                split(4)
                ffn()
                norm()
                for cp in range(4):
                    for j in range(2):
                        if cp:
                            eng.wait_ge(*ac.after("gate_free"))
                        a(gate[:, j, :], take()[:, 0:T], ACT.Sigmoid).then_inc(*ac.up("bankA_free"))
                        ac.mark("gate_ready")
                    split(2)
                eng.wait_ge(*ac.after("gate_free", 2))
            layers(eng, ac, body)
            eng.wait_ge(*ac.after("x_final", DEPTH))
            eng.dma_start(io["y_out"], x[:, :, :]).then_inc(sems("y_out"), 16)
            eng.wait_ge(sems("y_out"), 16)

        @block.vector
        def _(eng):
            ve = Lane(eng, sems, marks, found)
            state = {"V": 0, "split": 0, "merging": True}
            tt, ts, stt = nc.vector.tensor_tensor, nc.vector.tensor_scalar, nc.vector.scalar_tensor_tensor
            cp = nc.vector.tensor_copy
            for _ in range(4):
                eng.nop().then_inc(*ve.up("bankV_free"))
            eng.wait_ge(*ve.next("inputs_in", 32))
            eng.nop().then_inc(*ve.up("dve_step"))
            for _ in range(DC):
                ve.mark("x_ready")

            def take():
                eng.wait_ge(*ve.next("bankV_full"))
                b = ringV[state["V"] % 4]
                state["V"] += 1
                return b

            pc = lambda name, i=0: prm[:, PCOL[name] + i:PCOL[name] + i + 1]

            def split(n=1):
                for _ in range(n):
                    m_ = state["split"]
                    if m_ == len(SPLIT) or (SPLIT[m_] % NSLAB == 54 and not state["merging"]):
                        return
                    state["split"] += 1
                    eng.wait_ge(*ve.after("slab_rounded"))
                    w_ = ring[:, SPLIT[m_] % SLOTS, :]
                    tt(as_r(w_), w_, as_r(slab_r[:, m_ % ROUNDED, :]).bitcast(F32), ALU.subtract).then_inc(*ve.up("dve_step"))
                    ve.mark("slab_split")

            def rest(ap, rounded):
                tt(as_r(ap), ap, as_r(rounded).bitcast(F32), ALU.subtract).then_inc(*ve.up("dve_step"))

            def norm(gain, rounded=True):
                ts(rstd[:, :], take()[:, 0:T], 1.0 / D, EPS, ALU.mult, ALU.add).then_inc(*ve.up("bankV_free"))
                eng.wait_ge(*ve.own())
                ve.mark("mean_square")
                eng.wait_ge(*ve.after("root"))
                nc.vector.reciprocal(rstd[:, :], rstd[:, :]).then_inc(*ve.up("dve_step"))
                eng.wait_ge(*ve.own())
                for i in range(DC):
                    stt(h[:, i, :], x[:, i, :], pc(gain, i), rstd[:, :], ALU.mult, ALU.mult).then_inc(*ve.up("dve_step"))
                    if rounded:
                        ve.mark("h_chunk")
                if rounded:
                    for i in range(DC):
                        eng.wait_ge(*ve.after("h_rounded"))
                        rest(h[:, i, :], h_r[:, i, :])
                        ve.mark("h_ready")
                else:
                    ve.mark("h_whole")

            def ffn(gain):
                norm(gain)
                for j in range(FC):
                    eng.wait_ge(*ve.after("silu"))
                    tt(hid[:, j, :], take()[:, 0:T], hid[:, j, :], ALU.mult).then_inc(*ve.up("bankV_free"))
                    eng.wait_ge(*ve.own())
                    cp(as_r(hid_r[:, j, :]), hid[:, j, :]).then_inc(*ve.up("dve_step"))
                    eng.wait_ge(*ve.own())
                    rest(hid[:, j, :], hid_r[:, j, :])
                    ve.mark("hidden")
                    if j % 2:
                        split(2)
                for j in range(4):
                    split(2)
                    for i in (2 * j, 2 * j + 1):
                        stt(x[:, i, :], take()[:, 0:T], 0.5, x[:, i, :], ALU.mult, ALU.add).then_inc(*ve.up("bankV_free"))
                        ve.mark("x_ready")
                    split(1)

            def body(L):
                ve.mark("layer_ready")
                eng.wait_ge(*ve.next("params_in", 80))
                state["merging"] = False
                if L == 0:
                    split(ROUNDED)
                ffn("ffn1")
                ve.mark("ffn1_done")
                norm("mix", False)
                if L == 0:
                    eng.wait_ge(*ve.next("tables_in", 16))
                nc.vector.memset(qz[:, :, :, :], 0.0).then_inc(*ve.up("dve_step"))
                eng.wait_ge(*ve.own())
                ve.mark("qz_clear")
                for src, n, m, gain in ((q, 4, P, "qn"), (k, 2, P, "kn"), (kid, 1, HD, "in")):
                    for i in range(n):
                        ts(sq[0:m, 4 + i, :], take()[0:m, 0:T], 1.0 / HD, EPS, ALU.mult, ALU.add).then_inc(*ve.up("bankV_free"))
                    ve.mark("head_means")
                    eng.wait_ge(*ve.after("head_roots"))
                    nc.vector.reciprocal(sq[0:m, 4:4 + n, :], sq[0:m, 4:4 + n, :]).then_inc(*ve.up("dve_step"))
                    eng.wait_ge(*ve.own())
                    for i in range(n):
                        ap = kid[0:m, :] if src is kid else src[:, i, :]
                        stt(ap, ap, prm[0:m, PCOL[gain]:PCOL[gain] + 1], sq[0:m, 4 + i, :], ALU.mult, ALU.mult).then_inc(*ve.up("dve_step"))
                    eng.wait_ge(*ve.own())
                    if src is not kid:
                        ve.mark("sums_taken")
                    ve.mark("to_rotate")
                ve.mark("to_rotate")
                for src, n, m in ((q, 4, P), (k, 2, P), (kid, 1, HD), (qi, 4, P)):
                    for i in range(n):
                        ap = kid[0:m, :] if src is kid else src[:, i, :]
                        tt(rot_t[0:m, :], take()[0:m, 0:T], C("sin")[0:m, :], ALU.mult).then_inc(*ve.up("bankV_free"))
                        tt(ap, ap, C("cos")[0:m, :], ALU.mult).then_inc(*ve.up("dve_step"))
                        eng.wait_ge(*ve.own())
                        tt(ap, ap, rot_t[0:m, :], ALU.add).then_inc(*ve.up("dve_step"))
                        eng.wait_ge(*ve.own())
                ve.mark("rope_done")
                for i in range(2):
                    ts(witok[:, i, :], take()[:, 0:NH], float(np.float32(NH ** -0.5)), None, ALU.mult).then_inc(*ve.up("bankV_free"))
                    if i == 1:
                        eng.wait_ge(*ve.own())
                ps = take()
                tt(wsel[:, 0, :], ps[:, 0:NSM], C("wsel0"), ALU.mult).then_inc(*ve.up("dve_step"))
                tt(wsel[:, 1, :], ps[:, 0:NSM], C("wsel1"), ALU.mult).then_inc(*ve.up("bankV_free"))
                ve.mark("wsel_ready")
                for i in range(2):
                    for n, pair in enumerate(PAIRS):
                        eng.wait_ge(*ve.after("rl_prompt"))
                        for j, hd in enumerate(pair):
                            before = C("causal")[:, NPR * i:NPR * (i + 1)] if n + j == 0 else seenP[:, i, :]
                            stt(seenP[:, i, :], rl[:, (4 * i + n) % 2, NPR * j:NPR * (j + 1)], witok[:, i, hd:hd + 1],
                                   before, ALU.mult, ALU.add).then_inc(*ve.up("dve_step"))
                            eng.wait_ge(*ve.own())
                        ve.mark("rl_read_v")
                for kb in range(5):
                    n = 512 if kb < 4 else NSM
                    ps = take()
                    if kb < 4:
                        cp(sidx[0:NSM, 512 * kb:512 * kb + n], ps[0:NSM, 0:n]).then_inc(*ve.up("bankV_free"))
                    else:
                        tt(sidx[0:NSM, PAST:KEYS], ps[0:NSM, 0:n], C("cs")[0:NSM, :], ALU.add).then_inc(*ve.up("bankV_free"))
                        eng.wait_ge(*ve.own())

                def choose(ap, k_, m):
                    for _ in range(k_ // 8):
                        nc.vector.max(out=m8[0:m, :], in_=ap).then_inc(*ve.up("dve_step"))
                        eng.wait_ge(*ve.own())
                        nc.vector.match_replace(out=ap, in_to_replace=m8[0:m, :], in_values=ap, imm_value=TAKEN).then_inc(*ve.up("dve_step"))
                        eng.wait_ge(*ve.own())

                for i in range(2):
                    choose(seenP[:, i, :], TOPK_P, P)
                    ts(seenP[:, i, :], seenP[:, i, :], TAKEN / 2, NEG, ALU.is_gt, ALU.mult).then_inc(*ve.up("dve_step"))
                    eng.wait_ge(*ve.own())
                    tt(seenP[:, i, :], seenP[:, i, :], C("causal")[:, NPR * i:NPR * (i + 1)], ALU.add).then_inc(*ve.up("dve_step"))
                    eng.wait_ge(*ve.own())
                    ve.mark("prompt_mask")
                for i in range(2):
                    for pair in PAIRS:
                        two = pr[:, pair[0]:pair[1] + 1:2, :]
                        tt(two, take()[:, :].rearrange("p (a b) -> p a b", a=2), bc(seenP[:, i, :], 2), ALU.add).then_inc(*ve.up("bankV_free"))
                        eng.wait_ge(*ve.own())
                        nc.vector.tensor_reduce(stat[:, pair[0]:pair[1] + 1:2], two, AX.X, ALU.max).then_inc(*ve.up("dve_step"))
                        eng.wait_ge(*ve.own())
                        ts(stat[:, 8 + pair[0]:9 + pair[1]:2], stat[:, pair[0]:pair[1] + 1:2], -0.125, None, ALU.mult).then_inc(*ve.up("dve_step"))
                        eng.wait_ge(*ve.own())
                        ve.mark("prompt_max")
                    for c4 in range(4):
                        if c4 % 2 == 0:
                            eng.wait_ge(*ve.after("prompt_exp", 4))
                        nc.vector.reciprocal(stat[:, 32 + 2 * c4:34 + 2 * c4], stat[:, 16 + 2 * c4:18 + 2 * c4]).then_inc(*ve.up("dve_step"))
                        eng.wait_ge(*ve.own())
                        for hd in (2 * c4, 2 * c4 + 1):
                            ts(pr[:, hd, :], pr[:, hd, :], stat[:, 32 + hd:33 + hd], None, ALU.mult).then_inc(*ve.up("dve_step"))
                        ve.mark("prompt_probs")
                    for c4 in range(4):
                        cp(oc[:, c4, P * i:P * (i + 1)], take()[:, 0:P]).then_inc(*ve.up("bankV_free"))
                ve.mark("prompt_out")
                rows, more = slice(0, NSM), slice(NSM, 2 * NSM)
                cp(halves[rows, :], sidx[rows, 0:KEYS // 2]).then_inc(*ve.up("dve_step"))
                cp(halves[more, :], sidx[rows, KEYS // 2:KEYS]).then_inc(*ve.up("dve_step"))
                eng.wait_ge(*ve.own())
                for i in range(0, TOPK_S, 8):
                    nc.vector.max(out=best[0:2 * NSM, i:i + 8], in_=halves[0:2 * NSM, :]).then_inc(*ve.up("dve_step"))
                    eng.wait_ge(*ve.own())
                    if i + 8 < TOPK_S:
                        nc.vector.match_replace(out=halves[0:2 * NSM, :], in_to_replace=best[0:2 * NSM, i:i + 8],
                                                   in_values=halves[0:2 * NSM, :], imm_value=TAKEN).then_inc(*ve.up("dve_step"))
                        eng.wait_ge(*ve.own())
                cp(best2[rows, :], best[more, :]).then_inc(*ve.up("dve_step"))
                eng.wait_ge(*ve.own())
                tt(best[rows, :], best[rows, :], falling_to_rising(best2[rows, :]), ALU.max).then_inc(*ve.up("dve_step"))
                eng.wait_ge(*ve.own())
                bound, left = stat[rows, 56:57], stat[rows, 57:58]
                nc.vector.tensor_reduce(bound, best[rows, :], AX.X, ALU.min).then_inc(*ve.up("dve_step"))
                eng.wait_ge(*ve.own())
                eng.wait_ge(*ve.next("kv_out", 48))
                flag, equal = flags[rows, :], pt[rows, :, :].rearrange("p a b -> p (a b)")[:, 0:KEYS]
                ts(flag, sidx[rows, :], bound, None, ALU.is_gt).then_inc(*ve.up("dve_step"))
                eng.wait_ge(*ve.own())
                nc.vector.tensor_reduce(left, flag, AX.X, ALU.add).then_inc(*ve.up("dve_step"))
                eng.wait_ge(*ve.own())
                ts(left, left, -1.0, float(TOPK_S), ALU.mult, ALU.add).then_inc(*ve.up("dve_step"))
                eng.wait_ge(*ve.own())
                ts(equal, sidx[rows, :], bound, None, ALU.is_equal).then_inc(*ve.up("dve_step"))
                eng.wait_ge(*ve.own())
                nc.vector.tensor_tensor_scan(flag, equal, equal, 0.0, ALU.add, ALU.max).then_inc(*ve.up("dve_step"))
                eng.wait_ge(*ve.own())
                stt(flag, flag, left, equal, ALU.is_le, ALU.mult).then_inc(*ve.up("dve_step"))
                eng.wait_ge(*ve.own())
                stt(sidx[rows, :], sidx[rows, :], bound, flag, ALU.is_gt, ALU.add).then_inc(*ve.up("dve_step"))
                eng.wait_ge(*ve.own())
                ts(sidx[rows, :], sidx[rows, :], 1.0, -NEG, ALU.subtract, ALU.mult).then_inc(*ve.up("dve_step"))
                eng.wait_ge(*ve.own())
                ve.mark("sample_mask")
                for grp in range(2):
                    eng.wait_ge(*ve.after("sample_scores"))
                    for kb in range(5):
                        n = 512 if kb < 4 else NSM
                        part = scg[grp][:, 512 * kb:512 * kb + n]
                        tt(part, take()[:, 0:n], part, ALU.add).then_inc(*ve.up("bankV_free"))
                    eng.wait_ge(*ve.own())
                    o = 24 + 16 * grp
                    nc.vector.tensor_reduce(stat[:, o:o + 1], scg[grp], AX.X, ALU.max).then_inc(*ve.up("dve_step"))
                    eng.wait_ge(*ve.own())
                    ts(stat[:, o + 1:o + 2], stat[:, o:o + 1], -0.125, None, ALU.mult).then_inc(*ve.up("dve_step"))
                    eng.wait_ge(*ve.own())
                    ve.mark("sample_max")
                for grp in range(2):
                    eng.wait_ge(*ve.after("sample_exp"))
                    o = 24 + 16 * grp
                    nc.vector.reciprocal(stat[:, o + 3:o + 4], stat[:, o + 2:o + 3]).then_inc(*ve.up("dve_step"))
                    eng.wait_ge(*ve.own())
                nc.vector.memset(zx[:, :, 0:2], 0.0).then_inc(*ve.up("dve_step"))
                eng.wait_ge(*ve.own())
                for i in range(4):
                    cp(zx[:, i, 2 + NPR:ZX].rearrange("p (b s) -> p b s", b=NB)[:, :, 0:2], scv[:, i, :, :]).then_inc(*ve.up("dve_step"))
                    eng.wait_ge(*ve.own())
                eng.wait_ge(*ve.after("conv_in"))
                for i in range(4):
                    zp = zx[:, i, 0:2 + NPR]
                    zs = zx[:, i, 2 + NPR:ZX].rearrange("p (b s) -> p b s", b=NB)
                    c_s = cgate[:, i, NPR:T].rearrange("p (b t) -> p b t", t=NS)
                    o_s = ob[:, i, NPR:T].rearrange("p (b t) -> p b t", t=NS)
                    tt(zp[:, 2:], zp[:, 2:], cgate[:, i, 0:NPR], ALU.mult).then_inc(*ve.up("dve_step"))
                    tt(zs[:, :, 2:], zs[:, :, 2:], c_s, ALU.mult).then_inc(*ve.up("dve_step"))
                    eng.wait_ge(*ve.own())
                    cp(cvo[:, i, NB, :], zp[:, NPR:NPR + 2]).then_inc(*ve.up("dve_step"))
                    cp(cvo[:, i, 0:NB, :], zs[:, :, NS:NS + 2]).then_inc(*ve.up("dve_step"))
                    for j in range(3):
                        wj = pc("cw", 4 * j + i)
                        if j == 0:
                            ts(ob[:, i, 0:NPR], zp[:, 0:NPR], wj, None, ALU.mult).then_inc(*ve.up("dve_step"))
                            ts(o_s, zs[:, :, 0:NS], wj, None, ALU.mult).then_inc(*ve.up("dve_step"))
                            eng.wait_ge(*ve.own())
                        else:
                            stt(ob[:, i, 0:NPR], zp[:, j:j + NPR], wj, ob[:, i, 0:NPR], ALU.mult, ALU.add).then_inc(*ve.up("dve_step"))
                            stt(o_s, zs[:, :, j:j + NS], wj, o_s, ALU.mult, ALU.add).then_inc(*ve.up("dve_step"))
                            eng.wait_ge(*ve.own())
                tt(ob[:, :, :], ob[:, :, :], bgate[:, :, :], ALU.mult).then_inc(*ve.up("dve_step"))
                eng.wait_ge(*ve.own())
                for grp in range(2):
                    o = 24 + 16 * grp
                    ts(orow[:, grp, :], take()[:, 0:256], stat[:, o + 3:o + 4], None, ALU.mult).then_inc(*ve.up("bankV_free"))
                    ve.mark("sample_rows")
                for grp in range(2):
                    cp(ov[:, :, 4 * grp:4 * grp + 4, :],
                            take()[:, 0:256].rearrange("p (g b r) -> p g b r", g=2, b=4)).then_inc(*ve.up("bankV_free"))
                eng.wait_ge(*ve.own())
                for c4 in range(4):
                    for hh in range(2):
                        hd = 2 * c4 + hh
                        cp(oc[HD * hh:HD * hh + HD, c4, NPR:T].rearrange("p (b t) -> p b t", t=NS),
                              ov[HD * (c4 % 2):HD * (c4 % 2) + HD, c4 // 2, :, NS * hd:NS * hd + NS]).then_inc(*ve.up("dve_step"))
                eng.wait_ge(*ve.after("u_in"))
                barrier(ve, "dve")
                nc.vector.memset(uext[:, :, 0:1], 0.0).then_inc(*ve.up("dve_step"))
                sv = uext[:, :, 1 + NPR:UX].rearrange("p a (b s) -> p a b s", b=NB)
                cp(sv[:, :, :, 0], sft[:, :, :]).then_inc(*ve.up("dve_step"))
                eng.wait_ge(*ve.own())
                cp(sho[:, :, NB], uext[:, :, NPR]).then_inc(*ve.up("dve_step"))
                cp(sho[:, :, 0:NB], sv[:, :, :, NS]).then_inc(*ve.up("dve_step"))
                ve.mark("sho_ready")
                rT, kT_, vT = us[:, 0:4, :], us[:, 4:8, :], us[:, 8:12, :]
                for n, i in enumerate((12, 13, 4, 5, 6, 7, 0, 1, 2, 3, 8, 9, 10, 11)):
                    d = oa[:, (n % 2) * 2:(n % 2) * 2 + 2, :].rearrange("p a t -> p (a t)")[:, 0:UX - 1]
                    tt(d, uext[:, i, 0:UX - 1], uext[:, i, 1:UX], ALU.subtract).then_inc(*ve.up("dve_step"))
                    eng.wait_ge(*ve.own())
                    stt(us[:, i, 0:NPR], d[:, 0:NPR], pc("mu", i), uext[:, i, 1:1 + NPR], ALU.mult, ALU.add).then_inc(*ve.up("dve_step"))
                    ds_ = d[:, NPR:NPR + NB * (NS + 1)].rearrange("p (b s) -> p b s", b=NB)[:, :, 1:1 + NS]
                    stt(us[:, i, NPR:T].rearrange("p (b t) -> p b t", t=NS), ds_, pc("mu", i),
                           sv[:, i, :, 1:1 + NS], ALU.mult, ALU.add).then_inc(*ve.up("dve_step"))
                    if i == 13:
                        ve.mark("us_ready")
                    if i == 7:
                        eng.wait_ge(*ve.own())
                        for c4 in range(4):
                            ts(kk[:, c4, :], kT_[:, c4, :], pc("kk", c4), None, ALU.mult).then_inc(*ve.up("dve_step"))
                        ve.mark("kk_raw")
                eng.wait_ge(*ve.own())
                for i in range(4):
                    cp(gT[:, i, :], take()[:, 0:T]).then_inc(*ve.up("bankV_free"))
                eng.wait_ge(*ve.after("kk_norm"))
                ts(sq[:, 4:8, :], sq[:, 4:8, :], 1e-12, None, ALU.max).then_inc(*ve.up("dve_step"))
                eng.wait_ge(*ve.own())
                nc.vector.reciprocal(sq[:, 4:8, :], sq[:, 4:8, :]).then_inc(*ve.up("dve_step"))
                eng.wait_ge(*ve.own())
                tt(kk[:, :, :], kk[:, :, :], sq[:, 4:8, :], ALU.mult).then_inc(*ve.up("dve_step"))
                for i in range(4):
                    ts(sq[:, i, :], aa[:, i, :], 1.0, pc("ka", i), ALU.subtract, ALU.mult).then_inc(*ve.up("dve_step"))
                eng.wait_ge(*ve.own())
                stt(kT_, sq[:, 0:4, :], 1.0, kT_, ALU.add, ALU.mult).then_inc(*ve.up("dve_step"))
                eng.wait_ge(*ve.own())
                tt(bon[:, :, :], rT, kT_, ALU.mult).then_inc(*ve.up("dve_step"))
                eng.wait_ge(*ve.own())
                for i in range(4):
                    ts(bon[:, i, :], bon[:, i, :], pc("rk", i), None, ALU.mult).then_inc(*ve.up("dve_step"))
                ve.mark("bonus_in")
                flat = lambda ap: ap.rearrange("p a t -> p (a t)")
                tt(sq[:, 0:4, :], dec[:, :, :], bc(C("keep"), 4), ALU.mult).then_inc(*ve.up("dve_step"))
                tt(sq[:, 4:8, :], dec[:, :, :], bc(C("begin"), 4), ALU.mult).then_inc(*ve.up("dve_step"))
                eng.wait_ge(*ve.own())
                nc.vector.tensor_tensor_scan(flat(pcum[:, :, :]), flat(sq[:, 0:4, :]), flat(sq[:, 4:8, :]), 0.0,
                                                ALU.mult, ALU.add).then_inc(*ve.up("dve_step"))
                eng.wait_ge(*ve.own())
                nc.vector.reciprocal(pinv[:, :, :], pcum[:, :, :]).then_inc(*ve.up("dve_step"))
                cp(pend[:, :, 0:8], pcum[:, :, CH - 1:NPR:CH]).then_inc(*ve.up("dve_step"))
                cp(pend[:, :, 8:16], pcum[:, :, NPR + NS - 1:T:NS]).then_inc(*ve.up("dve_step"))
                tt(AR[:, :, 1, :], rT, pcum[:, :, :], ALU.mult).then_inc(*ve.up("dve_step"))
                stt(AR[:, :, 0, 1:T], kk[:, :, 1:T], -1.0, pcum[:, :, 0:T - 1], ALU.mult, ALU.mult).then_inc(*ve.up("dve_step"))
                eng.wait_ge(*ve.own())
                ts(AR[:, :, 0, 0:NPR:CH], kk[:, :, 0:NPR:CH], -1.0, None, ALU.mult).then_inc(*ve.up("dve_step"))
                ts(AR[:, :, 0, NPR:T:NS], kk[:, :, NPR:T:NS], -1.0, None, ALU.mult).then_inc(*ve.up("dve_step"))
                tt(Bt[:, :, :], kk[:, :, :], aa[:, :, :], ALU.mult).then_inc(*ve.up("dve_step"))
                eng.wait_ge(*ve.own())
                tt(Kt[:, :, :], kT_, pinv[:, :, :], ALU.mult).then_inc(*ve.up("dve_step"))
                tt(Bt[:, :, :], Bt[:, :, :], pinv[:, :, :], ALU.mult).then_inc(*ve.up("dve_step"))
                eng.wait_ge(*ve.own())
                for i in range(4):
                    tt(bon[:, i, :], take()[:, 0:T], vT[:, i, :], ALU.mult).then_inc(*ve.up("bankV_free"))
                eng.wait_ge(*ve.own())
                barrier(ve, "dve")
                ve.mark("tilde_ready")
                nc.vector.memset(S[0][:, :, :], 0.0).then_inc(*ve.up("dve_step"))
                nc.vector.memset(S[1][:, :, :], 0.0).then_inc(*ve.up("dve_step"))
                eng.wait_ge(*ve.own())
                ident4 = bc(C("ident"), 4)
                s_now = 0
                for i in range(2):
                    if i == 0:
                        eng.wait_ge(*ve.after("tok_ready"))
                    else:
                        eng.wait_ge(*ve.after("tile_done"))
                    ve.mark("chunks_go")
                    for hd in range(NH):
                        tt(G[:, hd, :], take(), C("gm"), ALU.mult).then_inc(*ve.up("bankV_free"))
                    ve.mark("g_ready")
                    cp(MV[:, :], take()).then_inc(*ve.up("bankV_free"))
                    eng.wait_ge(*ve.own())
                    for hh in range(2):
                        ps = chunk4(take()[:, :])
                        tt(nm["y8"][:, :, :], ps, bc(C("y8"), 4), ALU.mult).then_inc(*ve.up("dve_step"))
                        tt(nm["yo16"][:, :, :], ps, bc(C("y16"), 4), ALU.mult).then_inc(*ve.up("dve_step"))
                        tt(nm["yo32"][:, :, :], ps, bc(C("y32"), 4), ALU.mult).then_inc(*ve.up("bankV_free"))
                        eng.wait_ge(*ve.own())
                        tt(nm["iy8"][:, :, :], nm["y8"][:, :, :], ident4, ALU.add).then_inc(*ve.up("dve_step"))
                        eng.wait_ge(*ve.own())
                        ve.mark("y_ready")
                        ps = chunk4(take()[:, :])
                        cp(nm["y2"][:, :, :], ps).then_inc(*ve.up("dve_step"))
                        tt(nm["iy2"][:, :, :], ps, ident4, ALU.add).then_inc(*ve.up("bankV_free"))
                        ve.mark("y2_ready")
                        tt(nm["h4"][:, :, :], chunk4(take()[:, :]), ident4, ALU.add).then_inc(*ve.up("bankV_free"))
                        ve.mark("h4_ready")
                        tt(t16, chunk4(take()[:, :]), nm["dd"][:, :, :], ALU.add).then_inc(*ve.up("bankV_free"))
                        ve.mark("t16_ready")
                        tt(Ti[:, hh::2, :], chunk4(take()[:, :]), t16, ALU.add).then_inc(*ve.up("bankV_free"))
                        eng.wait_ge(*ve.own())
                    ve.mark("t_ready")
                    for cc in range(4):
                        o = 32 * cc
                        ve.mark("s_ready")
                        tt(R1[o:o + 32, :], take()[o:o + 32, :], MV[o:o + 32, :], ALU.add).then_inc(*ve.up("bankV_free"))
                        ve.mark("r1_ready")
                        s_new = 1 - s_now
                        ps = chunk4(take())
                        tt(Ssum[0:HD, :, :], ps[0:HD, :, 0:HD], S[s_now][0:HD, :, 0:HD], ALU.add).then_inc(*ve.up("dve_step"))
                        tt(Ssum[HD:P, :, :], ps[HD:P, :, HD:P], S[s_now][HD:P, :, HD:P], ALU.add).then_inc(*ve.up("bankV_free"))
                        eng.wait_ge(*ve.own())
                        if i or cc:
                            eng.wait_ge(*ve.after("o_read"))
                        for rows in (slice(0, HD), slice(HD, P)):
                            tt(S[s_new][rows, :, rows], Ssum[rows, :, :],
                                  pend[rows, :, 4 * i + cc:4 * i + cc + 1].to_broadcast([HD, 4, HD]), ALU.mult).then_inc(*ve.up("dve_step"))
                        eng.wait_ge(*ve.own())
                        s_now = s_new
                ve.mark("prompt_state")
                n = NSM
                eng.wait_ge(*ve.after("tile_done"))
                ve.mark("chunks_go")
                eng.wait_ge(*ve.after("o_read"))
                for hh in range(2):
                    tt(G[0:n, hh::2, 0:4 * n], chunk4(take()[0:n, :]), bc(C("gs")[0:n, :], 4), ALU.mult).then_inc(*ve.up("bankV_free"))
                flat_s = lambda ap: ap[0:n, :, :].rearrange("p a b -> p (a b)")[:, 0:NH * n].rearrange(
                    "p (a b) -> p a b", b=n)
                for hh in range(2):
                    tt(flat_s(nm["y8"])[:, hh::2, :], take()[0:n, 0:4 * n].rearrange("p (a b) -> p a b", b=n),
                            bc(C("ys")[0:n, :], 4), ALU.mult).then_inc(*ve.up("bankV_free"))
                    eng.wait_ge(*ve.own())
                idn = bc(C("ident")[0:n, 0:n], NH)
                tt(flat_s(nm["iy8"]), flat_s(nm["y8"]), idn, ALU.add).then_inc(*ve.up("dve_step"))
                eng.wait_ge(*ve.own())
                ve.mark("g_ready")
                cp(MV[0:n, :], take()[0:n, :]).then_inc(*ve.up("bankV_free"))
                eng.wait_ge(*ve.own())
                eng.wait_ge(*ve.after("xs2_ready"))
                v8 = lambda ap: ap[0:n, :].rearrange("p (a b) -> p a b", b=n)
                tt(v8(hs), v8(xs2), idn, ALU.add).then_inc(*ve.up("dve_step"))
                eng.wait_ge(*ve.own())
                ve.mark("hs_ready")
                ve.mark("hs_made")
                tt(R1[0:n, :], take()[0:n, :], MV[0:n, :], ALU.add).then_inc(*ve.up("bankV_free"))
                ve.mark("r1_ready")
                for c4 in range(4):
                    sm = s_sum.rearrange("p (b i) -> p b i", b=NB)
                    tt(sm, take()[:, :].rearrange("p (b i) -> p b i", b=NB), S0[:, c4, :, :], ALU.add).then_inc(*ve.up("bankV_free"))
                    eng.wait_ge(*ve.own())
                    tt(S0[:, c4, :, :], sm, pend[:, c4, 8:16].rearrange("p (b m) -> p b m", m=1).to_broadcast([P, NB, HD]),
                          ALU.mult).then_inc(*ve.up("dve_step"))
                    eng.wait_ge(*ve.own())
                ve.mark("state_ready")
                eng.wait_ge(*ve.after("o_ready"))
                for i in range(4):
                    stt(oa[:, i, :], take()[:, 0:T], -1.0 / HD, oa[:, i, :], ALU.mult, ALU.add).then_inc(*ve.up("bankV_free"))
                ve.mark("o_centred")
                for i in range(4):
                    ts(sq[:, 4 + i, :], take()[:, 0:T], 1.0 / HD, GN_EPS, ALU.mult, ALU.add).then_inc(*ve.up("bankV_free"))
                ve.mark("o_var")
                eng.wait_ge(*ve.after("o_root"))
                nc.vector.reciprocal(sq[:, 4:8, :], sq[:, 4:8, :]).then_inc(*ve.up("dve_step"))
                eng.wait_ge(*ve.own())
                tt(oa[:, :, :], oa[:, :, :], sq[:, 4:8, :], ALU.mult).then_inc(*ve.up("dve_step"))
                eng.wait_ge(*ve.own())
                for i in range(4):
                    ts(oa[:, i, :], oa[:, i, :], pc("lnw", i), pc("lnb", i), ALU.mult, ALU.add).then_inc(*ve.up("dve_step"))
                eng.wait_ge(*ve.own())
                tt(oa[:, :, :], oa[:, :, :], bon[:, :, :], ALU.add).then_inc(*ve.up("dve_step"))
                eng.wait_ge(*ve.own())
                tt(oa[:, :, :], oa[:, :, :], gT[:, :, :], ALU.mult).then_inc(*ve.up("dve_step"))
                eng.wait_ge(*ve.own())
                barrier(ve, "dve")
                state["merging"] = True
                for src, rounded in ((h, h_r), (oa, oa_r), (ob, ob_r), (oc, oc_r)):
                    eng.wait_ge(*ve.after("branch_rounded"))
                    rest(src[:, :, :], rounded[:, :, :])
                ve.mark("branches_ready")
                split(ROUNDED)
                for cp_ in range(4):
                    for br in range(3):
                        for j in range(2):
                            eng.wait_ge(*ve.after("gate_ready"))
                            ps = take()
                            to = sq[:, 2 * cp_ + j, :]
                            if br == 0:
                                tt(to, ps[:, 0:T], gate[:, j, :], ALU.mult).then_inc(*ve.up("bankV_free"))
                                eng.wait_ge(*ve.own())
                            else:
                                tt(gate[:, j, :], ps[:, 0:T], gate[:, j, :], ALU.mult).then_inc(*ve.up("bankV_free"))
                                eng.wait_ge(*ve.own())
                                tt(to, to, gate[:, j, :], ALU.add).then_inc(*ve.up("dve_step"))
                                eng.wait_ge(*ve.own())
                            ve.mark("gate_free")
                        split(1 if br == 0 else 2)
                ve.mark("merged_sum")
                eng.wait_ge(*ve.after("merged_rounded"))
                rest(sq[:, :, :], sq_r[:, :, :])
                ve.mark("merged")
                eng.wait_ge(*ve.after("ptk_rounded"))
                rest(ptk[:, :, :], ptk_r)
                for j in range(DC):
                    tt(x[:, j, :], take()[:, 0:T], x[:, j, :], ALU.add).then_inc(*ve.up("bankV_free"))
                    ve.mark("x_ready")
                    if j % 2:
                        split(1)
                ffn("ffn2")
                norm("ple")
                for j in range(DC):
                    eng.wait_ge(*ve.after("gate_ready"))
                    tt(gate[:, j % 2, :], take()[:, 0:T], gate[:, j % 2, :], ALU.mult).then_inc(*ve.up("bankV_free"))
                    eng.wait_ge(*ve.own())
                    tt(x[:, j, :], x[:, j, :], gate[:, j % 2, :], ALU.add).then_inc(*ve.up("dve_step"))
                    eng.wait_ge(*ve.own())
                    ve.mark("gate_free")
                    ve.mark("x_ready")
                    if j == DC - 1:
                        ve.mark("x_final")
                    if j % 2:
                        split(2)
            layers(eng, ve, body)


NSLAB = 34 + 20 + 20 + 4 + 34 + 8


def pack(i):
    f = lambda a: np.asarray(a, np.float32) if np.asarray(a).dtype == np.float32 else np.asarray(a)
    i = {n: f(a) for n, a in i.items()}
    tokens = lambda a, b: np.concatenate([a.reshape(NPR, -1), b.reshape(NSM, -1)], 0)
    fm = lambda a: np.ascontiguousarray(a.T.reshape(-1, P, a.shape[0]).transpose(1, 0, 2))
    cols = lambda a: a.reshape(-1, P).T
    out = {"const": CONST, "x": fm(tokens(i["x_prompt"], i["x_sample"])),
           "pages": np.ascontiguousarray(i["page_table"].reshape(1, -1))}
    w = np.zeros((DEPTH, NSLAB, P, SLAB), np.float32)
    prm = np.zeros((DEPTH, P, NPARAM), np.float32)
    p = np.zeros((DEPTH, P, 2 * T), np.float32)
    lora = np.zeros((DEPTH, P, 2 * 512), np.float32)
    for L in range(DEPTH):
        n = 0

        def slab(*mats):
            nonlocal n
            at = 0
            for m in mats:
                k, c = m.shape
                m = m.reshape(k // P, P, c).transpose(1, 0, 2).reshape(P, -1)
                w[L, n, :, at:at + m.shape[1]] = m
                at += m.shape[1]
            n += 1

        def ffn(name):
            for j in range(FC // 2):
                slab(i[name + "_wg"][L][:, 256 * j:256 * (j + 1)])
                slab(i[name + "_wu"][L][:, 256 * j:256 * (j + 1)])
            for j in range(4):
                for k0, k1 in ((0, 8), (8, 16), (16, 22)):
                    slab(i[name + "_wd"][L][P * k0:P * k1, 256 * j:256 * (j + 1)])

        ffn("ffn1")
        win = i["w_in"][L]
        a0 = 1792 + 1536
        for j in range(6):
            slab(win[:, a0 + 256 * j:a0 + 256 * (j + 1)])
        kiwi = np.zeros((D, 256), np.float32)
        kiwi[:, 0:72] = win[:, a0 + 1536:a0 + 1608]
        slab(kiwi)
        for j in range(6):
            slab(win[:, 1792 + 256 * j:1792 + 256 * (j + 1)])
        for j in range(7):
            slab(win[:, 256 * j:256 * (j + 1)])
        g0 = a0 + 1608
        for j in range(4):
            cs = slice(256 * j, 256 * (j + 1))
            for br in range(3):
                slab(win[:, g0 + 1024 * br + 256 * j:g0 + 1024 * br + 256 * (j + 1)])
                if br == 0:
                    slab(i["w_pa"][L][:, cs], i["w_pb"][L][:, cs])
                if br == 2:
                    slab(i["w_pc"][L][:, cs])
        for j in range(4):
            slab(i["w_out"][L][:, 256 * j:256 * (j + 1)])
        ffn("ffn2")
        for j in range(4):
            slab(i["ple_gate"][L][:, 256 * j:256 * (j + 1)])
            slab(i["ple_proj"][L][:, 256 * j:256 * (j + 1)])
        assert n == NSLAB
        put = lambda name, a: prm[L].__setitem__((slice(None), slice(PCOL[name], PCOL[name] + a.shape[1])), a)
        for name, src in (("ffn1", "ffn1_norm"), ("mix", "mix_norm"), ("ffn2", "ffn2_norm"), ("ple", "ple_norm"),
                          ("mu", "rwkv_mu"), ("w0", "rwkv_w0"), ("a0", "rwkv_a0"), ("kk", "rwkv_kk"), ("ka", "rwkv_ka"),
                          ("rk", "rwkv_rk"), ("lnw", "rwkv_lnx_w"), ("lnb", "rwkv_lnx_b")):
            put(name, cols(i[src][L].reshape(-1)))
        put("cw", cols(i["conv_w"][L].reshape(-1)))
        for name, src in (("qn", "q_norm"), ("kn", "k_norm"), ("in", "idx_k_norm")):
            put(name, np.concatenate([i[src][L], i[src][L]])[:, None])
        p[L] = fm(tokens(i["p_prompt"][L], i["p_sample"][L])).reshape(P, -1)
        lora[L, 0:HD, 0:512] = i["rwkv_w2"][L]
        lora[L, HD:P, 0:512] = i["rwkv_a2"][L]
        lora[L, :, 512:] = i["rwkv_g2"][L]
    out.update(w=w, prm=prm, p=p, lora=lora)
    s = i["state_shift"].reshape(DEPTH, NB, UC, P).transpose(0, 3, 2, 1)
    out["sft"] = np.ascontiguousarray(s.reshape(DEPTH, P, -1))
    s = i["state_conv"].reshape(DEPTH, NB, 2, 4, P).transpose(0, 4, 3, 1, 2)
    out["scv"] = np.ascontiguousarray(s.reshape(DEPTH, P, -1))
    s = i["state_wkv"].reshape(DEPTH, NB, 4, 2, HD, HD).transpose(0, 3, 5, 2, 1, 4)
    out["s0"] = np.ascontiguousarray(s.reshape(DEPTH, P, -1))
    s = i["cache_k"].reshape(DEPTH * NPHYS, PAGE, 2, 2, HD).transpose(0, 3, 4, 2, 1)
    out["k"] = np.ascontiguousarray(s.reshape(DEPTH * NPHYS, P, 256))
    out["v"] = np.ascontiguousarray(i["cache_v"].reshape(DEPTH * NPHYS, PAGE, 256))
    out["ki"] = np.ascontiguousarray(i["cache_kidx"].reshape(DEPTH * NPHYS, PAGE, HD).transpose(0, 2, 1))
    return out


OUTS = {"y_out": (P, DC, T), "k_out": (DEPTH, P, 2 * T), "v_out": (DEPTH, P, 2 * T), "ki_out": (DEPTH, HD, T),
        "s_out": (DEPTH, P, 4 * (NB + 1) * HD), "shift_out": (DEPTH, P, UC * (NB + 1)),
        "conv_out": (DEPTH, P, 4 * (NB + 1) * 2)}


def unpack(r):
    tok = lambda a: a.transpose(2, 1, 0).reshape(a.shape[2], -1)
    y = tok(r["y_out"])
    kv = {}
    for name in ("k_out", "v_out"):
        a = np.stack([tok(r[name][L].reshape(P, 2, T)) for L in range(DEPTH)])
        kv[name] = (a[:, :NPR].reshape(DEPTH, 1, NPR, 4, HD), a[:, NPR:].reshape(DEPTH, NB, NS, 4, HD))
    ki = r["ki_out"].transpose(0, 2, 1)
    s = r["s_out"].reshape(DEPTH, 2, HD, 4, NB + 1, HD).transpose(0, 4, 3, 1, 5, 2).reshape(DEPTH, NB + 1, NH, HD, HD)
    sh = r["shift_out"].reshape(DEPTH, P, UC, NB + 1).transpose(0, 3, 2, 1).reshape(DEPTH, NB + 1, UC * P)
    cv = r["conv_out"].reshape(DEPTH, P, 4, NB + 1, 2).transpose(0, 3, 4, 2, 1).reshape(DEPTH, NB + 1, 2, 512)
    got = (y[:NPR].reshape(1, NPR, D), y[NPR:].reshape(NB, NS, D), kv["k_out"][0], kv["v_out"][0],
           ki[:, :NPR].reshape(DEPTH, 1, NPR, HD), s[:, NB:], sh[:, NB:], cv[:, NB:],
           kv["k_out"][1], kv["v_out"][1], ki[:, NPR:].reshape(DEPTH, NB, NS, HD), s[:, :NB], sh[:, :NB], cv[:, :NB])
    return tuple(np.ascontiguousarray(a) for a in got)


def program(make, arrays):
    marks = {}
    for _ in range(2):
        nc, found, io = make(), {}, {}
        for name, a in arrays.items():
            io[name] = nc.dram_tensor(f"in_{name}", a.shape, I32 if name == "pages" else F32, kind="ExternalInput").ap()
        for name, shape in OUTS.items():
            io[name] = nc.dram_tensor(f"{name}", shape, F32, kind="ExternalOutput").ap()
        build(nc, io, marks, found)
        marks = found
    return nc


def kernel(**inputs):
    import concourse.bacc as bacc
    from concourse.bass_utils import run_bass_kernel_spmd as run

    arrays = pack(inputs)
    nc = program(lambda: bacc.Bacc("TRN2", target_bir_lowering=False, num_devices=1), arrays)
    r = run(nc, [{f"in_{n}": a for n, a in arrays.items()}], core_ids=[0]).results[0]
    return unpack({n: r[n] for n in OUTS})
```
